# Optimizing a Trainium2 kernel written in Bass

```python
import functools
import jax, jax.numpy as jnp
from jax import lax
import numpy as np

D_MODEL = 1024
BATCH = 1
SEQ = 128
DEPTH = 2
DEC_BATCH = 1
DEC_SEQ = 512
PAST_LEN = 128

GRID_W = 64
HEAD_DIM = 64
NA_HEADS = 8
NA_WIN_R = 8
NA_WIN_C = 16
GQA_HEADS = 8
GQA_KV_HEADS = 2
BRANCH_W = 512
N_BRANCH = 4
CONV_K = 3
POOL_WINDOWS = (2, 4, 8, 16)
POOL_GROUPS = 4
POOL_GW = BRANCH_W // POOL_GROUPS
N_EXPERTS = 16
EXPERT_FF = 1024
EC_CAPACITY = 2
Q_BLOCK = 128
ROPE_THETA = 10000.0
LN_EPS = 1e-6
RMS_EPS = 1e-6
N_MOD = 6
ADA_INIT = 0.5
DEEPNORM_ALPHA = (2 * DEPTH) ** 0.25
DEEPNORM_BETA = (8 * DEPTH) ** -0.25
NA_W = NA_HEADS * HEAD_DIM
GQA_QW = GQA_HEADS * HEAD_DIM
GQA_KW = GQA_KV_HEADS * HEAD_DIM
IN_SIZES = (NA_W, NA_W, NA_W, GQA_QW, GQA_KW, GQA_KW, BRANCH_W, BRANCH_W, BRANCH_W, BRANCH_W, N_BRANCH * D_MODEL)
IN_OFFSETS = tuple(int(v) for v in np.cumsum(IN_SIZES)[:-1])
IN_W = int(sum(IN_SIZES))

kernel_name = "hybrid_diffusion_gated_branch_trunk_step"

def layer_norm(x, g, b):
    xf = x.astype(jnp.float32)
    mu = jnp.mean(xf, -1, keepdims=True)
    var = jnp.mean(jnp.square(xf - mu), -1, keepdims=True)
    return ((xf - mu) * lax.rsqrt(var + LN_EPS) * g + b).astype(x.dtype)

def rms_norm(x, g):
    xf = x.astype(jnp.float32)
    return (xf * lax.rsqrt(jnp.mean(xf * xf, -1, keepdims=True) + RMS_EPS) * g).astype(x.dtype)

def adaln(cvec, w, b):
    return jnp.einsum("bd,dk->bk", jax.nn.silu(cvec), w) + b

def modulate(x, shift, scale):
    return x * (1 + scale) + shift

def _rotate(xh, ang):
    x1, x2 = jnp.split(xh.astype(jnp.float32), 2, axis=-1)
    cos = jnp.cos(ang)[None, :, None, :]
    sin = jnp.sin(ang)[None, :, None, :]
    return jnp.concatenate([x1 * cos - x2 * sin, x1 * sin + x2 * cos], -1)

def axial_rope(x):
    L = x.shape[1]
    t = jnp.arange(L)
    n_freq = HEAD_DIM // 4
    inv = ROPE_THETA ** (-jnp.arange(n_freq, dtype=jnp.float32) / n_freq)
    ang_r = (t // GRID_W).astype(jnp.float32)[:, None] * inv
    ang_c = (t % GRID_W).astype(jnp.float32)[:, None] * inv
    xr, xc = jnp.split(x, 2, axis=-1)
    return jnp.concatenate([_rotate(xr, ang_r), _rotate(xc, ang_c)], -1).astype(x.dtype)

def blocked_attention(q, k, v):
    B, Lq, H, dh = q.shape
    G = k.shape[2]
    R = H // G
    scale = dh ** -0.5
    nb = Lq // Q_BLOCK
    qb = q.reshape(B, nb, Q_BLOCK, G, R, dh).transpose(1, 0, 2, 3, 4, 5)

    def one_block(qi):
        s = jnp.einsum("bqgrd,bkgd->bgrqk", qi, k, preferred_element_type=jnp.float32) * scale
        p = jax.nn.softmax(s, axis=-1).astype(v.dtype)
        return jnp.einsum("bgrqk,bkgd->bqgrd", p, v)

    o = lax.map(one_block, qb)
    return o.transpose(1, 0, 2, 3, 4, 5).reshape(B, Lq, H * dh)

def neighbourhood_attention(q, k, v, kc, vc, rpb):
    B, L, H, dh = q.shape
    rows = L // GRID_W
    wr = min(NA_WIN_R, rows)
    wc = NA_WIN_C
    scale = dh ** -0.5
    qg = q.reshape(B, rows, GRID_W, H, dh).transpose(1, 0, 2, 3, 4)
    kg = k.reshape(B, rows, GRID_W, H, dh)
    vg = v.reshape(B, rows, GRID_W, H, dh)
    cols = np.arange(GRID_W)
    col_start = np.clip(cols - wc // 2, 0, GRID_W - wc)
    col_idx = col_start[:, None] + np.arange(wc)[None, :]
    col_rel = col_idx - cols[:, None] + (NA_WIN_C - 1)
    row_starts = jnp.asarray(np.clip(np.arange(rows) - wr // 2, 0, rows - wr), jnp.int32)
    row_ids = jnp.arange(rows, dtype=jnp.int32)

    def one_row(args):
        qr, r, rs = args
        k_rows = lax.dynamic_slice_in_dim(kg, rs, wr, axis=1)
        v_rows = lax.dynamic_slice_in_dim(vg, rs, wr, axis=1)
        k_win = k_rows[:, :, col_idx]
        v_win = v_rows[:, :, col_idx]
        row_rel = rs + jnp.arange(wr) - r + (NA_WIN_R - 1)
        bias = rpb[:, row_rel[:, None, None], col_rel[None, :, :]]
        s_loc = jnp.einsum("bqhd,biqjhd->bhqij", qr, k_win, preferred_element_type=jnp.float32) * scale
        s_loc = s_loc + bias.transpose(0, 2, 1, 3)[None]
        s_ctx = jnp.einsum("bqhd,bphd->bhqp", qr, kc, preferred_element_type=jnp.float32) * scale
        s = jnp.concatenate([s_loc.reshape(B, H, GRID_W, wr * wc), s_ctx], axis=-1)
        p = jax.nn.softmax(s, axis=-1).astype(v.dtype)
        p_loc = p[..., : wr * wc].reshape(B, H, GRID_W, wr, wc)
        p_ctx = p[..., wr * wc:]
        return (jnp.einsum("bhqij,biqjhd->bqhd", p_loc, v_win)
                + jnp.einsum("bhqp,bphd->bqhd", p_ctx, vc))

    o = lax.map(one_row, (qg, row_ids, row_starts))
    return o.transpose(1, 0, 2, 3, 4).reshape(B, L, H * dh)

def short_conv(xb, xc, xh, w, b):
    u = xc * xh
    y = lax.conv_general_dilated(u, w[:, None, :], window_strides=(1,),
                                 padding=[(CONV_K // 2, CONV_K // 2)],
                                 dimension_numbers=("NWC", "WIO", "NWC"),
                                 feature_group_count=BRANCH_W) + b
    return xb * y

def multiscale_pool(u, w_grp, scale):
    B, L, _ = u.shape
    uf = u.astype(jnp.float32)
    cs = jnp.concatenate([jnp.zeros((B, 1, BRANCH_W), jnp.float32), jnp.cumsum(uf, axis=1)], axis=1)
    t = jnp.arange(L)
    outs = []
    for g, win in enumerate(POOL_WINDOWS):
        lo = jnp.clip(t - win // 2, 0, L)
        hi = jnp.clip(t + win // 2, 0, L)
        sl = slice(g * POOL_GW, (g + 1) * POOL_GW)
        csg = cs[..., sl]
        cnt = (hi - lo).astype(jnp.float32)[None, :, None]
        outs.append((csg[:, hi] - csg[:, lo]) / cnt - uf[..., sl])
    pooled = jnp.stack(outs, axis=2).astype(u.dtype)
    mixed = jnp.einsum("blgc,gcd->blgd", pooled, w_grp)
    return mixed.reshape(B, L, BRANCH_W) * scale

def merge_branches(branches, gate_logits, w_branch, w_out):
    B, L, _ = gate_logits.shape
    bstack = jnp.stack(branches, axis=2)
    proj = jnp.einsum("blnc,ncd->blnd", bstack, w_branch)
    gates = jax.nn.sigmoid(gate_logits.reshape(B, L, N_BRANCH, D_MODEL))
    merged = jnp.sum(gates * proj, axis=2)
    return jnp.einsum("bld,de->ble", merged, w_out)

def split_inputs(h, w_in):
    return jnp.split(jnp.einsum("bld,dk->blk", h, w_in), IN_OFFSETS, axis=-1)

def mixer_context(h, p):
    B, L, _ = h.shape
    (na_q, na_k, na_v, g_q, g_k, g_v, cv_b, cv_c, cv_h, pl_u, gate_logits) = split_inputs(h, p["w_in"])
    na_q = na_q.reshape(B, L, NA_HEADS, HEAD_DIM)
    na_k = na_k.reshape(B, L, NA_HEADS, HEAD_DIM)
    na_v = na_v.reshape(B, L, NA_HEADS, HEAD_DIM)
    o_na = blocked_attention(na_q, na_k, na_v)
    g_q = rms_norm(g_q.reshape(B, L, GQA_HEADS, HEAD_DIM), p["qn_g"])
    g_k = rms_norm(g_k.reshape(B, L, GQA_KV_HEADS, HEAD_DIM), p["kn_g"])
    g_v = g_v.reshape(B, L, GQA_KV_HEADS, HEAD_DIM)
    o_gqa = blocked_attention(g_q, g_k, g_v)
    o_conv = short_conv(cv_b, cv_c, cv_h, p["conv_w"], p["conv_b"])
    o_pool = multiscale_pool(pl_u, p["pool_w"], p["pool_scale"])
    y = merge_branches((o_na, o_gqa, o_conv, o_pool), gate_logits, p["w_branch"], p["w_out"])
    return y, (na_k, na_v, g_k, g_v)

def mixer_latent(h, p, na_kc, na_vc, gqa_kc, gqa_vc):
    B, L, _ = h.shape
    (na_q, na_k, na_v, g_q, g_k, g_v, cv_b, cv_c, cv_h, pl_u, gate_logits) = split_inputs(h, p["w_in"])
    o_na = neighbourhood_attention(na_q.reshape(B, L, NA_HEADS, HEAD_DIM),
                                   na_k.reshape(B, L, NA_HEADS, HEAD_DIM),
                                   na_v.reshape(B, L, NA_HEADS, HEAD_DIM),
                                   na_kc, na_vc, p["na_rpb"])
    g_q = axial_rope(rms_norm(g_q.reshape(B, L, GQA_HEADS, HEAD_DIM), p["qn_g"]))
    g_k = axial_rope(rms_norm(g_k.reshape(B, L, GQA_KV_HEADS, HEAD_DIM), p["kn_g"]))
    g_v = g_v.reshape(B, L, GQA_KV_HEADS, HEAD_DIM)
    o_gqa = blocked_attention(g_q, jnp.concatenate([g_k, gqa_kc], axis=1),
                              jnp.concatenate([g_v, gqa_vc], axis=1))
    o_conv = short_conv(cv_b, cv_c, cv_h, p["conv_w"], p["conv_b"])
    o_pool = multiscale_pool(pl_u, p["pool_w"], p["pool_scale"])
    y = merge_branches((o_na, o_gqa, o_conv, o_pool), gate_logits, p["w_branch"], p["w_out"])
    return y, None

def expert_choice_moe(x, w_router, w_gate, w_up, w_down):
    B, L, D = x.shape
    n = B * L
    cap = EC_CAPACITY * n // N_EXPERTS
    xt = x.reshape(n, D)
    aff = jax.nn.softmax(jnp.einsum("nd,de->ne", xt, w_router, preferred_element_type=jnp.float32), axis=-1)
    g, idx = lax.top_k(aff.T, cap)
    xs = xt[idx]
    hdn = jax.nn.silu(jnp.einsum("ecd,edf->ecf", xs, w_gate)) * jnp.einsum("ecd,edf->ecf", xs, w_up)
    ye = jnp.einsum("ecf,efd->ecd", hdn, w_down) * g[..., None].astype(x.dtype)
    y = jnp.zeros_like(xt).at[idx.reshape(-1)].add(ye.reshape(-1, D))
    return y.reshape(B, L, D)

def post_norm_layer(x, mod, mix_fn, p):
    shift1, scale1, gate1, shift2, scale2, gate2 = jnp.split(mod, N_MOD, axis=-1)
    y_mix, ctx = mix_fn(modulate(x, shift1, scale1))
    x = layer_norm(DEEPNORM_ALPHA * x + gate1 * y_mix, p["ln1_g"], p["ln1_b"])
    y_ff = expert_choice_moe(modulate(x, shift2, scale2), p["w_router"], p["w_gate"], p["w_up"], p["w_down"])
    x = layer_norm(DEEPNORM_ALPHA * x + gate2 * y_ff, p["ln2_g"], p["ln2_b"])
    return x, ctx

def setup_inputs(seed: int = 0) -> dict:
    key = jax.random.key(seed)
    ks = jax.random.split(key, 32)
    nrm = lambda k, s: jax.random.normal(k, s, jnp.float32)
    D = D_MODEL
    return {
        "x_prompt": nrm(ks[0], (BATCH, SEQ, D)),
        "x_sample": nrm(ks[1], (DEC_BATCH, DEC_SEQ, D)),
        "cache_na_k": nrm(ks[2], (DEC_BATCH, DEPTH, PAST_LEN, NA_HEADS, HEAD_DIM)),
        "cache_na_v": nrm(ks[3], (DEC_BATCH, DEPTH, PAST_LEN, NA_HEADS, HEAD_DIM)),
        "cache_gqa_k": nrm(ks[4], (DEC_BATCH, DEPTH, PAST_LEN, GQA_KV_HEADS, HEAD_DIM)),
        "cache_gqa_v": nrm(ks[5], (DEC_BATCH, DEPTH, PAST_LEN, GQA_KV_HEADS, HEAD_DIM)),
        "c": nrm(ks[6], (DEC_BATCH, D)),
        "c_ctx": nrm(ks[7], (D,)),
        "w_ada": nrm(ks[8], (DEPTH, D, N_MOD * D)) * (ADA_INIT * D ** -0.5),
        "b_ada": nrm(ks[9], (DEPTH, N_MOD * D)) * 0.01,
        "w_in": nrm(ks[10], (DEPTH, D, IN_W)) * D ** -0.5,
        "na_rpb": nrm(ks[11], (DEPTH, NA_HEADS, 2 * NA_WIN_R - 1, 2 * NA_WIN_C - 1)) * 0.1,
        "qn_g": 1.0 + 0.01 * nrm(ks[12], (DEPTH, HEAD_DIM)),
        "kn_g": 1.0 + 0.01 * nrm(ks[13], (DEPTH, HEAD_DIM)),
        "conv_w": nrm(ks[14], (DEPTH, CONV_K, BRANCH_W)) * CONV_K ** -0.5,
        "conv_b": nrm(ks[15], (DEPTH, BRANCH_W)) * 0.01,
        "pool_w": nrm(ks[16], (DEPTH, POOL_GROUPS, POOL_GW, POOL_GW)) * POOL_GW ** -0.5,
        "pool_scale": 1.0 + 0.01 * nrm(ks[17], (DEPTH, BRANCH_W)),
        "w_branch": nrm(ks[18], (DEPTH, N_BRANCH, BRANCH_W, D)) * BRANCH_W ** -0.5,
        "w_out": nrm(ks[19], (DEPTH, D, D)) * (DEEPNORM_BETA * D ** -0.5),
        "ln1_g": 1.0 + 0.01 * nrm(ks[20], (DEPTH, D)),
        "ln1_b": 0.01 * nrm(ks[21], (DEPTH, D)),
        "ln2_g": 1.0 + 0.01 * nrm(ks[22], (DEPTH, D)),
        "ln2_b": 0.01 * nrm(ks[23], (DEPTH, D)),
        "w_router": nrm(ks[24], (DEPTH, D, N_EXPERTS)) * D ** -0.5,
        "w_gate": nrm(ks[25], (DEPTH, N_EXPERTS, D, EXPERT_FF)) * D ** -0.5,
        "w_up": nrm(ks[26], (DEPTH, N_EXPERTS, D, EXPERT_FF)) * D ** -0.5,
        "w_down": nrm(ks[27], (DEPTH, N_EXPERTS, EXPERT_FF, D)) * (DEEPNORM_BETA * EXPERT_FF ** -0.5),
    }

def reference(x_prompt, x_sample, cache_na_k, cache_na_v, cache_gqa_k, cache_gqa_v, c, c_ctx,
              w_ada, b_ada, w_in, na_rpb, qn_g, kn_g, conv_w, conv_b, pool_w, pool_scale,
              w_branch, w_out, ln1_g, ln1_b, ln2_g, ln2_b, w_router, w_gate, w_up, w_down):
    y_p = x_prompt
    y_s = x_sample
    na_k_list, na_v_list, gqa_k_list, gqa_v_list = [], [], [], []
    for l in range(DEPTH):
        p = {"w_in": w_in[l], "na_rpb": na_rpb[l], "qn_g": qn_g[l], "kn_g": kn_g[l],
             "conv_w": conv_w[l], "conv_b": conv_b[l], "pool_w": pool_w[l], "pool_scale": pool_scale[l],
             "w_branch": w_branch[l], "w_out": w_out[l], "ln1_g": ln1_g[l], "ln1_b": ln1_b[l],
             "ln2_g": ln2_g[l], "ln2_b": ln2_b[l], "w_router": w_router[l], "w_gate": w_gate[l],
             "w_up": w_up[l], "w_down": w_down[l]}
        mod_ctx = adaln(c_ctx[None, :], w_ada[l], b_ada[l])[:, None, :]
        mod_lat = adaln(c, w_ada[l], b_ada[l])[:, None, :]
        y_p, (k_na, v_na, k_g, v_g) = post_norm_layer(y_p, mod_ctx, functools.partial(mixer_context, p=p), p)
        na_k_list.append(k_na)
        na_v_list.append(v_na)
        gqa_k_list.append(k_g)
        gqa_v_list.append(v_g)
        mix_lat = functools.partial(mixer_latent, p=p, na_kc=cache_na_k[:, l], na_vc=cache_na_v[:, l],
                                    gqa_kc=cache_gqa_k[:, l], gqa_vc=cache_gqa_v[:, l])
        y_s, _ = post_norm_layer(y_s, mod_lat, mix_lat, p)
    state_na_k = jnp.stack(na_k_list, axis=1)
    state_na_v = jnp.stack(na_v_list, axis=1)
    state_gqa_k = jnp.stack(gqa_k_list, axis=1)
    state_gqa_v = jnp.stack(gqa_v_list, axis=1)
    return (y_p, y_s, state_na_k, state_na_v, state_gqa_k, state_gqa_v)


_drawn_inputs = setup_inputs


def setup_inputs(seed=0):
    import zlib

    import numpy as np

    out = dict(_drawn_inputs(seed))
    spreads = {}
    factors = {'cache_na_k': 8.0,
     'cache_na_v': 8.0,
     'cache_gqa_k': 8.0,
     'cache_gqa_v': 8.0,
     'b_ada': 4.148,
     'na_rpb': 64.0,
     'qn_g': 64.0,
     'kn_g': 102.018,
     'conv_b': 94.259,
     'pool_scale': 41.577,
     'ln1_g': 3.98,
     'ln1_b': 11.111,
     'ln2_g': 10.852,
     'ln2_b': 13.297}
    for name, (base, spread) in spreads.items():
        noise = np.random.default_rng([zlib.crc32(name.encode()), seed]).standard_normal(out[name].shape)
        drawn = base * np.exp(spread * noise) if base else spread * noise
        out[name] = __import__('jax').numpy.asarray(drawn.astype(out[name].dtype))
    for name, factor in factors.items():
        out[name] = (out[name] * factor).astype(out[name].dtype)
    return out
```

```python
from contextlib import ExitStack

import numpy as np

import concourse.bass as bass
from concourse import mybir

F32 = mybir.dt.float32
BF16 = mybir.dt.bfloat16
U32 = mybir.dt.uint32
ALU = mybir.AluOpType
ACT = mybir.ActivationFunctionType
AX = mybir.AxisListType

P = 128
BANK = 512
D = 1024
DK = D // P
DEPTH = 2
LAT, CTX, PAST = 512, 128, 128
TOK = LAT + CTX
NT = TOK // P
NLT = LAT // P
GW = 64
GR = LAT // GW
HD = 64
NH = 8
KVH = 2
BW = 512
BK = BW // P
WIN_R, WIN_C = 8, 16
NE = 16
FF = 1024
FK = FF // P
CAP_L = 2 * LAT // NE
CAP_C = 2 * CTX // NE
CAP = CAP_L + CAP_C
POOL_WINDOWS = (2, 4, 8, 16)
THETA = 10000.0
EPS = 1e-6
ALPHA = float((2 * DEPTH) ** 0.25)
QSCALE = HD ** -0.5

QC = P // GR
NB = GW // QC
KC = 32
KEY_COL = [min(max(QC * b - WIN_C // 2, 0), GW - KC) for b in range(NB)]
BIAS_W = KC + QC
BIAS_AT = [KEY_COL[b] - QC * b + QC for b in range(NB)]
NWIN = GR * KC
NA_KEYS = NWIN + PAST
MASKED = -(2.0 ** 99)

RING = 4
SLOT = DK * BANK
ADA_SLOTS = 12
MAIN = ["q", "k", "v", "gq", "gkv", "pool", "cc", "ch", "cb"]
SLOTS = [("ada", i) for i in range(ADA_SLOTS)] + [(m, 0) for m in MAIN]
for _dc in range(2):
    for _n in range(4):
        SLOTS += [("gate", 4 * _dc + _n), ("wb", 4 * _dc + _n)]
SLOTS += [("wo", 0), ("wo", 1)]
NSEQ = (len(SLOTS) + RING - 1) // RING * RING
PER_EXPERT = 6
EXPERTS_IN_BODY = 2
BODY_SLOTS = PER_EXPERT * EXPERTS_IN_BODY
assert BODY_SLOTS % RING == 0


def slot_of(key):
    s = SLOTS.index(key)
    return s % RING, s // RING


def uses_before_experts(r):
    return len([n for n in range(len(SLOTS)) if n % RING == r])


ATT = [(kind, b, h) for kind in ("na", "gqa") for b in range(NB + 1) for h in range(NH)]
NATT = len(ATT)
NBLK = NATT // NH
NA_UNITS = NATT // 2


def units_to_score(step):
    return [u for u in range(NATT) if max(u - (3 if u < NA_UNITS else 2), -1) == step]


def build_program(nc, x_sample, x_prompt, cna_k, cna_v, cg_k, cg_v, cond, small, w_ada, w_main, w_gkv,
                  w_gate_in, w_branch, w_out, bias_rows, pool_w, w_router, qk_gain, ln_p, w_exp,
                  ident_in, mask_in, rope_in, corr_in,
                  y_prompt, y_sample, st_na_k, st_na_v, st_g_k, st_g_v):
    with ExitStack() as ctx:
        def sb(name, shape, dt=F32):
            return ctx.enter_context(nc.sbuf_tensor(name, shape, dt))

        def sem(name):
            return ctx.enter_context(nc.semaphore(name))

        ring = sb("ring", [P, RING, SLOT])
        hT = sb("hT", [P, DK, TOK])
        br = sb("br", [P, 4, BK, TOK])
        shared = sb("shared", [P, 13568])
        work = sb("work", [P, 4224])
        ident = sb("ident", [P, P])
        ident_b = sb("ident_b", [P, P], BF16)
        mask_f = work[:, 0:3 * NWIN]
        mask_b = sb("mask_b", [P, 3, NWIN], BF16)
        rope = sb("rope", [P, NLT, 2, HD])
        corr = sb("corr", [P, 4, 16])
        gate_cols = sb("gate_cols", [P, 32])[:, :]
        eps = sb("eps", [P, 1])
        cvec = sb("cvec", [P, DK, 2])
        smallp = sb("smallp", [P, 68])
        mod = sb("mod", [P, 2, 48])
        gain = sb("gain", [P, 2, HD])
        poolw = sb("poolw", [P, 4, P])
        router = sb("router", [P, DK, NE])
        negmax = sb("negmax", [P, NATT])
        sums = sb("sums", [P, NATT])
        rsum = sb("rsum", [P, NATT])
        qk_ss = sb("qk_ss", [P, NT, 10])
        qk_std = sb("qk_std", [P, NT, 10])
        qk_rstd = sb("qk_rstd", [P, NT, 10])
        grow = sb("grow", [32, P])
        stats = sb("stats", [P, 2, NT, 12])
        mv = sb("mv", [P, 2, NT, 2])
        std = sb("std", [P, 2, NT])
        rstd = sb("rstd", [P, 2, NT])
        lg = sb("lg", [P, NT, 4 + NE])
        aff = sb("aff", [P, NT, NE])
        vals = sb("vals", [NE, CAP])
        idx_u = sb("idx_u", [NE, CAP], U32)
        idx_f = sb("idx_f", [NE, CAP])
        idx_t = sb("idx_t", [CAP, NE + 1], U32)
        g_t = sb("g_t", [CAP, NE + 1])
        idx_cur = sb("idx_cur", [CAP, 2], U32)
        g_cur = sb("g_cur", [CAP, 2])

        class Carve:
            def __init__(self, arena, size):
                self.arena, self.size, self.at = arena, size, 0

            def take(self, *dims):
                n = int(np.prod(dims))
                a = self.arena[:, self.at:self.at + n]
                self.at += n
                assert self.at <= self.size, (self.at, self.size)
                if len(dims) == 2:
                    a = a.rearrange("p (a b) -> p a b", a=dims[0])
                if len(dims) == 3:
                    a = a.rearrange("p (a b c) -> p a b c", a=dims[0], b=dims[1])
                return a

        c = Carve(shared, 13568)
        na_kT = c.take(BK, TOK + PAST)
        bias_at = c.at
        bias = c.take(NH, GR, BIAS_W)
        vwin = c.take(2 * NB, BW)
        vcache = c.take(BW)
        vctx = c.take(BW)
        gkT = c.take(KVH, TOK + PAST)
        gv = c.take(NT + 1, P)
        na_cached, g_cached = vwin[:, 0, :], vwin[:, 1, 0:P]
        xstage = shared[:, bias_at:bias_at + 2048].rearrange("p (a b) -> p a b", a=2)
        PW = 8 + LAT + 8 + 8 + CTX + 8
        pu = [shared[:, bias_at + i * PW:bias_at + (i + 1) * PW] for i in range(3)]
        c = Carve(shared, 13568)
        merged = c.take(DK, TOK)
        sg = c.take(2, TOK)
        prod = c.take(2, TOK)
        lng = c.take(D)
        lnb = c.take(D)
        gate1 = c.take(2, D)
        affT = sg.rearrange("p a b -> p (a b)")[0:NE, 0:TOK]
        xsT = c.take(2, DK * CAP)
        m = Carve(shared, DK * TOK)
        act_s = m.take(FF)[0:CAP, :]
        hdn = m.take(FF)[0:CAP, :]
        hdnT = m.take(FK * CAP)
        gate2 = m.take(D)[0:CAP, :]

        c = Carve(work, 4224)
        gtok = c.take(2, 768)
        t1 = c.take(640)
        t2 = c.take(640)
        kdup = c.take(2, 2 * P)
        c = Carve(work, 4224)
        probs = c.take(3, 640)
        pT = c.take(2, 640)
        otok = c.take(2, BW)
        conv_y = work[:, 0:TOK]
        adarow = work[0:2, 0:2 * BANK].rearrange("p (a b) -> p a b", a=2)
        k_state = work[:, 0:BW]

        qT = br[:, 0]
        gqT = br[:, 1]
        vstage = br[:, 3].rearrange("p a b -> p (a b)")[:, 0:NLT * BW].rearrange("p (t n) -> p t n", t=NLT)
        brf = br[:, :, :, :].rearrange("p a b c -> p (a b c)")
        zt = brf[:, 0:2048].rearrange("p (a b) -> p a b", a=2)
        x1 = brf[:, 2048:4096].rearrange("p (a b) -> p a b", a=2)
        xa = brf[:, 4096:6144].rearrange("p (a b) -> p a b", a=2)
        xin = brf[:, 6144:8192].rearrange("p (a b) -> p a b", a=2)
        xmT = brf[:, 8192:10240].rearrange("p (a b c) -> p a b c", a=2, b=DK)
        hf = hT[:, :, :].rearrange("p a b -> p (a b)")
        xs = hf[0:CAP, 0:2048].rearrange("p (a b) -> p a b", a=2)
        ye = hf[0:CAP, 2048:4096].rearrange("p (a b) -> p a b", a=2)

        acc = [ctx.enter_context(nc.psum_tensor(f"acc{i}", [P, 2, BANK], F32)) for i in range(4)]
        accf = [a[:, :, :].rearrange("p a b -> p (a b)") for a in acc]
        o_bank, ot_bank = acc[3][:, 0, :], acc[3][:, 1, :]

        v_scr = nc.dram_tensor("v_scr", [LAT, BW], F32, kind="Internal").ap()
        gate_scr = nc.dram_tensor("gate_scr", [32, P], F32, kind="Internal").ap()
        x1_scr = nc.dram_tensor("x1_scr", [TOK, D], F32, kind="Internal").ap()
        y_acc = nc.dram_tensor("y_acc", [TOK, D], F32, kind="Internal").ap()

        def out_rows(t):
            return y_sample[0, t * P:(t + 1) * P, :] if t < NLT else y_prompt[0, :, :]

        def bc(ap, *dims):
            return bass.AP(ap.tensor, ap.offset, [list(ap.ap[0])] + [list(d) for d in dims])

        consts_in = sem("consts_in")
        x_copied = sem("x_copied")
        const_ready = sem("const_ready")
        gather_done = sem("gather_done")
        scatter_done = sem("scatter_done")
        cleared_from = sem("cleared_from")
        slot_full = [sem(f"slot_full{r}") for r in range(RING)]
        x_in = [sem(f"x_in{i}") for i in range(2)]
        xin_in = [sem(f"xin_in{i}") for i in range(2)]
        x1_out = [sem(f"x1_out{i}") for i in range(2)]
        zin_in = [sem(f"zin_in{i}") for i in range(2)]
        x2_out = [sem(f"x2_out{i}") for i in range(2)]
        cond_in = sem("cond_in")
        small_in = sem("small_in")
        param_in = sem("param_in")
        ada_done = sem("ada_done")
        ada_copied = sem("ada_copied")
        mod_full = sem("mod_full")
        silu_ready = sem("silu_ready")
        xt_full = sem("xt_full")
        xt_copied = sem("xt_copied")
        mod_ready = sem("mod_ready")
        h_ready = sem("h_ready")
        gateT_full = sem("gateT_full")
        gateT_copied = sem("gateT_copied")
        gate_out = sem("gate_out")
        gate1_in = sem("gate1_in")
        ln1_in = sem("ln1_in")
        q_full = sem("q_full")
        q_copied = sem("q_copied")
        k_full = sem("k_full")
        k_copied = sem("k_copied")
        kcache_in = sem("kcache_in")
        kc_full = sem("kc_full")
        kc_copied = sem("kc_copied")
        ks_full = sem("ks_full")
        ks_copied = sem("ks_copied")
        v_full = sem("v_full")
        v_copied = sem("v_copied")
        vscr_out = sem("vscr_out")
        vwin_in = sem("vwin_in")
        cachev_in = sem("cachev_in")
        state_out = sem("state_out")
        g_full = sem("g_full")
        g_copied = sem("g_copied")
        ss_ready = sem("ss_ready")
        std_ready = sem("std_ready")
        gtok_ready = sem("gtok_ready")
        gt_full = sem("gt_full")
        gt_copied = sem("gt_copied")
        gc_dup = sem("gc_dup")
        gc_full = sem("gc_full")
        gc_copied = sem("gc_copied")
        pool_full = sem("pool_full")
        pool_ready = sem("pool_ready")
        mix_full = sem("mix_full")
        mix_copied = sem("mix_copied")
        c_full = sem("c_full")
        c_copied = sem("c_copied")
        ch_full = sem("ch_full")
        u_ready = sem("u_ready")
        cb_full = sem("cb_full")
        conv_ready = sem("conv_ready")
        bias_in = sem("bias_in")
        scores_full = sem("scores_full")
        rowmax_ready = sem("rowmax_ready")
        probs_ready = sem("probs_ready")
        pt_full = sem("pt_full")
        pt_copied_act = sem("pt_copied_act")
        pt_copied_dve = sem("pt_copied_dve")
        pv_done = sem("pv_done")
        o_copied = sem("o_copied")
        ot_full = sem("ot_full")
        ot_copied = sem("ot_copied")
        logit_full = sem("logit_full")
        sig_ready = sem("sig_ready")
        proj_full = sem("proj_full")
        merged_add = sem("merged_add")
        prod_done = sem("prod_done")
        y_full = sem("y_full")
        z_free = sem("z_free")
        var_ready = sem("var_ready")
        std1_ready = sem("std1_ready")
        x1_ready = sem("x1_ready")
        xa_ready = sem("xa_ready")
        x1T_full = sem("x1T_full")
        xmT_ready = sem("xmT_ready")
        r_full = sem("r_full")
        negl_ready = sem("negl_ready")
        el_ready = sem("el_ready")
        aff_ready = sem("aff_ready")
        affT_full = sem("affT_full")
        affT_copied = sem("affT_copied")
        topk_ready = sem("topk_ready")
        sel_full = sem("sel_full")
        sel_ready = sem("sel_ready")
        sel_cur = sem("sel_cur")
        xT_full = sem("xT_full")
        xsT_ready = sem("xsT_ready")
        gate0_done = sem("gate0_done")
        up0_done = sem("up0_done")
        gate1_done = sem("gate1_done")
        up1_done = sem("up1_done")
        down0_done = sem("down0_done")
        down1_done = sem("down1_done")
        silu_done = sem("silu_done")
        hidden_ready = sem("hidden_ready")
        hT_full = sem("hT_full")
        hT_copied = sem("hT_copied")
        gate2_in = sem("gate2_in")
        ye_ready = sem("ye_ready")
        ye_free = sem("ye_free")
        ln2_in = sem("ln2_in")
        var2_ready = sem("var2_ready")
        std2_ready = sem("std2_ready")
        x2_ready = sem("x2_ready")
        dve_step = sem("dve_step")
        dve_loop = sem("dve_loop")
        pool_turn = sem("pool_turn")
        cleared_to = sem("cleared_to")


        plan, freed_by = [], {}

        def unit(key, semaphore, count):
            freed_by[key] = (semaphore, count)
            plan.append(key)

        for t in range(NT):
            unit(("xt", t), xt_copied, t + 1)
        for i in range(ADA_SLOTS):
            unit(("ada", i), ada_copied, i + 1)
        unit(("gateT",), gateT_copied, 1)
        for f in range(BK):
            unit(("q", f), q_copied, 2 * f + 2)
        for f in range(BK):
            unit(("k", f), k_copied, f + 1)
        unit(("kc",), kc_copied, 1)
        unit(("ks",), ks_copied, 1)
        for t in range(NT):
            unit(("v", t), v_copied, t + 1)
        for t in range(NT + 1):
            if t < NT:
                unit(("g", t), g_copied, 2 * t + 2)
            if t >= 1:
                unit(("gt", t - 1), gt_copied, 2 * (t - 1) + 2)
        unit(("gc",), gc_copied, 1)
        for f in range(4):
            unit(("pool", f), pool_ready, 2 * f + 1)
        for f in range(BK):
            unit(("cc", f), c_copied, f + 1)
        for f in range(4):
            unit(("mix", f), mix_copied, f + 1)
        for f in range(BK):
            unit(("ch", f), u_ready, f + 1)
        for f in range(BK):
            unit(("cb", f), conv_ready, f + 1)
        AFTER_ATT = len(plan)
        for g in range(4 * DK):
            unit(("L", g), sig_ready, g + 1)
            unit(("B", g), prod_done, g + 1)
        for t in range(NT + 3):
            if t < NT:
                unit(("y", t), z_free, t + 1)
            if 2 <= t < NT + 2:
                unit(("r", t - 2), el_ready, t - 1)
            if t >= 3:
                unit(("affT", t - 3), affT_copied, t - 2)
            if 1 <= t < NT + 1:
                unit(("x1T", t - 1), xmT_ready, DK * t)
        unit(("sel",), sel_ready, 2)
        at = {key: n for n, key in enumerate(plan)}

        def pair(key):
            return at[key] % 3

        def scores_at(a):
            return accf[(a % 4) // 2][:, (a % 2) * BANK:] if a < NA_UNITS else accf[a % 2]

        def turned_at(a):
            return acc[2][:, a % 2, :] if a < NA_UNITS else accf[2]

        def out_at(block):
            return acc[3][:, block % 2, :]

        def turned_free(a):
            return (pt_copied_act, a + 1) if a < NA_UNITS else (pt_copied_dve, a - NA_UNITS + 1)

        def released(key):
            kind, n = key
            return {"ada": (ada_done, n + 1), "q": (q_full, BK), "k": (k_full, BK), "v": (v_full, NT),
                    "gq": (g_full, NT), "gkv": (g_full, NT), "pool": (pool_full, BK),
                    "cc": (c_full, BK), "ch": (ch_full, BK), "cb": (cb_full, BK),
                    "gate": (logit_full, 4 * n + 4), "wb": (proj_full, 4 * n + 4),
                    "wo": (y_full, NT)}[kind]

        part_done = [gate0_done, up0_done, gate1_done, up1_done, down0_done, down1_done]

        def key_tiles(a):
            kind, b, _ = ATT[a]
            return 1 if b == NB else (NA_KEYS if kind == "na" else LAT + PAST) // P

        def value_tile(a, j):
            kind, b, h = ATT[a]
            if kind == "na":
                cols = slice(h * HD, (h + 1) * HD)
                return vctx[:, cols] if b == NB else vwin[:, 2 * b + j, cols] if j < 2 else vcache[:, cols]
            g = h // (NH // KVH)
            tile = NT - 1 if b == NB else j if j < NLT else NT
            return gv[:, tile, g * HD:(g + 1) * HD]

        def bias_of(h, b):
            last = bias[:, h, GR - 1, BIAS_W - 1 - BIAS_AT[b]:BIAS_W - BIAS_AT[b]]
            return bc(last, (-BIAS_W, GR), (-1, KC))

        def group_cols(g):
            return slice(0, LAT) if g == 0 else slice(LAT, TOK)

        with nc.Block() as block:
            @block.sync
            def _(sp):
                sp.dma_start(y_sample[0], x_sample[0]).then_inc(x_copied, 16)
                sp.dma_start(y_prompt[0], x_prompt[0]).then_inc(x_copied, 16)
                sp.dma_start(ident[:], ident_in).then_inc(consts_in, 16)
                sp.dma_start(mask_f, mask_in).then_inc(consts_in, 16)
                sp.dma_start(rope[:], rope_in).then_inc(consts_in, 16)
                sp.dma_start(corr[:], corr_in).then_inc(consts_in, 16)
                sp.wait_ge(x_copied, 32)

            @block.vector
            def _(dve):
                nc.vector.memset(eps[:], EPS).then_inc(const_ready, 1)
                dve.wait_ge(consts_in, 64)
                nc.vector.tensor_copy(ident_b[:], ident[:]).then_inc(const_ready, 1)
                nc.vector.tensor_copy(mask_b[:].rearrange("p a b -> p (a b)"), mask_f).then_inc(const_ready, 1)
                dve.wait_ge(const_ready, 3)

        with nc.Fori(0, DEPTH) as layer:
            with nc.Block() as block:

                @block.sync
                def _(sp):
                    src = {"ada": lambda i: w_ada[layer, i], "gkv": lambda i: w_gkv[layer],
                           "gate": lambda i: w_gate_in[layer, i], "wb": lambda i: w_branch[layer, i],
                           "wo": lambda i: w_out[layer, i]}
                    for i, mname in enumerate(n for n in MAIN if n != "gkv"):
                        src[mname] = lambda _, i=i: w_main[layer, i]
                    sp.dma_start(cvec[:], cond).then_inc(cond_in, 16)
                    sp.dma_start(smallp[:], small[layer]).then_inc(small_in, 16)
                    for t in range(2):
                        sp.dma_start(xstage[:, t % 2, :], out_rows(t)).then_inc(x_in[t % 2], 16)
                    for n, key in enumerate(SLOTS):
                        r, use = slot_of(key)
                        a = src[key[0]](key[1])
                        if use >= 1:
                            sp.wait_ge(*released(SLOTS[n - RING]))
                        sp.dma_start(ring[:, r, 0:a.shape[1]], a).then_inc(slot_full[r], 16)
                        if n == 3:
                            for t in range(2, NT):
                                sp.wait_ge(xt_full, t - 1)
                                sp.dma_start(xstage[:, t % 2, :], out_rows(t)).then_inc(x_in[t % 2], 16)
                            sp.dma_start(na_cached, cna_k[layer]).then_inc(kcache_in, 16)
                            sp.dma_start(vcache, cna_v[layer]).then_inc(cachev_in, 16)
                            sp.dma_start(g_cached, cg_k[layer]).then_inc(kcache_in, 16)
                            sp.dma_start(gv[:, NT, :], cg_v[layer]).then_inc(cachev_in, 16)
                            sp.dma_start(gain[:].rearrange("p a b -> p (a b)"),
                                         bass.AP(qk_gain.tensor, qk_gain[layer].offset,
                                                 [[0, P], [1, 2 * HD]])).then_inc(param_in, 16)
                            sp.dma_start(poolw[:], pool_w[layer]).then_inc(param_in, 16)
                            sp.dma_start(router[:], w_router[layer]).then_inc(param_in, 16)
                    for n in range(RING):
                        if NSEQ + n - RING < len(SLOTS):
                            sp.wait_ge(*released(SLOTS[NSEQ + n - RING]))
                        elif NSEQ + n - 2 * RING >= 0:
                            sp.wait_ge(*released(SLOTS[NSEQ + n - 2 * RING]))
                        sp.dma_start(ring[:, n, :], w_exp[layer, 0, n]).then_inc(slot_full[n], 16)

                    def refill(i, n):
                        e, ahead = n // PER_EXPERT, n + RING
                        sp.wait_ge(part_done[n % PER_EXPERT], i * EXPERTS_IN_BODY + (e + 1))
                        sp.dma_start(ring[:, n % RING, :],
                                     w_exp[layer, i * EXPERTS_IN_BODY + ahead // PER_EXPERT, ahead % PER_EXPERT])\
                            .then_inc(slot_full[n % RING], 16)

                    last = NE // EXPERTS_IN_BODY - 1
                    with sp.Fori(0, last) as i:
                        for n in range(BODY_SLOTS):
                            refill(i, n)
                    for n in range(BODY_SLOTS - RING):
                        refill(last, n)

                @block.tensor
                def _(pe):
                    def acquire(key):
                        n = at[key]
                        if n >= 3 and not AFTER_ATT <= n < AFTER_ATT + 3:
                            pe.wait_ge(*freed_by[plan[n - 3]])
                        return accf[n % 3]

                    def arrived(key):
                        r, use = slot_of(key)
                        pe.wait_ge(slot_full[r], 16 * (use + 1))
                        return ring[:, r, :]

                    def feature_major(key, w, stride, col, n_k, rhs):
                        out = acquire(key)
                        for lo, hi, group in ((0, LAT, 0), (LAT, TOK, 1)):
                            for k in range(n_k):
                                mm = nc.tensor.matmul(out[:, lo:hi], w[:, k * stride + col:k * stride + col + P],
                                                      rhs(k, group), start=(k == 0), stop=(k == n_k - 1))
                        return mm

                    def h_cols(k, g):
                        return hT[:, k, group_cols(g)]

                    for t in range(NT):
                        pe.wait_ge(x_in[t % 2], 16 * (t // 2 + 1))
                        out = acquire(("xt", t))
                        for k in range(DK):
                            mm = nc.tensor.transpose(out[:, k * P:(k + 1) * P], xstage[:, t % 2, k * P:(k + 1) * P],
                                                     ident[:])
                        mm.then_inc(xt_full, 1)

                    pe.wait_ge(silu_ready, 1)
                    def turn_ada(i):
                        pe.wait_ge(ada_copied, i + 1)
                        for j in range(4):
                            c0 = 2 * (4 * i + j)
                            mm = nc.tensor.transpose(ot_bank[:, c0:c0 + 2], adarow[:, i % 2, j * P:(j + 1) * P],
                                                     ident[0:2, 0:2])
                        mm.then_inc(mod_full, 1)

                    for i in range(ADA_SLOTS):
                        w = arrived(("ada", i))
                        out = acquire(("ada", i))
                        for k in range(DK):
                            mm = nc.tensor.matmul(out[0:2, 0:BANK], cvec[:, k, :], w[:, k * BANK:(k + 1) * BANK],
                                                  start=(k == 0), stop=(k == DK - 1))
                        mm.then_inc(ada_done, 1)
                        if i:
                            turn_ada(i - 1)
                    turn_ada(ADA_SLOTS - 1)
                    pe.wait_ge(mod_ready, 2)
                    out = acquire(("gateT",))
                    nc.tensor.transpose(out[0:32, 0:P], gate_cols, ident[:]).then_inc(gateT_full, 1)

                    pe.wait_ge(h_ready, 2 * DK)
                    for key, full in (("q", q_full), ("k", k_full)):
                        w = arrived((key, 0))
                        for f in range(BK):
                            mm = feature_major((key, f), w, BANK, f * P, DK, h_cols)
                            mm.then_inc(full, 1)
                    pe.wait_ge(kcache_in, 32)
                    out = acquire(("kc",))
                    for f in range(BK):
                        mm = nc.tensor.transpose(out[:, f * P:(f + 1) * P], na_cached[:, f * P:(f + 1) * P],
                                                 ident[:])
                    mm.then_inc(kc_full, 1)
                    pe.wait_ge(k_copied, BK)
                    out = acquire(("ks",))
                    for f in range(BK):
                        mm = nc.tensor.transpose(out[:, f * P:(f + 1) * P], na_kT[:, f, LAT:TOK], ident[:])
                    mm.then_inc(ks_full, 1)

                    w = arrived(("v", 0))
                    for t in range(NT):
                        out = acquire(("v", t))
                        for k in range(DK):
                            mm = nc.tensor.matmul(out[:, 0:BW], hT[:, k, t * P:(t + 1) * P],
                                                  w[:, k * BANK:(k + 1) * BANK], start=(k == 0), stop=(k == DK - 1))
                        mm.then_inc(v_full, 1)

                    wq = arrived(("gq", 0))
                    wkv = arrived(("gkv", 0))
                    for t in range(NT + 1):
                        if t < NT:
                            out = acquire(("g", t))
                            for k in range(DK):
                                nc.tensor.matmul(out[:, 0:BW], hT[:, k, t * P:(t + 1) * P],
                                                 wq[:, k * BANK:(k + 1) * BANK], start=(k == 0), stop=(k == DK - 1))
                            for k in range(DK):
                                mm = nc.tensor.matmul(out[:, BW:BW + 2 * P], hT[:, k, t * P:(t + 1) * P],
                                                      wkv[:, k * 2 * P:(k + 1) * 2 * P],
                                                      start=(k == 0), stop=(k == DK - 1))
                            mm.then_inc(g_full, 1)
                        if t >= 1:
                            pe.wait_ge(gtok_ready, t)
                            out = acquire(("gt", t - 1))
                            for f in range(BK):
                                nc.tensor.transpose(out[:, f * P:(f + 1) * P],
                                                    gtok[:, (t - 1) % 2, f * P:(f + 1) * P], ident[:])
                            for g in range(KVH):
                                mm = nc.tensor.transpose(out[:, BW + g * P:BW + (g + 1) * P],
                                                         kdup[:, (t - 1) % 2, g * P:(g + 1) * P], ident[:])
                            mm.then_inc(gt_full, 1)
                    pe.wait_ge(gc_dup, 1)
                    out = acquire(("gc",))
                    for g in range(KVH):
                        mm = nc.tensor.transpose(out[:, g * P:(g + 1) * P], kdup[:, NT % 2, g * P:(g + 1) * P], ident[:])
                    mm.then_inc(gc_full, 1)

                    for key, full in (("pool", pool_full), ("cc", c_full)):
                        w = arrived((key, 0))
                        for f in range(BK):
                            feature_major((key, f), w, BANK, f * P, DK, h_cols).then_inc(full, 1)
                    pe.wait_ge(param_in, 48)
                    for f in range(4):
                        pe.wait_ge(pool_ready, 2 * f + 2)
                        feature_major(("mix", f), poolw[:, f, :], 0, 0, 1,
                                      lambda k, g: br[:, 3, f, group_cols(g)]).then_inc(mix_full, 1)
                    for key, full in (("ch", ch_full), ("cb", cb_full)):
                        w = arrived((key, 0))
                        for f in range(BK):
                            feature_major((key, f), w, BANK, f * P, DK, h_cols).then_inc(full, 1)

                    def scores(a):
                        kind, b, h = ATT[a]
                        if a < NA_UNITS:
                            if a >= 4:
                                pe.wait_ge(probs_ready, a - 3)
                        else:
                            pe.wait_ge(probs_ready, a - 1)
                        out = scores_at(a)
                        half = slice(HD * (h % 2), HD * (h % 2) + HD)
                        q = (qT if kind == "na" else gqT)[half, h // 2, b * P:(b + 1) * P]
                        if kind == "na":
                            kt = na_kT[half, h // 2, :]
                            if b < NB:
                                win = kt[:, 0:LAT].rearrange("p (r c) -> p r c", c=GW)[:, :, KEY_COL[b]:KEY_COL[b] + KC]
                                nc.tensor.matmul(out[:, 0:NWIN], q, win, start=True, stop=False)
                                nc.tensor.matmul(out[:, 0:NWIN], ident_b[:], mask_b[:, (0, 1, 1, 2)[b], :],
                                                 start=False, stop=True)
                                mm = nc.tensor.matmul(out[:, NWIN:NA_KEYS], q, kt[:, TOK:TOK + PAST],
                                                      start=True, stop=True)
                            else:
                                mm = nc.tensor.matmul(out[:, 0:CTX], q, kt[:, LAT:TOK], start=True, stop=True)
                        else:
                            kt = gkT[half, h // (NH // KVH), :]
                            if b < NB:
                                nc.tensor.matmul(out[:, 0:LAT], q, kt[:, 0:LAT], start=True, stop=True)
                                mm = nc.tensor.matmul(out[:, LAT:LAT + PAST], q, kt[:, TOK:TOK + PAST],
                                                      start=True, stop=True)
                            else:
                                mm = nc.tensor.matmul(out[:, 0:CTX], q, kt[:, LAT:TOK], start=True, stop=True)
                        mm.then_inc(scores_full, 1)

                    def turn_probs(a):
                        pe.wait_ge(probs_ready, a + 1)
                        if a >= 2:
                            pe.wait_ge(*turned_free(a - 2 if a < NA_UNITS else a - 1))
                        out = turned_at(a)
                        for j in range(key_tiles(a)):
                            mm = nc.tensor.transpose(out[:, j * P:(j + 1) * P], probs[:, a % 3, j * P:(j + 1) * P],
                                                     ident[:])
                        mm.then_inc(pt_full, 1)

                    def values(a):
                        n, h = key_tiles(a), ATT[a][2]
                        pe.wait_ge(*turned_free(a))
                        if h == 0 and a >= 2 * NH:
                            pe.wait_ge(ot_copied, a // NH - 1)
                        for j in range(n):
                            mm = nc.tensor.matmul(out_at(a // NH)[:, h * HD:(h + 1) * HD],
                                                  pT[:, a % 2, j * P:(j + 1) * P],
                                                  value_tile(a, j), start=(j == 0), stop=(j == n - 1))
                        mm.then_inc(pv_done, 1)

                    def turn_block(j):
                        pe.wait_ge(o_copied, j + 1)
                        for f in range(BK):
                            mm = nc.tensor.transpose(out_at(j)[:, f * P:(f + 1) * P], otok[:, j % 2, f * P:(f + 1) * P],
                                                     ident[:])
                        mm.then_inc(ot_full, 1)

                    pe.wait_ge(gt_copied, 2 * NT)
                    pe.wait_ge(gc_copied, 1)
                    pe.wait_ge(kc_copied, 1)
                    pe.wait_ge(vwin_in, 16 * 2 * NB)
                    pe.wait_ge(cachev_in, 32)
                    pe.wait_ge(conv_ready, BK)
                    pe.wait_ge(mix_copied, 4)
                    for a in range(-1, NATT):
                        for u in units_to_score(a):
                            scores(u)
                        if a + 1 < NATT:
                            turn_probs(a + 1)
                        if a >= 0:
                            values(a)
                        if a % NH == 1 and a > NH:
                            turn_block(a // NH - 1)
                    turn_block(NBLK - 1)

                    def branch_cols(n):
                        def rhs(k, g):
                            if n == 0 and g == 0:
                                return br[:, 0, k, 0:LAT].rearrange("p (b i r) -> p r b i", b=NB, i=QC)
                            return br[:, n, k, group_cols(g)]
                        return rhs

                    pe.wait_ge(ot_copied, NBLK)
                    pe.wait_ge(*turned_free(NATT - 1))
                    for gi in range(2 * 4):
                        n = gi % 4
                        wl = arrived(("gate", gi))
                        wb = arrived(("wb", gi))
                        for d in range(4):
                            g = 4 * gi + d
                            feature_major(("L", g), wl, BANK, d * P, DK, h_cols).then_inc(logit_full, 1)
                            feature_major(("B", g), wb, BANK, d * P, BK, branch_cols(n)).then_inc(proj_full, 1)

                    pe.wait_ge(merged_add, 2 * 4 * 4 - 2 * 4)
                    pe.wait_ge(prod_done, 4 * DK)
                    wo = [arrived(("wo", j)) for j in range(2)]
                    for t in range(NT + 3):
                        if t < NT:
                            out = acquire(("y", t))
                            for j in range(2):
                                for k in range(DK):
                                    mm = nc.tensor.matmul(out[:, j * BANK:(j + 1) * BANK], merged[:, k, t * P:(t + 1) * P],
                                                          wo[j][:, k * BANK:(k + 1) * BANK],
                                                          start=(k == 0), stop=(k == DK - 1))
                            mm.then_inc(y_full, 1)
                        if 2 <= t < NT + 2:
                            pe.wait_ge(xmT_ready, DK * (t - 1))
                            out = acquire(("r", t - 2))
                            for k in range(DK):
                                mm = nc.tensor.matmul(out[:, 0:NE], xmT[:, t % 2, k, :], router[:, k, :],
                                                      start=(k == 0), stop=(k == DK - 1))
                            mm.then_inc(r_full, 1)
                        if t >= 3:
                            pe.wait_ge(aff_ready, t - 2)
                            out = acquire(("affT", t - 3))
                            nc.tensor.transpose(out[0:NE, 0:P], aff[:, t - 3, :], ident[:]).then_inc(affT_full, 1)
                        if 1 <= t < NT + 1:
                            pe.wait_ge(x1_ready, t)
                            out = acquire(("x1T", t - 1))
                            for k in range(DK):
                                mm = nc.tensor.transpose(out[:, k * P:(k + 1) * P],
                                                         x1[:, (t - 1) % 2, k * P:(k + 1) * P], ident[:])
                            mm.then_inc(x1T_full, 1)
                    pe.wait_ge(topk_ready, 1)
                    out = acquire(("sel",))
                    nc.tensor.transpose(out[0:CAP, 0:NE], idx_f[:, :], ident[0:NE, 0:NE])
                    nc.tensor.transpose(out[0:CAP, NE:2 * NE], vals[:, :], ident[0:NE, 0:NE]).then_inc(sel_full, 1)

                    def part_waits(i, j, part):
                        n = PER_EXPERT * j + part
                        r = n % RING
                        pe.wait_ge(slot_full[r], i * (16 * BODY_SLOTS // RING)
                                   + 16 * (uses_before_experts(r) + n // RING + 1))
                        return ring[:, r, :]

                    def half_product(i, j, part, lhsT, pair_no, half):
                        w = part_waits(i, j, part)
                        for k in range(DK):
                            mm = nc.tensor.matmul(acc[pair_no][0:CAP, half, :], lhsT[:, k * CAP:(k + 1) * CAP],
                                                  w[:, k * BANK:(k + 1) * BANK], start=(k == 0), stop=(k == DK - 1))
                        mm.then_inc(part_done[part], 1)

                    def down_product(i, j, half):
                        w = part_waits(i, j, 4 + half)
                        for c in range(2):
                            for k in range(4):
                                kk = 4 * half + k
                                mm = nc.tensor.matmul(acc[2][0:CAP, c, :], hdnT[:, kk * CAP:(kk + 1) * CAP],
                                                      w[:, k * D + c * BANK:k * D + (c + 1) * BANK],
                                                      start=(kk == 0), stop=(kk == DK - 1))
                        mm.then_inc(part_done[4 + half], 1)

                    def turn_hidden(half):
                        for k in range(4):
                            mm = nc.tensor.transpose(acc[3][:, 0, k * CAP:(k + 1) * CAP],
                                                     hdn[:, half * BANK + k * P:half * BANK + (k + 1) * P],
                                                     ident[0:CAP, 0:CAP])
                        mm.then_inc(hT_full, 1)

                    def turn_rows(j, half):
                        for k in range(4):
                            mm = nc.tensor.transpose(acc[3][:, 1, k * CAP:(k + 1) * CAP],
                                                     xs[:, j, (4 * half + k) * P:(4 * half + k + 1) * P],
                                                     ident[0:CAP, 0:CAP])
                        mm.then_inc(xT_full, 1)

                    pe.wait_ge(gather_done, layer * (16 * (NE + 1)) + 16)
                    turn_rows(0, 0)
                    pe.wait_ge(xsT_ready, 1)
                    turn_rows(0, 1)
                    with pe.Fori(0, NE // EXPERTS_IN_BODY) as i:
                        for j in range(EXPERTS_IN_BODY):
                            e1 = i * EXPERTS_IN_BODY + (j + 1)
                            e2 = i * (2 * EXPERTS_IN_BODY) + 2 * (j + 1)
                            pe.wait_ge(xsT_ready, e2)
                            pe.wait_ge(silu_done, e2 - 1)
                            half_product(i, j, 0, xsT[:, j, :], 0, 0)
                            pe.wait_ge(hidden_ready, e2 - 1)
                            half_product(i, j, 1, xsT[:, j, :], 1, 0)
                            pe.wait_ge(silu_done, e2)
                            half_product(i, j, 2, xsT[:, j, :], 0, 1)
                            pe.wait_ge(hidden_ready, e2 + 1)
                            pe.wait_ge(hT_copied, e2)
                            turn_hidden(0)
                            half_product(i, j, 3, xsT[:, j, :], 1, 1)
                            pe.wait_ge(gather_done, layer * (16 * (NE + 1)) + i * (16 * EXPERTS_IN_BODY) + 16 * (j + 2))
                            turn_rows(1 - j, 0)
                            pe.wait_ge(hT_copied, e2 + 1)
                            pe.wait_ge(ye_ready, e1)
                            down_product(i, j, 0)
                            pe.wait_ge(hidden_ready, e2 + 2)
                            turn_hidden(1)
                            pe.wait_ge(xsT_ready, e2 + 1)
                            turn_rows(1 - j, 1)
                            pe.wait_ge(hT_copied, e2 + 2)
                            down_product(i, j, 1)

                @block.scalar
                def _(act):
                    copy = ACT.Copy
                    act.wait_ge(cond_in, 16)
                    nc.scalar.activation(cvec[:], cvec[:], ACT.Silu).then_inc(silu_ready, 1)
                    for t in range(NT):
                        act.wait_ge(xt_full, t + 1)
                        nc.scalar.activation(hT[:, :, t * P:(t + 1) * P],
                                             accf[pair(("xt", t))].rearrange("p (k n) -> p k n", k=DK), copy)\
                            .then_inc(xt_copied, 1)
                    for i in range(ADA_SLOTS):
                        act.wait_ge(ada_done, i + 1)
                        if i >= 2:
                            act.wait_ge(mod_full, i - 1)
                        nc.scalar.activation(adarow[:, i % 2, :], accf[pair(("ada", i))][0:2, 0:BANK], copy)\
                            .then_inc(ada_copied, 1)
                    act.wait_ge(gateT_full, 1)
                    nc.scalar.activation(grow[:], accf[pair(("gateT",))][0:32, 0:P], copy).then_inc(gateT_copied, 1)
                    act.wait_ge(gateT_copied, 1)
                    act.dma_start(gate_scr, grow[:]).then_inc(gate_out, 16)
                    for f in range(BK):
                        act.wait_ge(q_full, f + 1)
                        a = accf[pair(("q", f))]
                        nc.scalar.activation(qT[:, f, 0:LAT].rearrange("p (b i r) -> p r b i", b=NB, i=QC),
                                             a[:, 0:LAT].rearrange("p (r b i) -> p r b i", r=GR, b=NB),
                                             copy, scale=QSCALE).then_inc(q_copied, 1)
                        nc.scalar.activation(qT[:, f, LAT:TOK], a[:, LAT:TOK], copy, scale=QSCALE)\
                            .then_inc(q_copied, 1)
                    for f in range(BK):
                        act.wait_ge(k_full, f + 1)
                        nc.scalar.activation(na_kT[:, f, 0:TOK], accf[pair(("k", f))][:, 0:TOK], copy)\
                            .then_inc(k_copied, 1)
                    act.wait_ge(kc_full, 1)
                    nc.scalar.activation(na_kT[:, :, TOK:TOK + PAST],
                                         accf[pair(("kc",))][:, 0:BW].rearrange("p (f n) -> p f n", f=BK), copy)\
                        .then_inc(kc_copied, 1)
                    act.wait_ge(ks_full, 1)
                    nc.scalar.activation(k_state, accf[pair(("ks",))][:, 0:BW], copy).then_inc(ks_copied, 1)
                    act.wait_ge(ks_copied, 1)
                    act.dma_start(st_na_k[layer], k_state).then_inc(state_out, 16)
                    for t in range(NT):
                        act.wait_ge(v_full, t + 1)
                        nc.scalar.activation(vstage[:, t, :] if t < NLT else vctx, accf[pair(("v", t))][:, 0:BW], copy)\
                            .then_inc(v_copied, 1)
                    act.wait_ge(v_copied, NT)
                    act.dma_start(st_na_v[layer], vctx).then_inc(state_out, 16)
                    act.dma_start(v_scr.rearrange("(t p) n -> p t n", p=P), vstage).then_inc(vscr_out, 16)

                    act.wait_ge(state_out, 32)
                    for t in range(NT + 1):
                        if t < NT:
                            act.wait_ge(g_full, t + 1)
                            a = accf[pair(("g", t))]
                            if t >= 2:
                                act.wait_ge(gt_full, t - 1)
                            nc.scalar.activation(gtok[:, t % 2, 0:640], a[:, 0:640], copy).then_inc(g_copied, 1)
                            nc.scalar.activation(gv[:, t, :], a[:, 640:768], copy).then_inc(g_copied, 1)
                            act.wait_ge(ss_ready, t + 1)
                            nc.scalar.activation(qk_std[:, t, :], qk_ss[:, t, :], ACT.Sqrt, bias=eps[:, 0:1],
                                                 scale=1.0 / HD).then_inc(std_ready, 1)
                        if t >= 1:
                            act.wait_ge(gt_full, t)
                            a = accf[pair(("gt", t - 1))]
                            c0 = (t - 1) * P
                            nc.scalar.activation(gqT[:, :, c0:c0 + P],
                                                 a[:, 0:BW].rearrange("p (f n) -> p f n", f=BK), copy, scale=QSCALE)\
                                .then_inc(gt_copied, 1)
                            nc.scalar.activation(gkT[:, :, c0:c0 + P],
                                                 a[:, BW:BW + 2 * P].rearrange("p (f n) -> p f n", f=KVH), copy)\
                                .then_inc(gt_copied, 1)
                    act.wait_ge(gtok_ready, NT)
                    act.dma_start(st_g_k[layer], gtok[:, (NT - 1) % 2, BW:BW + P]).then_inc(state_out, 16)
                    act.wait_ge(g_copied, 2 * NT)
                    act.dma_start(st_g_v[layer], gv[:, NT - 1, :]).then_inc(state_out, 16)
                    act.wait_ge(gc_full, 1)
                    nc.scalar.activation(gkT[:, :, TOK:TOK + PAST],
                                         accf[pair(("gc",))][:, 0:2 * P].rearrange("p (f n) -> p f n", f=KVH), copy)\
                        .then_inc(gc_copied, 1)
                    act.wait_ge(vscr_out, 16)
                    act.wait_ge(kc_full, 1)
                    act.wait_ge(gc_dup, 1)
                    for b in range(NB):
                        for half in range(2):
                            rows = v_scr.rearrange("(r c) n -> r c n", c=GW)[4 * half:4 * half + 4,
                                                                           KEY_COL[b]:KEY_COL[b] + KC, :]
                            act.dma_start(vwin[:, 2 * b + half, :], rows).then_inc(vwin_in, 16)
                    for f in range(BK):
                        act.wait_ge(c_full, f + 1)
                        nc.scalar.activation(br[:, 2, f, :], accf[pair(("cc", f))][:, 0:TOK], copy).then_inc(c_copied, 1)
                    act.wait_ge(small_in, 16)
                    for f in range(4):
                        act.wait_ge(mix_full, f + 1)
                        nc.scalar.activation(br[:, 3, f, :], accf[pair(("mix", f))][:, 0:TOK], copy,
                                             scale=smallp[:, 64 + f:65 + f]).then_inc(mix_copied, 1)
                    act.wait_ge(mix_full, 4)
                    act.wait_ge(pool_ready, 8)
                    for r in range(GR):
                        for rr in range(GR):
                            a = bias_rows[layer]
                            srcap = bass.AP(a.tensor, a.offset + (r + rr) * 64, [[1, QC], [15 * 64, NH], [1, BIAS_W]])
                            dst = bias[r:P:GR, :, rr, :]
                            act.dma_start(dst, srcap).then_inc(bias_in, 16)

                    def exps(a):
                        n = key_tiles(a) * P
                        act.wait_ge(rowmax_ready, a + 1)
                        if a >= 3:
                            act.wait_ge(pt_full, a - 2)
                        nc.scalar.activation(probs[:, a % 3, 0:n], scores_at(a)[:, 0:n], ACT.Exp,
                                             bias=negmax[:, a:a + 1], accum_out=sums[:, a:a + 1])\
                            .then_inc(probs_ready, 1)

                    def block_out(j):
                        kind, b, _ = ATT[j * NH]
                        act.wait_ge(ot_full, j + 1)
                        dst = (qT if kind == "na" else gqT)[:, :, b * P:(b + 1) * P]
                        nc.scalar.activation(dst, out_at(j).rearrange("p (f n) -> p f n", f=BK), copy)\
                            .then_inc(ot_copied, 1)

                    act.wait_ge(state_out, 64)
                    for a in range(-1, NATT):
                        for u in units_to_score(a):
                            exps(u)
                        if a + 1 < NA_UNITS:
                            n = key_tiles(a + 1) * P
                            act.wait_ge(pt_full, a + 2)
                            if a >= 1:
                                act.wait_ge(pv_done, a)
                            nc.scalar.activation(pT[:, (a + 1) % 2, 0:n], turned_at(a + 1)[:, 0:n], copy)\
                                .then_inc(pt_copied_act, 1)
                        if a % NH == 1 and a > NH:
                            block_out(a // NH - 1)
                    block_out(NBLK - 1)

                    act.wait_ge(ot_copied, NBLK)
                    act.wait_ge(gate_out, 16)
                    for n, dst in ((0, lng), (1, lnb)):
                        a = ln_p[layer, n]
                        act.dma_start(dst, bass.AP(a.tensor, a.offset, [[0, P], [1, D]])).then_inc(ln1_in, 16)
                    for g in range(2):
                        act.dma_start(gate1[:, g, :].rearrange("p (k n) -> p k n", k=DK),
                                      bass.AP(gate_scr.tensor, gate_scr.offset + g * P, [[0, P], [2 * P, DK], [1, P]]))\
                            .then_inc(gate1_in, 16)
                    for g in range(4 * DK):
                        act.wait_ge(logit_full, g + 1)
                        if g >= 2:
                            act.wait_ge(prod_done, g - 1)
                        nc.scalar.activation(sg[:, g % 2, :], accf[pair(("L", g))][:, 0:TOK], ACT.Sigmoid)\
                            .then_inc(sig_ready, 1)

                    def load_x(t):
                        if t >= 2:
                            act.wait_ge(z_free, t - 1)
                        act.dma_start(xin[:, t % 2, :], out_rows(t)).then_inc(xin_in[t % 2], 16)

                    act.wait_ge(prod_done, 4 * DK)
                    load_x(0)
                    load_x(1)
                    for t in range(NT + 2):
                        if t < NT:
                            act.wait_ge(var_ready, t + 1)
                            nc.scalar.activation(std[:, 0, t:t + 1], mv[:, 0, t, 1:2], ACT.Sqrt, bias=eps[:, 0:1])\
                                .then_inc(std1_ready, 1)
                            if t + 2 < NT:
                                load_x(t + 2)
                            act.wait_ge(x1_ready, t + 1)
                            act.dma_start(x1_scr[t * P:(t + 1) * P, :], x1[:, t % 2, :]).then_inc(x1_out[t % 2], 16)
                            act.wait_ge(xa_ready, t + 1)
                            act.dma_start(y_acc[t * P:(t + 1) * P, :], xa[:, t % 2, :]).then_inc(x1_out[t % 2], 16)
                        if t >= 2:
                            act.wait_ge(negl_ready, t - 1)
                            nc.scalar.activation(lg[:, t - 2, 4:4 + NE], accf[pair(("r", t - 2))][:, 0:NE], ACT.Exp,
                                                 bias=lg[:, t - 2, 1:2], accum_out=lg[:, t - 2, 2:3])\
                                .then_inc(el_ready, 1)
                        if 1 <= t < NT + 1:
                            act.wait_ge(x1T_full, t)
                            if t >= 3:
                                act.wait_ge(r_full, t - 2)
                            g = 0 if t - 1 < NLT else 1
                            for k in range(DK):
                                nc.scalar.activation(xmT[:, (t - 1) % 2, k, :],
                                                     accf[pair(("x1T", t - 1))][:, k * P:(k + 1) * P], ACT.Identity,
                                                     scale=mod[:, g, 32 + k:33 + k], bias=mod[:, g, 24 + k:25 + k])\
                                    .then_inc(xmT_ready, 1)

                    act.sem_inc(silu_done, 2)
                    act.sem_inc(hT_copied, 2)
                    act.wait_ge(xa_ready, NT)
                    for n, dst in ((2, lng), (3, lnb)):
                        a = ln_p[layer, n]
                        act.dma_start(dst, bass.AP(a.tensor, a.offset, [[0, P], [1, D]])).then_inc(ln2_in, 16)
                    act.wait_ge(y_full, NT)
                    for g, lo, hi in ((0, 0, CAP_L), (1, CAP_L, CAP)):
                        act.dma_start(gate2[lo:hi, :].rearrange("p (k n) -> p k n", k=DK),
                                      bass.AP(gate_scr.tensor, gate_scr.offset + (16 + g) * P,
                                              [[0, hi - lo], [2 * P, DK], [1, P]])).then_inc(gate2_in, 16)
                    with act.Fori(0, NE // EXPERTS_IN_BODY) as i:
                        for j in range(EXPERTS_IN_BODY):
                            e1 = i * EXPERTS_IN_BODY + (j + 1)
                            e2 = i * (2 * EXPERTS_IN_BODY) + 2 * (j + 1)
                            for half, done in ((0, gate0_done), (1, gate1_done)):
                                cols = slice(half * BANK, (half + 1) * BANK)
                                act.wait_ge(done, e1)
                                act.wait_ge(hidden_ready, e2 - 1 + half)
                                nc.scalar.activation(act_s[:, cols], acc[0][0:CAP, half, :], ACT.Silu)\
                                    .then_inc(silu_done, 1)
                            for half in range(2):
                                act.wait_ge(hT_full, e2 - 1 + half)
                                nc.scalar.activation(hdnT[:, half * 4 * CAP:(half + 1) * 4 * CAP],
                                                     acc[3][:, 0, 0:4 * CAP], copy).then_inc(hT_copied, 1)

                    act.wait_ge(scatter_done, layer * (16 * NE) + 16 * NE)
                    for t in range(2):
                        act.dma_start(xin[:, t % 2, :], y_acc[t * P:(t + 1) * P, :]).then_inc(zin_in[t % 2], 16)
                    for t in range(NT):
                        act.wait_ge(var2_ready, t + 1)
                        nc.scalar.activation(std[:, 1, t:t + 1], mv[:, 1, t, 1:2], ACT.Sqrt, bias=eps[:, 0:1])\
                            .then_inc(std2_ready, 1)
                        act.wait_ge(x2_ready, t + 1)
                        act.dma_start(out_rows(t), x1[:, t % 2, :]).then_inc(x2_out[t % 2], 16)
                        if t + 2 < NT:
                            act.dma_start(xin[:, t % 2, :], y_acc[(t + 2) * P:(t + 3) * P, :]).then_inc(zin_in[t % 2], 16)
                    for p in range(2):
                        act.wait_ge(x2_out[p], 16 * ((NT + 1 - p) // 2))

                @block.vector
                def _(dve):
                    v = nc.vector
                    chained = [0]

                    def link(ins):
                        chained[0] += 1
                        ins.then_inc(dve_step, 1)
                        dve.wait_ge(dve_step, chained[0])

                    dve.wait_ge(small_in, 16)
                    dve.wait_ge(mod_full, ADA_SLOTS)
                    a = ot_bank
                    v.tensor_tensor(mod[:].rearrange("p g c -> p c g"),
                                    a[:, 0:96].rearrange("p (c g) -> p c g", g=2),
                                    bc(smallp[:, 0:48], (1, 48), (0, 2)), ALU.add).then_inc(mod_ready, 1)
                    dve.wait_ge(mod_ready, 1)
                    sc = bc(mod[:, 0, 8:16], (48, 2), (24, 2), (1, 8))
                    v.tensor_scalar(sc, sc, 1.0, None, ALU.add).then_inc(dve_step, 1)
                    chained[0] += 1
                    v.tensor_copy(gate_cols.rearrange("p (j k g) -> p j k g", j=2, g=2),
                                  bc(mod[:, 0, 16:24], (24, 2), (1, DK), (48, 2))).then_inc(mod_ready, 1)
                    dve.wait_ge(dve_step, chained[0])
                    dve.wait_ge(xt_copied, NT)
                    for k in range(DK):
                        for g in range(2):
                            x = hT[:, k, group_cols(g)]
                            v.tensor_scalar(x, x, mod[:, g, 8 + k:9 + k], mod[:, g, k:k + 1], ALU.mult, ALU.add)\
                                .then_inc(h_ready, 1)

                    def duplicate(dst, src):
                        return v.tensor_copy(dst.rearrange("p (g c n) -> p g c n", g=KVH, c=2),
                                             bc(src, (HD, KVH), (0, 2), (1, HD)))

                    dve.wait_ge(param_in, 48)
                    for t in range(NT):
                        x = gtok[:, t % 2, 0:640]
                        dve.wait_ge(g_copied, 2 * t + 2)
                        link(v.tensor_tensor(t1, x, x, ALU.mult))
                        v.tensor_reduce(qk_ss[:, t, :], t1.rearrange("p (h d) -> p h d", d=HD), AX.X, ALU.add)\
                            .then_inc(ss_ready, 1)
                        dve.wait_ge(std_ready, t + 1)
                        link(v.reciprocal(qk_rstd[:, t, :], qk_std[:, t, :]))
                        xh = x.rearrange("p (h d) -> p h d", d=HD)
                        link(v.tensor_tensor(xh, xh, bc(qk_rstd[:, t, :], (1, 10), (0, HD)), ALU.mult))
                        link(v.tensor_tensor(xh[:, 0:NH, :], xh[:, 0:NH, :], bc(gain[:, 0, :], (0, NH), (1, HD)), ALU.mult))
                        link(v.tensor_tensor(xh[:, NH:10, :], xh[:, NH:10, :], bc(gain[:, 1, :], (0, KVH), (1, HD)), ALU.mult))
                        if t < NLT:
                            link(v.tensor_tensor(t1.rearrange("p (h d) -> p h d", d=HD), xh,
                                                 bc(rope[:, t, 0, :], (0, 10), (1, HD)), ALU.mult))
                            link(v.tensor_tensor(t2.rearrange("p (h d) -> p h d", d=HD), xh,
                                                 bc(rope[:, t, 1, :], (0, 10), (1, HD)), ALU.mult))
                            x4, c4, s4 = (z.rearrange("p (h q n) -> p h q n", h=20, q=2) for z in (x, t1, t2))
                            link(v.tensor_tensor(x4[:, :, 0, :], c4[:, :, 0, :], s4[:, :, 1, :], ALU.subtract))
                            link(v.tensor_tensor(x4[:, :, 1, :], s4[:, :, 0, :], c4[:, :, 1, :], ALU.add))
                        if t >= 2:
                            dve.wait_ge(gt_full, t - 1)
                        duplicate(kdup[:, t % 2, :], x[:, BW:BW + P]).then_inc(gtok_ready, 1)
                    dve.wait_ge(kcache_in, 32)
                    dve.wait_ge(gt_full, NT - 1)
                    duplicate(kdup[:, NT % 2, :], g_cached).then_inc(gc_dup, 1)

                    dve.wait_ge(xt_full, NT)
                    dve.wait_ge(vscr_out, 16)
                    for i in range(3):
                        link(v.memset(pu[i], 0.0))
                    for f, win in enumerate(POOL_WINDOWS):
                        dve.wait_ge(pool_full, f + 1)
                        if f:
                            dve.wait_ge(pool_ready, 2 * f)
                        a = accf[pair(("pool", f))]
                        u, wa, wb = pu[0], pu[1], pu[2]
                        link(v.tensor_copy(u[:, 8:8 + LAT], a[:, 0:LAT]))
                        v.tensor_copy(u[:, 24 + LAT:24 + TOK], a[:, LAT:TOK]).then_inc(pool_ready, 1)
                        dve.wait_ge(pool_ready, 2 * f + 1)
                        link(v.tensor_tensor(wa[:, 1:PW], u[:, 0:PW - 1], u[:, 1:PW], ALU.add))
                        cur, other, step, lo = wa, wb, 1, 1
                        while 2 * step < win:
                            lo += step
                            link(v.tensor_tensor(other[:, lo:PW - lo + 1], cur[:, lo - step:PW - lo + 1 - step],
                                                 cur[:, lo + step:PW - lo + 1 + step], ALU.add))
                            cur, other, step = other, cur, 2 * step
                        for at0, n in ((8, LAT), (24 + LAT, CTX)):
                            e = bc(cur[:, at0:at0 + 1], (n - 8, 2), (1, 8))
                            link(v.tensor_tensor(e, e, corr[:, f, :].rearrange("p (a b) -> p a b", a=2), ALU.mult))
                        for at0, n, o in ((8, LAT, 0), (24 + LAT, CTX, LAT)):
                            ins = v.scalar_tensor_tensor(out=br[:, 3, f, o:o + n], in0=cur[:, at0:at0 + n],
                                                         scalar=1.0 / win, in1=u[:, at0:at0 + n],
                                                         op0=ALU.mult, op1=ALU.subtract)
                            if o == 0:
                                link(ins)
                        ins.then_inc(pool_ready, 1)

                    for f in range(BK):
                        dve.wait_ge(c_copied, f + 1)
                        dve.wait_ge(ch_full, f + 1)
                        v.tensor_tensor(br[:, 2, f, :], accf[pair(("ch", f))][:, 0:TOK], br[:, 2, f, :], ALU.mult)\
                            .then_inc(u_ready, 1)
                    dve.wait_ge(state_out, 64)
                    for f in range(BK):
                        dve.wait_ge(u_ready, f + 1)
                        if f:
                            dve.wait_ge(conv_ready, f)
                        u = br[:, 2, f, :]
                        tap = [smallp[:, 48 + 3 * f + j:49 + 3 * f + j] for j in range(3)]
                        link(v.tensor_scalar(conv_y, u, tap[1], smallp[:, 60 + f:61 + f], ALU.mult, ALU.add))
                        for lo, hi in ((0, LAT), (LAT, TOK)):
                            link(v.scalar_tensor_tensor(out=conv_y[:, lo + 1:hi], in0=u[:, lo:hi - 1], scalar=tap[0],
                                                        in1=conv_y[:, lo + 1:hi], op0=ALU.mult, op1=ALU.add))
                            link(v.scalar_tensor_tensor(out=conv_y[:, lo:hi - 1], in0=u[:, lo + 1:hi], scalar=tap[2],
                                                        in1=conv_y[:, lo:hi - 1], op0=ALU.mult, op1=ALU.add))
                        dve.wait_ge(cb_full, f + 1)
                        v.tensor_tensor(br[:, 2, f, :], accf[pair(("cb", f))][:, 0:TOK], conv_y, ALU.mult)\
                            .then_inc(conv_ready, 1)

                    def maxima(a):
                        kind, b, h = ATT[a]
                        n = key_tiles(a) * P
                        out = scores_at(a)
                        dve.wait_ge(scores_full, a + 1)
                        if kind == "na" and b < NB:
                            if a == 0:
                                dve.wait_ge(bias_in, 16 * GR * GR)
                            win = out[:, 0:NWIN].rearrange("p (r c) -> p r c", c=KC)
                            link(v.tensor_tensor(win, win, bias_of(h, b), ALU.add))
                        v.reduce_max(negmax[:, a:a + 1], out[:, 0:n], AX.X, negate=True).then_inc(rowmax_ready, 1)

                    def block_norm(j):
                        dve.wait_ge(pv_done, NH * (j + 1))
                        link(v.reciprocal(rsum[:, NH * j:NH * (j + 1)], sums[:, NH * j:NH * (j + 1)]))
                        if j >= 2:
                            dve.wait_ge(ot_full, j - 1)
                        v.tensor_tensor(otok[:, j % 2, :].rearrange("p (h d) -> p h d", d=HD),
                                        out_at(j).rearrange("p (h d) -> p h d", d=HD),
                                        bc(rsum[:, NH * j:NH * (j + 1)], (1, NH), (0, HD)), ALU.mult)\
                            .then_inc(o_copied, 1)

                    for a in range(-1, NATT):
                        for u in units_to_score(a):
                            maxima(u)
                        if NA_UNITS <= a + 1 < NATT:
                            n = key_tiles(a + 1) * P
                            dve.wait_ge(pt_full, a + 2)
                            dve.wait_ge(pv_done, a)
                            v.tensor_copy(pT[:, (a + 1) % 2, 0:n], turned_at(a + 1)[:, 0:n])\
                                .then_inc(pt_copied_dve, 1)
                        if a >= 0 and a % NH == NH - 1:
                            block_norm(a // NH)

                    dve.wait_ge(ot_full, NBLK)
                    added = 0
                    for g in range(4 * DK):
                        n, d = (g // 4) % 4, 4 * (g // 16) + g % 4
                        a = accf[pair(("B", g))][:, 0:TOK]
                        dve.wait_ge(sig_ready, g + 1)
                        dve.wait_ge(proj_full, g + 1)
                        if n == 0:
                            v.tensor_tensor(merged[:, d, :], a, sg[:, g % 2, :], ALU.mult).then_inc(prod_done, 1)
                            continue
                        if added:
                            dve.wait_ge(merged_add, added)
                        added += 1
                        v.tensor_tensor(prod[:, g % 2, :], a, sg[:, g % 2, :], ALU.mult).then_inc(prod_done, 1)
                        dve.wait_ge(prod_done, g + 1)
                        v.tensor_tensor(merged[:, d, :], merged[:, d, :], prod[:, g % 2, :], ALU.add)\
                            .then_inc(merged_add, 1)

                    def layer_norm(n, t, z, out, var_ready, std_ready, got):
                        for j in range(2):
                            link(v.bn_stats(stats[:, n, t, 6 * j:6 * j + 6], z[:, j * BANK:(j + 1) * BANK]))
                        v.bn_aggr(mv[:, n, t, :], stats[:, n, t, :]).then_inc(var_ready, 1)
                        dve.wait_ge(std_ready, t + 1)
                        link(v.reciprocal(rstd[:, n, t:t + 1], std[:, n, t:t + 1]))
                        link(v.tensor_scalar(z, z, mv[:, n, t, 0:1], rstd[:, n, t:t + 1], ALU.subtract, ALU.mult))
                        link(v.tensor_tensor(z, z, lng, ALU.mult))
                        v.tensor_tensor(out, z, lnb, ALU.add).then_inc(got, 1)

                    dve.wait_ge(ln1_in, 32)
                    dve.wait_ge(gate1_in, 32)
                    for t in range(NT + 3):
                        if t < NT:
                            g = 0 if t < NLT else 1
                            z = zt[:, t % 2, :]
                            dve.wait_ge(y_full, t + 1)
                            link(v.tensor_tensor(z, accf[pair(("y", t))], gate1[:, g, :], ALU.mult))
                            dve.wait_ge(xin_in[t % 2], 16 * (t // 2 + 1))
                            v.scalar_tensor_tensor(out=z, in0=xin[:, t % 2, :], scalar=ALPHA, in1=z,
                                                   op0=ALU.mult, op1=ALU.add).then_inc(z_free, 1)
                            dve.wait_ge(z_free, t + 1)
                            if t >= 2:
                                dve.wait_ge(x1T_full, t - 1)
                                dve.wait_ge(x1_out[t % 2], 32 * (t // 2))
                            layer_norm(0, t, z, x1[:, t % 2, :], var_ready, std1_ready, x1_ready)
                            dve.wait_ge(x1_ready, t + 1)
                            v.tensor_scalar(xa[:, t % 2, :], x1[:, t % 2, :], ALPHA, None, ALU.mult)\
                                .then_inc(xa_ready, 1)
                        if 2 <= t < NT + 2:
                            q = t - 2
                            a = accf[pair(("r", q))][:, 0:NE]
                            dve.wait_ge(r_full, q + 1)
                            v.reduce_max(lg[:, q, 1:2], a, AX.X, negate=True).then_inc(negl_ready, 1)
                            dve.wait_ge(el_ready, q + 1)
                            link(v.reciprocal(lg[:, q, 3:4], lg[:, q, 2:3]))
                            v.tensor_scalar(aff[:, q, :], lg[:, q, 4:4 + NE], lg[:, q, 3:4], None, ALU.mult)\
                                .then_inc(aff_ready, 1)
                        if t >= 3:
                            q = t - 3
                            dve.wait_ge(affT_full, q + 1)
                            v.tensor_copy(affT[:, q * P:(q + 1) * P], accf[pair(("affT", q))][0:NE, 0:P])\
                                .then_inc(affT_copied, 1)

                    dve.wait_ge(affT_copied, NT)
                    for g, cap, first in ((0, CAP_L, 0), (1, CAP_C, CAP_L)):
                        row = affT[:, group_cols(g)]
                        for r in range(cap // 8):
                            v8 = vals[:, first + 8 * r:first + 8 * r + 8]
                            link(v.max(v8, row))
                            link(v.max_index(idx_u[:, first + 8 * r:first + 8 * r + 8], v8, row))
                            link(v.match_replace(row, v8, row, -1.0))
                    link(v.tensor_copy(idx_f[:, 0:CAP_L], idx_u[:, 0:CAP_L]))
                    v.tensor_scalar(idx_f[:, CAP_L:CAP], idx_u[:, CAP_L:CAP], float(LAT), None, ALU.add)\
                        .then_inc(topk_ready, 1)
                    dve.wait_ge(sel_full, 1)
                    a = accf[pair(("sel",))]
                    link(v.tensor_copy(idx_t[:, NE:NE + 1], a[0:CAP, 0:1]))
                    link(v.tensor_copy(g_t[:, NE:NE + 1], a[0:CAP, NE:NE + 1]))
                    v.tensor_copy(idx_t[:, 0:NE], a[0:CAP, 0:NE]).then_inc(sel_ready, 1)
                    v.tensor_copy(g_t[:, 0:NE], a[0:CAP, NE:2 * NE]).then_inc(sel_ready, 1)
                    dve.wait_ge(sel_ready, 2)

                    dve.sem_inc(hidden_ready, 2)
                    dve.sem_inc(ye_ready, 1)

                    def choose(e, j, first):
                        v.tensor_copy(idx_cur[:, j:j + 1], idx_t[:, bass.ds(e, 1)]).then_inc(first, 1)
                        v.tensor_copy(g_cur[:, j:j + 1], g_t[:, bass.ds(e, 1)]).then_inc(sel_cur, 1)

                    def modulate(x, half, sem_, count):
                        def parts(a, base, step):
                            return bc(a[:, base:base + 1], (CAP, 4), (1, step))
                        for vec, op in ((32 + 4 * half, ALU.mult), (24 + 4 * half, ALU.add)):
                            for g, c0, n in ((0, 0, CAP_L), (1, CAP_L, CAP_C)):
                                dst = parts(x, 4 * CAP * half + c0, n)
                                src = parts(acc[3][:, 1, :], c0, n) if op == ALU.mult else dst
                                ins = v.tensor_tensor(dst, src, bc(mod[:, g, vec:vec + 1], (1, 4), (0, n)), op)
                                if op == ALU.add and g == 1:
                                    ins.then_inc(xsT_ready, 1)
                                else:
                                    ins.then_inc(sem_, 1)
                            if op == ALU.mult:
                                dve.wait_ge(sem_, count + 2)

                    choose(0, 0, dve_step)
                    chained[0] += 1
                    for half in range(2):
                        dve.wait_ge(xT_full, half + 1)
                        modulate(xsT[:, 0, :], half, dve_step, chained[0])
                        chained[0] += 3
                    dve.wait_ge(gate2_in, 32)
                    LOOP_INCS = 7
                    with dve.Fori(0, NE // EXPERTS_IN_BODY) as i:
                        for j in range(EXPERTS_IN_BODY):
                            e1 = i * EXPERTS_IN_BODY + (j + 1)
                            e2 = i * (2 * EXPERTS_IN_BODY) + 2 * (j + 1)
                            base = i * (LOOP_INCS * EXPERTS_IN_BODY) + LOOP_INCS * j

                            def hidden(half):
                                cols = slice(half * BANK, (half + 1) * BANK)
                                dve.wait_ge((up0_done, up1_done)[half], e1)
                                dve.wait_ge(silu_done, e2 + 1 + half)
                                v.tensor_tensor(hdn[:, cols], acc[1][0:CAP, half, :], act_s[:, cols], ALU.mult)\
                                    .then_inc(hidden_ready, 1)

                            hidden(0)
                            dve.wait_ge(ye_free, e1 + 1)
                            choose(e1, 1 - j, dve_loop)
                            hidden(1)
                            for half in range(2):
                                dve.wait_ge(xT_full, e2 + 1 + half)
                                modulate(xsT[:, 1 - j, :], half, dve_loop, base + 1 + 3 * half)
                            dve.wait_ge(down1_done, e1)
                            dve.wait_ge(ye_free, e1)
                            v.scalar_tensor_tensor(out=ye[:, j, :], in0=accf[2][0:CAP, :], scalar=g_cur[:, j:j + 1],
                                                   in1=gate2, op0=ALU.mult, op1=ALU.mult).then_inc(ye_ready, 1)

                    dve.wait_ge(ln2_in, 32)
                    for t in range(NT):
                        dve.wait_ge(zin_in[t % 2], 16 * (t // 2 + 1))
                        if t >= 2:
                            dve.wait_ge(x2_out[t % 2], 16 * (t // 2))
                        layer_norm(1, t, xin[:, t % 2, :], x1[:, t % 2, :], var2_ready, std2_ready, x2_ready)

                @block.gpsimd
                def _(pool):
                    pool.sem_inc(ye_free, 2)
                    for p in range(2):
                        pool.wait_ge(x1_out[p], 32 * ((NT + 1 - p) // 2))

                    def gather(j):
                        pool.indirect_dma_start(xs[:, j, :], None, x1_scr,
                                                bass.IndirectOffsetOnAxis(ap=idx_cur[:, j:j + 1], axis=0))\
                            .then_inc(gather_done, 16)

                    pool.wait_ge(sel_cur, 1)
                    gather(0)
                    with pool.Fori(0, NE // EXPERTS_IN_BODY) as i:
                        for j in range(EXPERTS_IN_BODY):
                            e1 = i * EXPERTS_IN_BODY + (j + 1)
                            pool.wait_ge(sel_cur, e1 + 1)
                            pool.sem_inc(pool_turn, 1)
                            gather(1 - j)
                            pool.wait_ge(ye_ready, e1 + 1)
                            pool.sem_inc(pool_turn, 1)
                            pool.indirect_dma_start(y_acc, bass.IndirectOffsetOnAxis(ap=idx_cur[:, j:j + 1], axis=0),
                                                    ye[:, j, :], None, compute_op=ALU.add).then_inc(scatter_done, 16)
                            pool.wait_ge(scatter_done, layer * (16 * NE) + i * (16 * EXPERTS_IN_BODY) + 16 * (j + 1))
                            pool.sem_inc(ye_free, 1)
                    pool.wait_ge(gather_done, layer * (16 * (NE + 1)) + 16 * (NE + 1))

            nc.multi_engine_barrier(nc.engines, sems_to_clear=range(cleared_from.num, cleared_to.num + 1))


def layout(inputs):
    a = {k: np.asarray(v) for k, v in inputs.items()}

    def blocks(w, n_k, width):
        lead = w.shape[:-2]
        w = w.reshape(*lead, n_k, P, w.shape[-1] // width, width)
        w = np.moveaxis(w, -2, -4)
        w = np.swapaxes(w, -3, -2)
        return np.ascontiguousarray(w).reshape(*lead, w.shape[-4], P, n_k * width)

    def columns(v):
        return np.swapaxes(v.reshape(*v.shape[:-1], -1, P), -1, -2)

    gate, up = (blocks(a[n], DK, BANK) for n in ("w_gate", "w_up"))
    down = a["w_down"].reshape(DEPTH, NE, 2, 4, P, D).swapaxes(3, 4).reshape(DEPTH, NE, 2, P, SLOT)
    experts = np.stack([gate[:, :, 0], up[:, :, 0], gate[:, :, 1], up[:, :, 1], down[:, :, 0], down[:, :, 1]],
                       axis=2)
    L = DEPTH
    w_in = a["w_in"]
    offs = np.cumsum([0, 512, 512, 512, 512, 128, 128, 512, 512, 512, 512])
    col = {n: w_in[:, :, offs[i]:offs[i + 1]] for i, n in
           enumerate(["q", "k", "v", "gq", "gk", "gv", "cb", "cc", "ch", "pool"])}
    gates = w_in[:, :, offs[-1]:].reshape(L, D, 4, 2, BANK).transpose(0, 3, 2, 1, 4)
    out = {
        "x_sample": a["x_sample"], "x_prompt": a["x_prompt"],
        "cna_k": a["cache_na_k"].reshape(L, PAST, BW), "cna_v": a["cache_na_v"].reshape(L, PAST, BW),
        "cg_k": a["cache_gqa_k"].reshape(L, PAST, P), "cg_v": a["cache_gqa_v"].reshape(L, PAST, P),
        "cond": np.stack([columns(a["c"][0]), columns(a["c_ctx"])], axis=-1),
        "small": np.concatenate([columns(a["b_ada"]),
                                 columns(a["conv_w"]).transpose(0, 2, 3, 1).reshape(L, P, 12),
                                 columns(a["conv_b"]), columns(a["pool_scale"])], axis=-1),
        "w_ada": blocks(a["w_ada"], DK, BANK),
        "w_main": np.stack([blocks(col[n], DK, BANK)[:, 0] for n in MAIN if n != "gkv"], axis=1),
        "w_gkv": blocks(np.concatenate([col["gk"], col["gv"]], axis=-1), DK, 2 * P)[:, 0],
        "w_gate_in": blocks(gates, DK, BANK).reshape(L, 8, P, SLOT),
        "w_branch": blocks(a["w_branch"], BK, BANK).transpose(0, 2, 1, 3, 4).reshape(L, 8, P, BK * BANK),
        "w_out": blocks(a["w_out"], DK, BANK),
        "bias_rows": np.pad(a["na_rpb"], ((0, 0), (0, 0), (0, 0), (QC, QC)))[:, :, ::-1, ::-1],
        "pool_w": a["pool_w"].transpose(0, 2, 1, 3),
        "w_router": a["w_router"].reshape(L, DK, P, NE).transpose(0, 2, 1, 3),
        "qk_gain": np.concatenate([a["qn_g"], a["kn_g"]], axis=-1),
        "ln_p": np.stack([a["ln1_g"], a["ln1_b"], a["ln2_g"], a["ln2_b"]], axis=1),
        "w_exp": experts,
    }
    out["bias_rows"] = np.pad(out["bias_rows"], ((0, 0), (0, 0), (0, 0), (0, 1)))
    return {k: np.ascontiguousarray(v) for k, v in out.items()}


def shape_constants():
    q = np.arange(P)
    i, keys = q // GR, np.arange(NWIN)
    mask = np.zeros((P, 3, NWIN), np.float32)
    for n, b in ((0, 0), (1, 1), (2, NB - 1)):
        start = np.clip(QC * b + i - WIN_C // 2, 0, GW - WIN_C)[:, None]
        ck = KEY_COL[b] + keys[None, :] % KC
        mask[:, n] = np.where((ck >= start) & (ck < start + WIN_C), 0.0, MASKED)
    n_freq = HD // 4
    inv = THETA ** (-np.arange(n_freq, dtype=np.float32) / n_freq)
    t = np.arange(LAT)
    rope = np.zeros((LAT, 2, 2, 2, n_freq), np.float32)
    for n, pos in enumerate((t // GW, t % GW)):
        ang = pos.astype(np.float32)[:, None] * inv.astype(np.float32)
        rope[:, 0, n] = np.cos(ang)[:, None, :]
        rope[:, 1, n] = np.sin(ang)[:, None, :]
    rope = rope.reshape(NLT, P, 2, HD).transpose(1, 0, 2, 3)
    corr = np.ones((4, 2, 8), np.float32)
    for g, win in enumerate(POOL_WINDOWS):
        n = 64
        pos = np.arange(n)
        count = np.clip(pos + win // 2, 0, n) - np.clip(pos - win // 2, 0, n)
        corr[g, 0], corr[g, 1] = win / count[:8], win / count[-8:]
    return {"ident_in": np.eye(P, dtype=np.float32), "mask_in": mask.reshape(P, 3 * NWIN),
            "rope_in": np.ascontiguousarray(rope),
            "corr_in": np.ascontiguousarray(np.broadcast_to(corr.reshape(1, 4, 16), (P, 4, 16)))}


OUTS = {"y_prompt": (1, CTX, D), "y_sample": (1, LAT, D), "st_na_k": (DEPTH, CTX, BW),
        "st_na_v": (DEPTH, CTX, BW), "st_g_k": (DEPTH, CTX, P), "st_g_v": (DEPTH, CTX, P)}


def kernel(**inputs):
    import concourse.bacc as bacc
    from concourse.bass_utils import run_bass_kernel_spmd

    arrays = {**layout(inputs), **shape_constants()}
    nc = bacc.Bacc("TRN2", target_bir_lowering=False, num_devices=1)
    args = {n: nc.dram_tensor(n, a.shape, F32, kind="ExternalInput").ap() for n, a in arrays.items()}
    for n, shape in OUTS.items():
        args[n] = nc.dram_tensor(n, shape, F32, kind="ExternalOutput").ap()
    build_program(nc, **args)
    r = run_bass_kernel_spmd(nc, [arrays], core_ids=[0]).results[0]
    return (r["y_prompt"], r["y_sample"],
            r["st_na_k"].reshape(1, DEPTH, CTX, NH, HD), r["st_na_v"].reshape(1, DEPTH, CTX, NH, HD),
            r["st_g_k"].reshape(1, DEPTH, CTX, KVH, HD), r["st_g_v"].reshape(1, DEPTH, CTX, KVH, HD))
```

```python
from contextlib import ExitStack

import numpy as np

import concourse.bass as bass
from concourse import mybir

F32 = mybir.dt.float32
F32R = mybir.dt.float32r
BF16 = mybir.dt.bfloat16
U32 = mybir.dt.uint32
ALU = mybir.AluOpType
ACT = mybir.ActivationFunctionType
AX = mybir.AxisListType

P = 128
BANK = 512
D = 1024
DK = D // P
DEPTH = 2
LAT, CTX, PAST = 512, 128, 128
TOK = LAT + CTX
NT = TOK // P
NLT = LAT // P
HT = TOK // 2
GW = 64
GR = LAT // GW
HD = 64
NH = 8
KVH = 2
BW = 512
BK = BW // P
WIN_R, WIN_C = 8, 16
NE = 16
FF = 1024
FK = FF // P
CAP_L = 2 * LAT // NE
CAP_C = 2 * CTX // NE
CAP = CAP_L + CAP_C
POOL_WINDOWS = (2, 4, 8, 16)
THETA = 10000.0
EPS = 1e-6
ALPHA = float((2 * DEPTH) ** 0.25)
QSCALE = HD ** -0.5

QC = P // GR
NB = GW // QC
KC = 32
KEY_COL = [min(max(QC * b - WIN_C // 2, 0), GW - KC) for b in range(NB)]
BIAS_W = KC + QC
BIAS_AT = [KEY_COL[b] - QC * b + QC for b in range(NB)]
NWIN = GR * KC
NA_KEYS = NWIN + PAST
MASKED = -(2.0 ** 99)
FILLERS = 5

RING = 3
SLOT = DK * BANK
ADA_SLOTS = 12
MAIN = ["q", "k", "v", "gq", "gkv", "pool", "cc", "ch", "cb"]
SLOTS = [("ada", i) for i in range(ADA_SLOTS)] + [(m, 0) for m in MAIN]
for _n in range(4):
    for _dc in range(2):
        SLOTS += [("gate", 4 * _dc + _n), ("wb", 4 * _dc + _n)]
SLOTS += [("wo", 0), ("wo", 1)]
NSEQ = (len(SLOTS) + RING - 1) // RING * RING
PER_EXPERT = 6
EXPERTS_IN_BODY = 2
BODY_SLOTS = PER_EXPERT * EXPERTS_IN_BODY
assert BODY_SLOTS % RING == 0


def slot_of(key):
    s = SLOTS.index(key)
    return s % RING, s // RING


def uses_before_experts(r):
    return len([n for n in range(len(SLOTS)) if n % RING == r])


PROJ = [(m, f) for m in MAIN for f in range(2 if m == "gkv" else BK)]
NPROJ = len(PROJ)
PRODUCTS = list(PROJ)
for _g in range(4 * DK):
    PRODUCTS += [("L", _g), ("B", _g)]
PRODUCT_NO = {key: n for n, key in enumerate(PRODUCTS)}
STEP_PRODUCTS = [[18], [19, 20], [21], [22, 23], [24], [25]]
assert PROJ[18] == ("pool", 0) and PROJ[25] == ("cc", BK - 1)


def merge_unit(g):
    return g // 8, g // 4 % 2, g % 8


def slot_key(key):
    kind, g = key
    if kind in ("L", "B"):
        n, dc, _ = merge_unit(g)
        return ("gate" if kind == "L" else "wb"), 4 * dc + n
    return kind, 0


ATT = [(kind, b, h) for kind in ("na", "gqa") for b in range(NB + 1) for h in range(NH)]
NATT = len(ATT)
NBLK = NATT // NH
NA_UNITS = NATT // 2


def units_to_score(step):
    return [u for u in range(NATT) if max(u - (3 if u < NA_UNITS else 2), -1) == step]


def build_program(nc, x_sample, x_prompt, cna_k, cna_v, cg_k, cg_v, cond, small, w_ada, w_main, w_gkv,
                  w_gate_in, w_branch, w_out, bias_rows, pool_w, w_router, qk_gain, ln_p, w_exp,
                  ident_in, mask_in, rope_in, corr_in,
                  y_prompt, y_sample, st_na_k, st_na_v, st_g_k, st_g_v):
    with ExitStack() as ctx:
        def sb(name, shape, dt=F32):
            return ctx.enter_context(nc.sbuf_tensor(name, shape, dt))

        def sem(name):
            return ctx.enter_context(nc.semaphore(name))

        def sb_twice(name, shape):
            with nc.sbuf_tensor(name, shape, F32) as plain:
                pass
            return plain, sb(name + "_r", shape, F32R)

        ring, ring_r = sb_twice("ring", [P, RING, SLOT])
        hT, hT_r = sb_twice("hT", [P, DK, TOK])
        h_high = sb("h_high", [P, DK, TOK], F32R)
        br, br_r = sb_twice("br", [P, 4, BK, TOK])
        shared, shared_r = sb_twice("shared", [P, 13568])
        work, work_r = sb_twice("work", [P, 4224])
        ident = sb("ident", [P, P])
        ident_b = sb("ident_b", [P, P], BF16)
        mask_f = work[:, 0:3 * NWIN]
        mask_b = sb("mask_b", [P, 3, NWIN], BF16)
        rope = sb("rope", [P, NLT, 2, HD])
        corr = sb("corr", [P, 4, 16])
        gate_cols = sb("gate_cols", [P, 32])[:, :]
        eps = sb("eps", [P, 1])
        cvec = sb("cvec", [P, DK, 2])
        smallp = sb("smallp", [P, 68])
        mod = sb("mod", [P, 2, 48])
        router = sb("router", [P, DK, NE])
        negmax = sb("negmax", [P, NATT])
        sums = sb("sums", [P, NATT])
        qk_ss = sb("qk_ss", [P, NT, 10])
        qk_std = sb("qk_std", [P, NT, 10])
        qk_rstd = sb("qk_rstd", [P, NT, 10])
        grow = sb("grow", [32, P])
        stats = sb("stats", [P, 2, NT, 12])
        mv = sb("mv", [P, 2, NT, 2])
        std = sb("std", [P, 2, NT])
        rstd = sb("rstd", [P, 2, NT])
        lg = sb("lg", [P, NT, 4 + NE])
        aff = sb("aff", [P, NT, NE])
        rsum = aff[:, :, :].rearrange("p a b -> p (a b)")[:, 0:NATT]
        vals = sb("vals", [NE, CAP])
        idx_u = sb("idx_u", [NE, CAP], U32)
        idx_f = sb("idx_f", [NE, CAP])
        idx_t = sb("idx_t", [CAP, NE + 1], U32)
        g_t = sb("g_t", [CAP, NE + 1])
        idx_cur = sb("idx_cur", [CAP, 2], U32)
        g_cur = sb("g_cur", [CAP, 2])

        class Carve:
            def __init__(self, arena, size):
                self.arena, self.size, self.at = arena, size, 0

            def take(self, *dims):
                n = int(np.prod(dims))
                a = self.arena[:, self.at:self.at + n]
                self.at += n
                assert self.at <= self.size, (self.at, self.size)
                if len(dims) == 2:
                    a = a.rearrange("p (a b) -> p a b", a=dims[0])
                if len(dims) == 3:
                    a = a.rearrange("p (a b c) -> p a b c", a=dims[0], b=dims[1])
                return a

        c = Carve(shared, 13568)
        na_kT = c.take(BK, TOK + PAST)
        bias_at = c.at
        bias = c.take(NH, GR, BIAS_W)
        vwin_at = c.at
        vwin = c.take(2 * NB, BW)
        vcache = c.take(BW)
        vctx = c.take(BW)
        gkT = c.take(KVH, TOK + PAST)
        gv = c.take(NT + 1, P)
        na_cached, g_cached = vwin[:, 0, :], vwin[:, 1, 0:P]
        gain = vwin[:, 1, P:2 * P].rearrange("p (a b) -> p a b", a=2)
        poolw = vwin[:, 2, :].rearrange("p (a b) -> p a b", a=4)
        high_at = vwin_at + 4 * BW
        gq_raw = shared[:, bias_at:bias_at + BK * TOK].rearrange("p (a b) -> p a b", a=BK)
        PW = 8 + LAT + 8 + 8 + CTX + 8
        pu = [work[:, 1536 + i * PW:1536 + (i + 1) * PW] for i in range(3)]
        c = Carve(shared, 13568)
        merged = c.take(DK, TOK)
        sg = c.take(2, TOK)
        prod = c.take(2, TOK)
        br_high_at = c.at
        c.take(BK, TOK)
        br_high = shared_r[:, br_high_at:c.at].rearrange("p (a b) -> p a b", a=BK)
        L_high_at = c.at
        assert L_high_at == vwin_at + 2 * NB * BW
        c.take(DK * P)
        gate1 = c.take(2, D)
        affT = sg.rearrange("p a b -> p (a b)")[0:NE, 0:TOK]
        lng = prod.rearrange("p a b -> p (a b)")[:, 0:D]
        xsT = shared[:, br_high_at:br_high_at + 2 * DK * CAP].rearrange("p (a b) -> p a b", a=2)
        m = Carve(shared, DK * TOK)
        act_s = m.take(FF)[0:CAP, :]
        hdn = m.take(FF)[0:CAP, :]
        hdnT = m.take(FK * CAP)
        gate2 = m.take(D)[0:CAP, :]

        c = Carve(work, 4224)
        gtok = c.take(2, 768)
        t1 = c.take(640)
        t2 = c.take(640)
        kdup = c.take(2, 2 * P)
        c = Carve(work, 4224)
        probs = c.take(3, 640)
        pT = c.take(2, 640)
        otok = c.take(2, BW)
        conv_y = work[:, 3200:3200 + TOK]
        L_high = [shared_r[:, L_high_at:L_high_at + DK * P], work_r[:, 640:640 + DK * P]]
        B_high = [work_r[:, 1664 + i * BK * P:1664 + (i + 1) * BK * P] for i in range(2)]
        lnb = work[:, 2688:2688 + D]
        adarow = work[0:2, 0:2 * BANK].rearrange("p (a b) -> p a b", a=2)
        k_state = work[:, 0:BW]

        qT = br[:, 0]
        gqT = br[:, 1]
        vT = br[:, 1]
        kv_slot = SLOTS.index(("gkv", 0)) % RING
        kv_raw = ring[:, kv_slot, SLOT // 2:SLOT // 2 + 2 * TOK].rearrange("p (a b) -> p a b", a=2)
        vstage = br[:, 3].rearrange("p a b -> p (a b)")[:, 0:NLT * BW].rearrange("p (t n) -> p t n", t=NLT)
        brf = br[:, :, :, :].rearrange("p a b c -> p (a b c)")
        xstage = brf[:, 0:NT * D].rearrange("p (a b) -> p a b", a=NT)
        zt = brf[:, 0:2048].rearrange("p (a b) -> p a b", a=2)
        x1 = brf[:, 2048:4096].rearrange("p (a b) -> p a b", a=2)
        xa = brf[:, 4096:6144].rearrange("p (a b) -> p a b", a=2)
        xin = brf[:, 6144:8192].rearrange("p (a b) -> p a b", a=2)
        xmT = brf[:, 8192:10240].rearrange("p (a b c) -> p a b c", a=2, b=DK)
        hf = hT[:, :, :].rearrange("p a b -> p (a b)")
        xs = hf[0:CAP, 0:2048].rearrange("p (a b) -> p a b", a=2)
        ye = hf[0:CAP, 2048:4096].rearrange("p (a b) -> p a b", a=2)

        acc = [ctx.enter_context(nc.psum_tensor(f"acc{i}", [P, 2, BANK], F32)) for i in range(4)]
        accf = [a[:, :, :].rearrange("p a b -> p (a b)") for a in acc]
        o_bank, ot_bank = acc[3][:, 0, :], acc[3][:, 1, :]

        v_scr = nc.dram_tensor("v_scr", [LAT, BW], F32, kind="Internal").ap()
        gate_scr = nc.dram_tensor("gate_scr", [32, P], F32, kind="Internal").ap()
        x1_scr = nc.dram_tensor("x1_scr", [TOK, D], F32, kind="Internal").ap()
        y_acc = nc.dram_tensor("y_acc", [TOK, D], F32, kind="Internal").ap()

        def out_rows(t):
            return y_sample[0, t * P:(t + 1) * P, :] if t < NLT else y_prompt[0, :, :]

        def bc(ap, *dims):
            return bass.AP(ap.tensor, ap.offset, [list(ap.ap[0])] + [list(d) for d in dims])

        consts_in = sem("consts_in")
        x_copied = sem("x_copied")
        const_ready = sem("const_ready")
        gather_done = sem("gather_done")
        scatter_done = sem("scatter_done")
        cleared_from = sem("cleared_from")
        slot_full = [sem(f"slot_full{r}") for r in range(RING)]
        x_in = sem("x_in")
        xin_in = [sem(f"xin_in{i}") for i in range(2)]
        x1_out = [sem(f"x1_out{i}") for i in range(2)]
        zin_in = [sem(f"zin_in{i}") for i in range(2)]
        x2_out = [sem(f"x2_out{i}") for i in range(2)]
        cond_in = sem("cond_in")
        small_in = sem("small_in")
        param_in = sem("param_in")
        ada_done = sem("ada_done")
        ada_copied = sem("ada_copied")
        mod_full = sem("mod_full")
        silu_ready = sem("silu_ready")
        xt_full = sem("xt_full")
        xt_copied = sem("xt_copied")
        mod_ready = sem("mod_ready")
        h_whole = sem("h_whole")
        h_high_ready = sem("h_high_ready")
        h_ready = sem("h_ready")
        w_high_ready = sem("w_high_ready")
        w_ready = sem("w_ready")
        product_done = sem("product_done")
        vraw_copied = sem("vraw_copied")
        graw_copied = sem("graw_copied")
        pool_copied = sem("pool_copied")
        br_high_ready = sem("br_high_ready")
        br_ready = sem("br_ready")
        gateT_full = sem("gateT_full")
        gateT_copied = sem("gateT_copied")
        gate_out = sem("gate_out")
        gate1_in = sem("gate1_in")
        ln1_in = sem("ln1_in")
        q_copied = sem("q_copied")
        k_copied = sem("k_copied")
        kcache_in = sem("kcache_in")
        kc_full = sem("kc_full")
        kc_copied = sem("kc_copied")
        ks_full = sem("ks_full")
        ks_copied = sem("ks_copied")
        v_full = sem("v_full")
        v_copied = sem("v_copied")
        vscr_out = sem("vscr_out")
        vwin_in = [sem(f"vwin_in{i}") for i in range(2)]
        cachev_in = sem("cachev_in")
        state_out = sem("state_out")
        g_full = sem("g_full")
        g_copied = sem("g_copied")
        ss_ready = sem("ss_ready")
        std_ready = sem("std_ready")
        gtok_ready = sem("gtok_ready")
        gt_full = sem("gt_full")
        gt_copied = sem("gt_copied")
        gc_dup = sem("gc_dup")
        gc_full = sem("gc_full")
        gc_copied = sem("gc_copied")
        pool_ready = sem("pool_ready")
        mix_full = sem("mix_full")
        mix_copied = sem("mix_copied")
        c_copied = sem("c_copied")
        u_ready = sem("u_ready")
        conv_ready = sem("conv_ready")
        bias_in = sem("bias_in")
        scores_full = sem("scores_full")
        rowmax_ready = sem("rowmax_ready")
        probs_ready = sem("probs_ready")
        pt_full = sem("pt_full")
        pt_copied_act = sem("pt_copied_act")
        pt_copied_dve = sem("pt_copied_dve")
        pv_done = sem("pv_done")
        o_copied = sem("o_copied")
        ot_full = sem("ot_full")
        ot_copied = sem("ot_copied")
        sig_ready = sem("sig_ready")
        merged_add = sem("merged_add")
        prod_done = sem("prod_done")
        y_full = sem("y_full")
        z_free = sem("z_free")
        var_ready = sem("var_ready")
        std1_ready = sem("std1_ready")
        x1_ready = sem("x1_ready")
        xa_ready = sem("xa_ready")
        x1T_full = sem("x1T_full")
        xmT_ready = sem("xmT_ready")
        r_full = sem("r_full")
        negl_ready = sem("negl_ready")
        el_ready = sem("el_ready")
        aff_ready = sem("aff_ready")
        affT_full = sem("affT_full")
        affT_copied = sem("affT_copied")
        topk_ready = sem("topk_ready")
        sel_full = sem("sel_full")
        sel_ready = sem("sel_ready")
        sel_cur = sem("sel_cur")
        xT_full = sem("xT_full")
        xsT_ready = sem("xsT_ready")
        gate0_done = sem("gate0_done")
        up0_done = sem("up0_done")
        gate1_done = sem("gate1_done")
        up1_done = sem("up1_done")
        down0_done = sem("down0_done")
        down1_done = sem("down1_done")
        silu_done = sem("silu_done")
        hidden_ready = sem("hidden_ready")
        hT_full = sem("hT_full")
        hT_copied = sem("hT_copied")
        gate2_in = sem("gate2_in")
        ye_ready = sem("ye_ready")
        ye_free = sem("ye_free")
        ln2_in = sem("ln2_in")
        var2_ready = sem("var2_ready")
        std2_ready = sem("std2_ready")
        x2_ready = sem("x2_ready")
        dve_step = sem("dve_step")
        dve_loop = sem("dve_loop")
        pool_turn = sem("pool_turn")
        cleared_to = sem("cleared_to")


        plan, freed_by = [], {}

        def unit(key, semaphore, count):
            freed_by[key] = (semaphore, count)
            plan.append(key)

        for i in range(ADA_SLOTS):
            unit(("ada", i), ada_copied, i + 1)
            if i == 0:
                for t in range(NT):
                    unit(("xt", t), xt_copied, t + 1)
        for f in range(BK):
            unit(("q", f), q_copied, 3 * f + 3)
        unit(("gateT",), gateT_copied, 1)
        for f in range(BK):
            unit(("k", f), k_copied, f + 1)
        for f in range(BK):
            unit(("v", f), vraw_copied, f + 1)
            if f == 0:
                unit(("kc",), kc_copied, 1)
                unit(("ks",), ks_copied, 1)
        for f in range(BK):
            unit(("gq", f), graw_copied, f + 1)
            if f == 0:
                for t in range(NT):
                    unit(("vt", t), v_copied, t + 1)
        for f in range(2):
            unit(("gkv", f), graw_copied, BK + f + 1)
        for t in range(NT + 1):
            if t < NT:
                unit(("g", t), g_copied, 2 * t + 2)
            for n in STEP_PRODUCTS[t]:
                kind, f = PROJ[n]
                unit(PROJ[n], pool_copied if kind == "pool" else c_copied, f + 1)
            if t >= 1:
                unit(("gt", t - 1), gt_copied, 2 * (t - 1) + 2)
        unit(("gc",), gc_copied, 1)
        for f in range(BK):
            unit(("ch", f), u_ready, f + 1)
            unit(("mix", f), mix_copied, f + 1)
        for f in range(BK):
            unit(("cb", f), conv_ready, f + 1)
        AFTER_ATT = len(plan)
        for g in range(4 * DK):
            unit(("L", g), sig_ready, g + 1)
            unit(("B", g), prod_done, g + 1)
        for t in range(NT + 3):
            if t < NT:
                unit(("y", t), z_free, t + 1)
            if 2 <= t < NT + 2:
                unit(("r", t - 2), el_ready, t - 1)
            if t >= 3:
                unit(("affT", t - 3), affT_copied, t - 2)
            if 1 <= t < NT + 1:
                unit(("x1T", t - 1), xmT_ready, DK * t)
        unit(("sel",), sel_ready, 2)
        at = {key: n for n, key in enumerate(plan)}

        place = [n % 3 if n < AFTER_ATT else (n - AFTER_ATT) % 3 for n in range(len(plan))]
        place[at["cb", 2]], place[at["cb", 3]] = 2, 3

        def last_user(n):
            first = 0 if n < AFTER_ATT else AFTER_ATT
            users = [i for i in range(first, n) if place[i] == place[n]]
            return users[-1] if users else None

        def pair(key):
            return place[at[key]]

        def scores_at(a):
            return accf[(a % 4) // 2][:, (a % 2) * BANK:] if a < NA_UNITS else accf[a % 2]

        def turned_at(a):
            return acc[2][:, a % 2, :] if a < NA_UNITS else accf[2]

        def out_at(block):
            return acc[3][:, block % 2, :]

        def turned_free(a):
            return (pt_copied_act, a + 1) if a < NA_UNITS else (pt_copied_dve, a - NA_UNITS + 1)

        def halves(key):
            return acc[pair(key)][:, :, 0:HT]

        def by_half(a):
            return a.rearrange("p (a b) -> p a b", a=2)

        def released(key):
            kind, n = key
            if kind == "ada":
                return ada_done, n + 1
            if kind == "wo":
                return y_full, NT
            if kind == "gkv":
                return g_full, NT
            return product_done, max(PRODUCT_NO[p] for p in PRODUCTS if slot_key(p) == key) + 1

        def done(n):
            return product_done, n + 1

        def weight_tile(n):
            kind, f = PRODUCTS[n]
            r, _ = slot_of(slot_key(PRODUCTS[n]))
            n_k = BK if kind == "B" else DK
            width = 2 * P if kind == "gkv" else BANK
            col = (f % 4) * P
            if n < NPROJ:
                high = shared_r[:, high_at + (n % 2) * DK * P:high_at + (n % 2 + 1) * DK * P]
            else:
                high = (B_high if kind == "B" else L_high)[f % 2]
            whole, low = (a[:, r, 0:n_k * width].rearrange("p (k n) -> p k n", k=n_k)[:, :, col:col + P]
                          for a in (ring, ring_r))
            return whole, low, high.rearrange("p (k n) -> p k n", k=n_k)

        part_done = [gate0_done, up0_done, gate1_done, up1_done, down0_done, down1_done]

        def key_tiles(a):
            kind, b, _ = ATT[a]
            return 1 if b == NB else (NA_KEYS if kind == "na" else LAT + PAST) // P

        def value_tile(a, j):
            kind, b, h = ATT[a]
            if kind == "na":
                cols = slice(h * HD, (h + 1) * HD)
                return vctx[:, cols] if b == NB else vwin[:, 2 * b + j, cols] if j < 2 else vcache[:, cols]
            g = h // (NH // KVH)
            tile = NT - 1 if b == NB else j if j < NLT else NT
            return gv[:, tile, g * HD:(g + 1) * HD]

        def bias_of(h, b):
            last = bias[:, h, GR - 1, BIAS_W - 1 - BIAS_AT[b]:BIAS_W - BIAS_AT[b]]
            return bc(last, (-BIAS_W, GR), (-1, KC))

        def group_cols(g):
            return slice(0, LAT) if g == 0 else slice(LAT, TOK)

        with nc.Block() as block:
            @block.sync
            def _(sp):
                sp.dma_start(y_sample[0], x_sample[0]).then_inc(x_copied, 16)
                sp.dma_start(y_prompt[0], x_prompt[0]).then_inc(x_copied, 16)
                sp.dma_start(ident[:], ident_in).then_inc(consts_in, 16)
                sp.dma_start(mask_f, mask_in).then_inc(consts_in, 16)
                sp.dma_start(rope[:], rope_in).then_inc(consts_in, 16)
                sp.dma_start(corr[:], corr_in).then_inc(consts_in, 16)
                sp.wait_ge(x_copied, 32)

            @block.vector
            def _(dve):
                nc.vector.memset(eps[:], EPS).then_inc(const_ready, 1)
                dve.wait_ge(consts_in, 64)
                nc.vector.tensor_copy(ident_b[:], ident[:]).then_inc(const_ready, 1)
                nc.vector.tensor_copy(mask_b[:].rearrange("p a b -> p (a b)"), mask_f).then_inc(const_ready, 1)
                dve.wait_ge(const_ready, 3)

        with nc.Fori(0, DEPTH) as layer:
            with nc.Block() as block:

                @block.sync
                def _(sp):
                    src = {"ada": lambda i: w_ada[layer, i], "gkv": lambda i: w_gkv[layer],
                           "gate": lambda i: w_gate_in[layer, i], "wb": lambda i: w_branch[layer, i],
                           "wo": lambda i: w_out[layer, i]}
                    for i, mname in enumerate(n for n in MAIN if n != "gkv"):
                        src[mname] = lambda _, i=i: w_main[layer, i]
                    sp.dma_start(cvec[:], cond).then_inc(cond_in, 16)
                    sp.dma_start(smallp[:], small[layer]).then_inc(small_in, 16)
                    for n, key in enumerate(SLOTS):
                        r, use = slot_of(key)
                        a = src[key[0]](key[1])
                        if use >= 1:
                            sp.wait_ge(*released(SLOTS[n - RING]))
                        sp.dma_start(ring[:, r, 0:a.shape[1]], a).then_inc(slot_full[r], 16)
                        if key == ("cb", 0):
                            sp.wait_ge(g_full, NT)
                            for row in range(GR):
                                for rr in range(GR):
                                    a = bias_rows[layer]
                                    sp.dma_start(bias[row:P:GR, :, rr, :],
                                                 bass.AP(a.tensor, a.offset + (row + rr) * 64,
                                                         [[1, QC], [15 * 64, NH], [1, BIAS_W]])).then_inc(bias_in, 16)
                        if n == 0:
                            sp.dma_start(xstage[:, 0:NLT, :], y_sample[0].rearrange("(t p) n -> p t n", p=P))\
                                .then_inc(x_in, 16)
                            sp.dma_start(xstage[:, NLT, :], y_prompt[0]).then_inc(x_in, 16)
                        if n == 2:
                            sp.dma_start(na_cached, cna_k[layer]).then_inc(kcache_in, 16)
                            sp.dma_start(vcache, cna_v[layer]).then_inc(cachev_in, 16)
                            sp.dma_start(g_cached, cg_k[layer]).then_inc(kcache_in, 16)
                            sp.dma_start(gv[:, NT, :], cg_v[layer]).then_inc(cachev_in, 16)
                            sp.dma_start(gain.rearrange("p a b -> p (a b)"),
                                         bass.AP(qk_gain.tensor, qk_gain[layer].offset,
                                                 [[0, P], [1, 2 * HD]])).then_inc(param_in, 16)
                            sp.dma_start(poolw, pool_w[layer]).then_inc(param_in, 16)
                            sp.dma_start(router[:], w_router[layer]).then_inc(param_in, 16)
                    for n in range(RING):
                        if NSEQ + n - RING < len(SLOTS):
                            sp.wait_ge(*released(SLOTS[NSEQ + n - RING]))
                        elif NSEQ + n - 2 * RING >= 0:
                            sp.wait_ge(*released(SLOTS[NSEQ + n - 2 * RING]))
                        sp.dma_start(ring[:, n, :], w_exp[layer, 0, n]).then_inc(slot_full[n], 16)

                    def refill(i, n):
                        e, ahead = n // PER_EXPERT, n + RING
                        sp.wait_ge(part_done[n % PER_EXPERT], i * EXPERTS_IN_BODY + (e + 1))
                        sp.dma_start(ring[:, n % RING, :],
                                     w_exp[layer, i * EXPERTS_IN_BODY + ahead // PER_EXPERT, ahead % PER_EXPERT])\
                            .then_inc(slot_full[n % RING], 16)

                    last = NE // EXPERTS_IN_BODY - 1
                    with sp.Fori(0, last) as i:
                        for n in range(BODY_SLOTS):
                            refill(i, n)
                    for n in range(BODY_SLOTS - RING):
                        refill(last, n)

                @block.tensor
                def _(pe):
                    def acquire(key):
                        n = last_user(at[key])
                        if n is not None:
                            pe.wait_ge(*freed_by[plan[n]])
                        return accf[pair(key)]

                    def arrived(key):
                        r, use = slot_of(key)
                        pe.wait_ge(slot_full[r], 16 * (use + 1))
                        return ring[:, r, :]

                    def h_cols(k, half):
                        cols = slice(half * HT, (half + 1) * HT)
                        return h_high[:, k, cols], hT_r[:, k, cols]

                    def product(key, rhs, groups=((0, HT), (BANK, HT))):
                        n = PRODUCT_NO[key]
                        pe.wait_ge(w_ready, n + 1)
                        out = acquire(key)
                        _, low, high = weight_tile(n)
                        n_k = low.shape[1]
                        for i, (at0, count) in enumerate(groups):
                            o = out[:, at0:at0 + count]
                            for k in range(n_k):
                                x_high, x_low = rhs(k, i)
                                nc.tensor.matmul(o, high[:, k, :], x_high, start=(k == 0), stop=False)
                                nc.tensor.matmul(o, high[:, k, :], x_low, start=False, stop=False)
                                mm = nc.tensor.matmul(o, low[:, k, :], x_high, start=False, stop=(k == n_k - 1))
                        mm.then_inc(product_done, 1)

                    def turn_input():
                        pe.wait_ge(x_in, 32)
                        for t in range(NT):
                            out = acquire(("xt", t))
                            for k in range(DK):
                                mm = nc.tensor.transpose(out[:, k * P:(k + 1) * P], xstage[:, t, k * P:(k + 1) * P],
                                                         ident[:])
                            mm.then_inc(xt_full, 1)

                    pe.wait_ge(silu_ready, 1)
                    def turn_ada(i):
                        pe.wait_ge(ada_copied, i + 1)
                        for j in range(4):
                            c0 = 2 * (4 * i + j)
                            bank = o_bank if i < 4 else ot_bank
                            mm = nc.tensor.transpose(bank[:, c0:c0 + 2], adarow[:, i % 2, j * P:(j + 1) * P],
                                                     ident[0:2, 0:2])
                        mm.then_inc(mod_full, 1)

                    for i in range(ADA_SLOTS):
                        w = arrived(("ada", i))
                        out = acquire(("ada", i))
                        for k in range(DK):
                            mm = nc.tensor.matmul(out[0:2, 0:BANK], cvec[:, k, :], w[:, k * BANK:(k + 1) * BANK],
                                                  start=(k == 0), stop=(k == DK - 1))
                        mm.then_inc(ada_done, 1)
                        if i == 0:
                            turn_input()
                        else:
                            turn_ada(i - 1)
                    turn_ada(ADA_SLOTS - 1)
                    pe.wait_ge(h_ready, DK)
                    for f in range(BK):
                        product(("q", f), h_cols)
                    pe.wait_ge(mod_ready, 2)
                    out = acquire(("gateT",))
                    nc.tensor.transpose(out[0:32, 0:P], gate_cols, ident[:]).then_inc(gateT_full, 1)
                    for f in range(BK):
                        product(("k", f), h_cols)
                    for f in range(BK):
                        product(("v", f), h_cols)
                        if f == 0:
                            pe.wait_ge(kcache_in, 32)
                            out = acquire(("kc",))
                            for i in range(BK):
                                mm = nc.tensor.transpose(out[:, i * P:(i + 1) * P], na_cached[:, i * P:(i + 1) * P],
                                                         ident[:])
                            mm.then_inc(kc_full, 1)
                            pe.wait_ge(k_copied, BK)
                            out = acquire(("ks",))
                            for i in range(BK):
                                mm = nc.tensor.transpose(out[:, i * P:(i + 1) * P], na_kT[:, i, LAT:TOK], ident[:])
                            mm.then_inc(ks_full, 1)
                    for f in range(BK):
                        product(("gq", f), h_cols)
                        if f == 0:
                            pe.wait_ge(vraw_copied, BK)
                            for t in range(NT):
                                out = acquire(("vt", t))
                                for i in range(BK):
                                    mm = nc.tensor.transpose(out[:, i * P:(i + 1) * P], vT[:, i, t * P:(t + 1) * P],
                                                             ident[:])
                                mm.then_inc(v_full, 1)
                    for f in range(2):
                        product(("gkv", f), h_cols)

                    pe.wait_ge(graw_copied, BK + 2)
                    for t in range(NT + 1):
                        if t < NT:
                            out = acquire(("g", t))
                            for f in range(BK + 2):
                                src = gq_raw[:, f, :] if f < BK else kv_raw[:, f - BK, :]
                                mm = nc.tensor.transpose(out[:, f * P:(f + 1) * P], src[:, t * P:(t + 1) * P], ident[:])
                            mm.then_inc(g_full, 1)
                        for n in STEP_PRODUCTS[t]:
                            product(PROJ[n], h_cols)
                        if t >= 1:
                            pe.wait_ge(gtok_ready, t)
                            out = acquire(("gt", t - 1))
                            for f in range(BK):
                                nc.tensor.transpose(out[:, f * P:(f + 1) * P],
                                                    gtok[:, (t - 1) % 2, f * P:(f + 1) * P], ident[:])
                            for g in range(KVH):
                                mm = nc.tensor.transpose(out[:, BW + g * P:BW + (g + 1) * P],
                                                         kdup[:, (t - 1) % 2, g * P:(g + 1) * P], ident[:])
                            mm.then_inc(gt_full, 1)
                    pe.wait_ge(gc_dup, 1)
                    out = acquire(("gc",))
                    for g in range(KVH):
                        mm = nc.tensor.transpose(out[:, g * P:(g + 1) * P], kdup[:, NT % 2, g * P:(g + 1) * P], ident[:])
                    mm.then_inc(gc_full, 1)

                    pe.wait_ge(param_in, 48)
                    for f in range(4):
                        product(("ch", f), h_cols)
                        pe.wait_ge(pool_ready, f + 1)
                        out = acquire(("mix", f))
                        for g, (lo, hi) in enumerate(((0, LAT), (LAT, TOK))):
                            mm = nc.tensor.matmul(out[:, lo:hi], poolw[:, f, :], br[:, 3, f, lo:hi],
                                                  start=True, stop=True)
                        mm.then_inc(mix_full, 1)
                    for f in range(BK - 1):
                        product(("cb", f), h_cols)

                    def scores(a):
                        kind, b, h = ATT[a]
                        if a < NA_UNITS:
                            if a >= 4:
                                pe.wait_ge(probs_ready, a - 3)
                        else:
                            pe.wait_ge(probs_ready, a - 1)
                        out = scores_at(a)
                        half = slice(HD * (h % 2), HD * (h % 2) + HD)
                        q = (qT if kind == "na" else gqT)[half, h // 2, b * P:(b + 1) * P]
                        if kind == "na":
                            kt = na_kT[half, h // 2, :]
                            if b < NB:
                                win = kt[:, 0:LAT].rearrange("p (r c) -> p r c", c=GW)[:, :, KEY_COL[b]:KEY_COL[b] + KC]
                                nc.tensor.matmul(out[:, 0:NWIN], q, win, start=True, stop=False)
                                nc.tensor.matmul(out[:, 0:NWIN], ident_b[:], mask_b[:, (0, 1, 1, 2)[b], :],
                                                 start=False, stop=True)
                                mm = nc.tensor.matmul(out[:, NWIN:NA_KEYS], q, kt[:, TOK:TOK + PAST],
                                                      start=True, stop=True)
                            else:
                                mm = nc.tensor.matmul(out[:, 0:CTX], q, kt[:, LAT:TOK], start=True, stop=True)
                        else:
                            kt = gkT[half, h // (NH // KVH), :]
                            if b < NB:
                                nc.tensor.matmul(out[:, 0:LAT], q, kt[:, 0:LAT], start=True, stop=True)
                                mm = nc.tensor.matmul(out[:, LAT:LAT + PAST], q, kt[:, TOK:TOK + PAST],
                                                      start=True, stop=True)
                            else:
                                mm = nc.tensor.matmul(out[:, 0:CTX], q, kt[:, LAT:TOK], start=True, stop=True)
                        mm.then_inc(scores_full, 1)

                    def turn_probs(a):
                        if a >= 2:
                            pe.wait_ge(*turned_free(a - 2 if a < NA_UNITS else a - 1))
                        out = turned_at(a)
                        if key_tiles(a) == 1:
                            for _ in range(FILLERS):
                                nc.tensor.matmul(out[:, P:P + NWIN], ident_b[:], mask_b[:, 0, :], start=True, stop=True)
                        pe.wait_ge(probs_ready, a + 1)
                        for j in range(key_tiles(a)):
                            mm = nc.tensor.transpose(out[:, j * P:(j + 1) * P], probs[:, a % 3, j * P:(j + 1) * P],
                                                     ident[:])
                        mm.then_inc(pt_full, 1)

                    def values(a):
                        n, h = key_tiles(a), ATT[a][2]
                        pe.wait_ge(*turned_free(a))
                        if h == 0 and a >= 2 * NH:
                            pe.wait_ge(ot_copied, a // NH - 1)
                        if a == 2 * NH:
                            pe.wait_ge(vwin_in[1], 16 * NB)
                        for j in range(n):
                            mm = nc.tensor.matmul(out_at(a // NH)[:, h * HD:(h + 1) * HD],
                                                  pT[:, a % 2, j * P:(j + 1) * P],
                                                  value_tile(a, j), start=(j == 0), stop=(j == n - 1))
                        mm.then_inc(pv_done, 1)

                    def turn_block(j):
                        pe.wait_ge(o_copied, j + 1)
                        for f in range(BK):
                            mm = nc.tensor.transpose(out_at(j)[:, f * P:(f + 1) * P], otok[:, j % 2, f * P:(f + 1) * P],
                                                     ident[:])
                        mm.then_inc(ot_full, 1)

                    pe.wait_ge(gt_copied, 2 * NT)
                    pe.wait_ge(gc_copied, 1)
                    pe.wait_ge(kc_copied, 1)
                    pe.wait_ge(mix_copied, 4)
                    pe.wait_ge(conv_ready, 2)
                    for a in range(-1, NATT):
                        for u in units_to_score(a):
                            scores(u)
                        if a == -1:
                            product(("cb", BK - 1), h_cols)
                            pe.wait_ge(vwin_in[0], 16 * NB)
                            pe.wait_ge(cachev_in, 32)
                            pe.wait_ge(conv_ready, BK)
                        if a + 1 < NATT:
                            turn_probs(a + 1)
                        if a == NATT - 1:
                            product(("L", 0), h_cols)
                        if a >= 0:
                            values(a)
                        if a % NH == 1 and a > NH:
                            turn_block(a // NH - 1)
                    turn_block(NBLK - 1)

                    def branch_cols(n):
                        def rhs(k, i):
                            high, low = br_high[:, k, :], br_r[:, n, k, :]
                            if n == 0:
                                if i == 0:
                                    return tuple(a[:, 0:LAT].rearrange("p (b i r) -> p r b i", b=NB, i=QC)
                                                 for a in (high, low))
                                return high[:, LAT:TOK], low[:, LAT:TOK]
                            return high[:, i * HT:(i + 1) * HT], low[:, i * HT:(i + 1) * HT]
                        return rhs

                    pe.wait_ge(ot_copied, NBLK)
                    pe.wait_ge(*turned_free(NATT - 1))
                    for g in range(4 * DK):
                        n = merge_unit(g)[0]
                        if g:
                            product(("L", g), h_cols)
                        pe.wait_ge(br_ready, BK * (n + 1))
                        if n == 0:
                            product(("B", g), branch_cols(n), ((0, LAT), (LAT, CTX)))
                        else:
                            product(("B", g), branch_cols(n))

                    pe.wait_ge(merged_add, 2 * 4 * 4 - 2 * 4)
                    pe.wait_ge(prod_done, 4 * DK)
                    wo = [arrived(("wo", j)) for j in range(2)]
                    for t in range(NT + 3):
                        if t < NT:
                            out = acquire(("y", t))
                            for j in range(2):
                                for k in range(DK):
                                    mm = nc.tensor.matmul(out[:, j * BANK:(j + 1) * BANK], merged[:, k, t * P:(t + 1) * P],
                                                          wo[j][:, k * BANK:(k + 1) * BANK],
                                                          start=(k == 0), stop=(k == DK - 1))
                            mm.then_inc(y_full, 1)
                        if 2 <= t < NT + 2:
                            pe.wait_ge(xmT_ready, DK * (t - 1))
                            out = acquire(("r", t - 2))
                            for k in range(DK):
                                mm = nc.tensor.matmul(out[:, 0:NE], xmT[:, t % 2, k, :], router[:, k, :],
                                                      start=(k == 0), stop=(k == DK - 1))
                            mm.then_inc(r_full, 1)
                        if t >= 3:
                            pe.wait_ge(aff_ready, t - 2)
                            out = acquire(("affT", t - 3))
                            nc.tensor.transpose(out[0:NE, 0:P], aff[:, t - 3, :], ident[:]).then_inc(affT_full, 1)
                        if 1 <= t < NT + 1:
                            pe.wait_ge(x1_ready, t)
                            out = acquire(("x1T", t - 1))
                            for k in range(DK):
                                mm = nc.tensor.transpose(out[:, k * P:(k + 1) * P],
                                                         x1[:, (t - 1) % 2, k * P:(k + 1) * P], ident[:])
                            mm.then_inc(x1T_full, 1)
                    pe.wait_ge(topk_ready, 1)
                    out = acquire(("sel",))
                    nc.tensor.transpose(out[0:CAP, 0:NE], idx_f[:, :], ident[0:NE, 0:NE])
                    nc.tensor.transpose(out[0:CAP, NE:2 * NE], vals[:, :], ident[0:NE, 0:NE]).then_inc(sel_full, 1)

                    def part_waits(i, j, part):
                        n = PER_EXPERT * j + part
                        r = n % RING
                        pe.wait_ge(slot_full[r], i * (16 * BODY_SLOTS // RING)
                                   + 16 * (uses_before_experts(r) + n // RING + 1))
                        return ring[:, r, :]

                    def half_product(i, j, part, lhsT, pair_no, half):
                        w = part_waits(i, j, part)
                        for k in range(DK):
                            mm = nc.tensor.matmul(acc[pair_no][0:CAP, half, :], lhsT[:, k * CAP:(k + 1) * CAP],
                                                  w[:, k * BANK:(k + 1) * BANK], start=(k == 0), stop=(k == DK - 1))
                        mm.then_inc(part_done[part], 1)

                    def down_product(i, j, half):
                        w = part_waits(i, j, 4 + half)
                        for c in range(2):
                            for k in range(4):
                                kk = 4 * half + k
                                mm = nc.tensor.matmul(acc[2][0:CAP, c, :], hdnT[:, kk * CAP:(kk + 1) * CAP],
                                                      w[:, k * D + c * BANK:k * D + (c + 1) * BANK],
                                                      start=(kk == 0), stop=(kk == DK - 1))
                        mm.then_inc(part_done[4 + half], 1)

                    def turn_hidden(half):
                        for k in range(4):
                            mm = nc.tensor.transpose(acc[3][:, 0, k * CAP:(k + 1) * CAP],
                                                     hdn[:, half * BANK + k * P:half * BANK + (k + 1) * P],
                                                     ident[0:CAP, 0:CAP])
                        mm.then_inc(hT_full, 1)

                    def turn_rows(j, half):
                        for k in range(4):
                            mm = nc.tensor.transpose(acc[3][:, 1, k * CAP:(k + 1) * CAP],
                                                     xs[:, j, (4 * half + k) * P:(4 * half + k + 1) * P],
                                                     ident[0:CAP, 0:CAP])
                        mm.then_inc(xT_full, 1)

                    pe.wait_ge(gather_done, layer * (16 * (NE + 1)) + 16)
                    turn_rows(0, 0)
                    pe.wait_ge(xsT_ready, 1)
                    turn_rows(0, 1)
                    with pe.Fori(0, NE // EXPERTS_IN_BODY) as i:
                        for j in range(EXPERTS_IN_BODY):
                            e1 = i * EXPERTS_IN_BODY + (j + 1)
                            e2 = i * (2 * EXPERTS_IN_BODY) + 2 * (j + 1)
                            pe.wait_ge(xsT_ready, e2)
                            pe.wait_ge(silu_done, e2 - 1)
                            half_product(i, j, 0, xsT[:, j, :], 0, 0)
                            pe.wait_ge(hidden_ready, e2 - 1)
                            half_product(i, j, 1, xsT[:, j, :], 1, 0)
                            pe.wait_ge(silu_done, e2)
                            half_product(i, j, 2, xsT[:, j, :], 0, 1)
                            pe.wait_ge(hidden_ready, e2 + 1)
                            pe.wait_ge(hT_copied, e2)
                            turn_hidden(0)
                            half_product(i, j, 3, xsT[:, j, :], 1, 1)
                            pe.wait_ge(gather_done, layer * (16 * (NE + 1)) + i * (16 * EXPERTS_IN_BODY) + 16 * (j + 2))
                            turn_rows(1 - j, 0)
                            pe.wait_ge(hT_copied, e2 + 1)
                            pe.wait_ge(ye_ready, e1)
                            down_product(i, j, 0)
                            pe.wait_ge(hidden_ready, e2 + 2)
                            turn_hidden(1)
                            pe.wait_ge(xsT_ready, e2 + 1)
                            turn_rows(1 - j, 1)
                            pe.wait_ge(hT_copied, e2 + 2)
                            down_product(i, j, 1)

                @block.scalar
                def _(act):
                    copy = ACT.Copy
                    act.wait_ge(cond_in, 16)
                    nc.scalar.activation(cvec[:], cvec[:], ACT.Silu).then_inc(silu_ready, 1)

                    def high_weights(n):
                        r, use = slot_of(slot_key(PRODUCTS[n]))
                        kind, f = PRODUCTS[n]
                        act.wait_ge(slot_full[r], 16 * (use + 1))
                        if n < NPROJ:
                            if n >= 2:
                                act.wait_ge(*done(n - 2))
                        elif f >= 2:
                            act.wait_ge(*done(PRODUCT_NO[kind, f - 2]))
                        whole, _, high = weight_tile(n)
                        nc.scalar.activation(high, whole, copy).then_inc(w_high_ready, 1)

                    def high_ahead_of(n):
                        if 1 <= n < NPROJ - 1:
                            high_weights(n + 1)
                        act.wait_ge(*done(n))

                    for i in range(ADA_SLOTS):
                        act.wait_ge(ada_done, i + 1)
                        if i >= 2:
                            act.wait_ge(mod_full, i - 1)
                        nc.scalar.activation(adarow[:, i % 2, :], accf[pair(("ada", i))][0:2, 0:BANK], copy)\
                            .then_inc(ada_copied, 1)
                        if i == 0:
                            for t in range(NT):
                                act.wait_ge(xt_full, t + 1)
                                nc.scalar.activation(hT[:, :, t * P:(t + 1) * P],
                                                     accf[pair(("xt", t))].rearrange("p (k n) -> p k n", k=DK), copy)\
                                    .then_inc(xt_copied, 1)
                        if i in (5, 6):
                            for k in range((i - 5) * 4, (i - 4) * 4):
                                act.wait_ge(h_whole, 2 * (k + 1))
                                nc.scalar.activation(h_high[:, k, :], hT[:, k, :], copy).then_inc(h_high_ready, 1)
                        if i == ADA_SLOTS - 2:
                            high_weights(0)
                            high_weights(1)
                    for f in range(BK):
                        high_ahead_of(PRODUCT_NO["q", f])
                        a = acc[pair(("q", f))]
                        blocks = qT[:, f, 0:LAT].rearrange("p (b i r) -> p r b i", b=NB, i=QC)
                        rows = HT // GW
                        nc.scalar.activation(blocks[:, 0:rows], a[:, 0, 0:HT].rearrange("p (r b i) -> p r b i", r=rows, b=NB),
                                             copy, scale=QSCALE).then_inc(q_copied, 1)
                        nc.scalar.activation(blocks[:, rows:GR], a[:, 1, 0:LAT - HT]
                                             .rearrange("p (r b i) -> p r b i", r=GR - rows, b=NB),
                                             copy, scale=QSCALE).then_inc(q_copied, 1)
                        nc.scalar.activation(qT[:, f, LAT:TOK], a[:, 1, LAT - HT:HT], copy, scale=QSCALE)\
                            .then_inc(q_copied, 1)
                    act.wait_ge(gateT_full, 1)
                    nc.scalar.activation(grow[:], accf[pair(("gateT",))][0:32, 0:P], copy).then_inc(gateT_copied, 1)
                    act.wait_ge(gateT_copied, 1)
                    act.dma_start(gate_scr, grow[:]).then_inc(gate_out, 16)
                    for f in range(BK):
                        high_ahead_of(PRODUCT_NO["k", f])
                        nc.scalar.activation(by_half(na_kT[:, f, 0:TOK]), halves(("k", f)), copy).then_inc(k_copied, 1)
                    for f in range(BK):
                        high_ahead_of(PRODUCT_NO["v", f])
                        nc.scalar.activation(by_half(vT[:, f, :]), halves(("v", f)), copy).then_inc(vraw_copied, 1)
                        if f == 0:
                            act.wait_ge(kc_full, 1)
                            nc.scalar.activation(na_kT[:, :, TOK:TOK + PAST],
                                                 accf[pair(("kc",))][:, 0:BW].rearrange("p (f n) -> p f n", f=BK), copy)\
                                .then_inc(kc_copied, 1)
                            act.wait_ge(ks_full, 1)
                            nc.scalar.activation(k_state, accf[pair(("ks",))][:, 0:BW], copy).then_inc(ks_copied, 1)
                            act.wait_ge(ks_copied, 1)
                            act.dma_start(st_na_k[layer], k_state).then_inc(state_out, 16)

                    def copy_gq(f):
                        high_ahead_of(PRODUCT_NO["gq", f])
                        nc.scalar.activation(by_half(gq_raw[:, f, :]), halves(("gq", f)), copy).then_inc(graw_copied, 1)

                    copy_gq(0)
                    for t in range(NT):
                        act.wait_ge(v_full, t + 1)
                        nc.scalar.activation(vstage[:, t, :] if t < NLT else vctx, accf[pair(("vt", t))][:, 0:BW], copy)\
                            .then_inc(v_copied, 1)
                    act.wait_ge(v_copied, NT)
                    act.dma_start(st_na_v[layer], vctx).then_inc(state_out, 16)
                    act.dma_start(v_scr.rearrange("(t p) n -> p t n", p=P), vstage).then_inc(vscr_out, 16)

                    for f in range(1, BK):
                        copy_gq(f)
                    for f in range(2):
                        high_ahead_of(PRODUCT_NO["gkv", f])
                        nc.scalar.activation(by_half(kv_raw[:, f, :]), halves(("gkv", f)), copy)\
                            .then_inc(graw_copied, 1)

                    act.wait_ge(state_out, 32)
                    for t in range(NT + 1):
                        if t < NT:
                            act.wait_ge(g_full, t + 1)
                            a = accf[pair(("g", t))]
                            if t >= 2:
                                act.wait_ge(gt_full, t - 1)
                            nc.scalar.activation(gtok[:, t % 2, 0:640], a[:, 0:640], copy).then_inc(g_copied, 1)
                            nc.scalar.activation(gv[:, t, :], a[:, 640:768], copy).then_inc(g_copied, 1)
                            act.wait_ge(ss_ready, t + 1)
                            nc.scalar.activation(qk_std[:, t, :], qk_ss[:, t, :], ACT.Sqrt, bias=eps[:, 0:1],
                                                 scale=1.0 / HD).then_inc(std_ready, 1)
                        for n in STEP_PRODUCTS[t]:
                            high_ahead_of(n)
                            kind, f = PROJ[n]
                            if n == 18:
                                act.wait_ge(vscr_out, 16)
                            nc.scalar.activation(by_half(br[:, 3 if kind == "pool" else 2, f, :]), halves((kind, f)), copy)\
                                .then_inc(pool_copied if kind == "pool" else c_copied, 1)
                        if t >= 1:
                            act.wait_ge(gt_full, t)
                            a = accf[pair(("gt", t - 1))]
                            c0 = (t - 1) * P
                            nc.scalar.activation(gqT[:, :, c0:c0 + P],
                                                 a[:, 0:BW].rearrange("p (f n) -> p f n", f=BK), copy, scale=QSCALE)\
                                .then_inc(gt_copied, 1)
                            nc.scalar.activation(gkT[:, :, c0:c0 + P],
                                                 a[:, BW:BW + 2 * P].rearrange("p (f n) -> p f n", f=KVH), copy)\
                                .then_inc(gt_copied, 1)
                    act.wait_ge(gtok_ready, NT)
                    act.dma_start(st_g_k[layer], gtok[:, (NT - 1) % 2, BW:BW + P]).then_inc(state_out, 16)
                    act.wait_ge(g_copied, 2 * NT)
                    act.dma_start(st_g_v[layer], gv[:, NT - 1, :]).then_inc(state_out, 16)
                    act.wait_ge(gc_full, 1)
                    nc.scalar.activation(gkT[:, :, TOK:TOK + PAST],
                                         accf[pair(("gc",))][:, 0:2 * P].rearrange("p (f n) -> p f n", f=KVH), copy)\
                        .then_inc(gc_copied, 1)
                    act.wait_ge(small_in, 16)
                    for f in range(4):
                        high_weights(PRODUCT_NO["ch", f] + 1)
                        act.wait_ge(mix_full, f + 1)
                        nc.scalar.activation(br[:, 3, f, :], accf[pair(("mix", f))][:, 0:TOK], copy,
                                             scale=smallp[:, 64 + f:65 + f]).then_inc(mix_copied, 1)

                    def load_windows(first):
                        for b in range(first, first + 2):
                            for half in range(2):
                                rows = v_scr.rearrange("(r c) n -> r c n", c=GW)[4 * half:4 * half + 4,
                                                                               KEY_COL[b]:KEY_COL[b] + KC, :]
                                act.dma_start(vwin[:, 2 * b + half, :], rows).then_inc(vwin_in[first // 2], 16)

                    for f in range(1, BK):
                        high_weights(PRODUCT_NO["cb", f])
                        if f == 1:
                            act.wait_ge(kc_full, 1)
                            act.wait_ge(gc_dup, 1)
                            act.wait_ge(gtok_ready, NT)
                            load_windows(0)
                    def exps(a):
                        n = key_tiles(a) * P
                        act.wait_ge(rowmax_ready, a + 1)
                        if a >= 3:
                            act.wait_ge(pt_full, a - 2)
                        nc.scalar.activation(probs[:, a % 3, 0:n], scores_at(a)[:, 0:n], ACT.Exp,
                                             bias=negmax[:, a:a + 1], accum_out=sums[:, a:a + 1])\
                            .then_inc(probs_ready, 1)

                    def block_out(j):
                        kind, b, _ = ATT[j * NH]
                        act.wait_ge(ot_full, j + 1)
                        dst = (qT if kind == "na" else gqT)[:, :, b * P:(b + 1) * P]
                        nc.scalar.activation(dst, out_at(j).rearrange("p (f n) -> p f n", f=BK), copy)\
                            .then_inc(ot_copied, 1)

                    def high_branch(n):
                        for k in range(BK):
                            nc.scalar.activation(br_high[:, k, :], br[:, n, k, :], copy).then_inc(br_high_ready, 1)

                    act.wait_ge(state_out, 64)
                    for a in range(-1, NATT):
                        if a == NATT - 2:
                            high_weights(PRODUCT_NO["L", 0])
                            act.wait_ge(ot_copied, NBLK // 2)
                            high_branch(0)
                        for u in units_to_score(a):
                            exps(u)
                        if a + 1 < NA_UNITS:
                            n = key_tiles(a + 1) * P
                            act.wait_ge(pt_full, a + 2)
                            if a >= 1:
                                act.wait_ge(pv_done, a)
                            nc.scalar.activation(pT[:, (a + 1) % 2, 0:n], turned_at(a + 1)[:, 0:n], copy)\
                                .then_inc(pt_copied_act, 1)
                        if a == 0:
                            act.wait_ge(*done(NPROJ - 1))
                            load_windows(2)
                        if a % NH == 1 and a > NH:
                            block_out(a // NH - 1)
                    block_out(NBLK - 1)

                    act.wait_ge(ot_copied, NBLK)
                    act.wait_ge(conv_ready, BK)
                    high_weights(PRODUCT_NO["B", 0])
                    act.wait_ge(gate_out, 16)

                    def load_ln(n, dst, signal):
                        a = ln_p[layer, n]
                        act.dma_start(dst, bass.AP(a.tensor, a.offset, [[0, P], [1, D]])).then_inc(signal, 16)

                    load_ln(1, lnb, ln1_in)
                    for g in range(2):
                        act.dma_start(gate1[:, g, :].rearrange("p (k n) -> p k n", k=DK),
                                      bass.AP(gate_scr.tensor, gate_scr.offset + g * P, [[0, P], [2 * P, DK], [1, P]]))\
                            .then_inc(gate1_in, 16)
                    for g in range(4 * DK):
                        if g + 1 < 4 * DK:
                            high_weights(PRODUCT_NO["L", g + 1])
                            high_weights(PRODUCT_NO["B", g + 1])
                        if g and g % DK == 0:
                            act.wait_ge(*done(PRODUCT_NO["B", g - 1]))
                            high_branch(g // DK)
                        act.wait_ge(*done(PRODUCT_NO["L", g]))
                        if g >= 2:
                            act.wait_ge(prod_done, g - 1)
                        nc.scalar.activation(by_half(sg[:, g % 2, :]), halves(("L", g)), ACT.Sigmoid)\
                            .then_inc(sig_ready, 1)

                    def load_x(t):
                        if t >= 2:
                            act.wait_ge(z_free, t - 1)
                        act.dma_start(xin[:, t % 2, :], out_rows(t)).then_inc(xin_in[t % 2], 16)

                    act.wait_ge(prod_done, 4 * DK)
                    act.wait_ge(merged_add, 3 * DK)
                    load_ln(0, lng, ln1_in)
                    load_x(0)
                    load_x(1)
                    for t in range(NT + 2):
                        if t < NT:
                            act.wait_ge(var_ready, t + 1)
                            nc.scalar.activation(std[:, 0, t:t + 1], mv[:, 0, t, 1:2], ACT.Sqrt, bias=eps[:, 0:1])\
                                .then_inc(std1_ready, 1)
                            if t + 2 < NT:
                                load_x(t + 2)
                            act.wait_ge(x1_ready, t + 1)
                            act.dma_start(x1_scr[t * P:(t + 1) * P, :], x1[:, t % 2, :]).then_inc(x1_out[t % 2], 16)
                            act.wait_ge(xa_ready, t + 1)
                            act.dma_start(y_acc[t * P:(t + 1) * P, :], xa[:, t % 2, :]).then_inc(x1_out[t % 2], 16)
                        if t >= 2:
                            act.wait_ge(negl_ready, t - 1)
                            nc.scalar.activation(lg[:, t - 2, 4:4 + NE], accf[pair(("r", t - 2))][:, 0:NE], ACT.Exp,
                                                 bias=lg[:, t - 2, 1:2], accum_out=lg[:, t - 2, 2:3])\
                                .then_inc(el_ready, 1)
                        if 1 <= t < NT + 1:
                            act.wait_ge(x1T_full, t)
                            if t >= 3:
                                act.wait_ge(r_full, t - 2)
                            g = 0 if t - 1 < NLT else 1
                            for k in range(DK):
                                nc.scalar.activation(xmT[:, (t - 1) % 2, k, :],
                                                     accf[pair(("x1T", t - 1))][:, k * P:(k + 1) * P], ACT.Identity,
                                                     scale=mod[:, g, 32 + k:33 + k], bias=mod[:, g, 24 + k:25 + k])\
                                    .then_inc(xmT_ready, 1)

                    act.sem_inc(silu_done, 2)
                    act.sem_inc(hT_copied, 2)
                    act.wait_ge(xa_ready, NT)
                    load_ln(2, lng, ln2_in)
                    load_ln(3, lnb, ln2_in)
                    act.wait_ge(y_full, NT)
                    for g, lo, hi in ((0, 0, CAP_L), (1, CAP_L, CAP)):
                        act.dma_start(gate2[lo:hi, :].rearrange("p (k n) -> p k n", k=DK),
                                      bass.AP(gate_scr.tensor, gate_scr.offset + (16 + g) * P,
                                              [[0, hi - lo], [2 * P, DK], [1, P]])).then_inc(gate2_in, 16)
                    with act.Fori(0, NE // EXPERTS_IN_BODY) as i:
                        for j in range(EXPERTS_IN_BODY):
                            e1 = i * EXPERTS_IN_BODY + (j + 1)
                            e2 = i * (2 * EXPERTS_IN_BODY) + 2 * (j + 1)
                            for half, gate_done in ((0, gate0_done), (1, gate1_done)):
                                cols = slice(half * BANK, (half + 1) * BANK)
                                act.wait_ge(gate_done, e1)
                                act.wait_ge(hidden_ready, e2 - 1 + half)
                                nc.scalar.activation(act_s[:, cols], acc[0][0:CAP, half, :], ACT.Silu)\
                                    .then_inc(silu_done, 1)
                            for half in range(2):
                                act.wait_ge(hT_full, e2 - 1 + half)
                                nc.scalar.activation(hdnT[:, half * 4 * CAP:(half + 1) * 4 * CAP],
                                                     acc[3][:, 0, 0:4 * CAP], copy).then_inc(hT_copied, 1)

                    act.wait_ge(scatter_done, layer * (16 * NE) + 16 * NE)
                    for t in range(2):
                        act.dma_start(xin[:, t % 2, :], y_acc[t * P:(t + 1) * P, :]).then_inc(zin_in[t % 2], 16)
                    for t in range(NT):
                        act.wait_ge(var2_ready, t + 1)
                        nc.scalar.activation(std[:, 1, t:t + 1], mv[:, 1, t, 1:2], ACT.Sqrt, bias=eps[:, 0:1])\
                            .then_inc(std2_ready, 1)
                        act.wait_ge(x2_ready, t + 1)
                        act.dma_start(out_rows(t), x1[:, t % 2, :]).then_inc(x2_out[t % 2], 16)
                        if t + 2 < NT:
                            act.dma_start(xin[:, t % 2, :], y_acc[(t + 2) * P:(t + 3) * P, :]).then_inc(zin_in[t % 2], 16)
                    for p in range(2):
                        act.wait_ge(x2_out[p], 16 * ((NT + 1 - p) // 2))

                @block.vector
                def _(dve):
                    v = nc.vector
                    chained = [0]

                    def link(ins):
                        chained[0] += 1
                        ins.then_inc(dve_step, 1)
                        dve.wait_ge(dve_step, chained[0])

                    def low_weights(n):
                        dve.wait_ge(w_high_ready, n + 1)
                        whole, low, high = weight_tile(n)
                        v.tensor_tensor(low, whole, high, ALU.subtract).then_inc(w_ready, 1)

                    def modulation(lo, hi, bank):
                        return v.tensor_tensor(mod[:].rearrange("p g c -> p c g")[:, lo:hi],
                                               bank[:, 2 * lo:2 * hi].rearrange("p (c g) -> p c g", g=2),
                                               bc(smallp[:, lo:hi], (1, hi - lo), (0, 2)), ALU.add)

                    dve.wait_ge(small_in, 16)
                    dve.wait_ge(mod_full, 4)
                    link(modulation(0, 16, o_bank))
                    link(v.tensor_scalar(mod[:, :, 8:16], mod[:, :, 8:16], 1.0, None, ALU.add))
                    dve.wait_ge(xt_copied, NT)
                    for k in range(DK):
                        for g in range(2):
                            x = hT[:, k, group_cols(g)]
                            v.tensor_scalar(x, x, mod[:, g, 8 + k:9 + k], mod[:, g, k:k + 1], ALU.mult, ALU.add)\
                                .then_inc(h_whole, 1)
                    for k in range(DK):
                        dve.wait_ge(h_high_ready, k + 1)
                        v.tensor_tensor(hT_r[:, k, :], hT[:, k, :], h_high[:, k, :], ALU.subtract).then_inc(h_ready, 1)
                    low_weights(0)
                    low_weights(1)
                    dve.wait_ge(mod_full, ADA_SLOTS)
                    modulation(16, 48, ot_bank).then_inc(mod_ready, 1)
                    dve.wait_ge(mod_ready, 1)
                    v.tensor_scalar(mod[:, :, 32:40], mod[:, :, 32:40], 1.0, None, ALU.add).then_inc(dve_step, 1)
                    chained[0] += 1
                    v.tensor_copy(gate_cols.rearrange("p (j k g) -> p j k g", j=2, g=2),
                                  bc(mod[:, 0, 16:24], (24, 2), (1, DK), (48, 2))).then_inc(mod_ready, 1)
                    dve.wait_ge(dve_step, chained[0])
                    for n in range(2, 19):
                        low_weights(n)

                    def duplicate(dst, src):
                        return v.tensor_copy(dst.rearrange("p (g c n) -> p g c n", g=KVH, c=2),
                                             bc(src, (HD, KVH), (0, 2), (1, HD)))

                    dve.wait_ge(param_in, 48)
                    for t in range(NT):
                        x = gtok[:, t % 2, 0:640]
                        dve.wait_ge(g_copied, 2 * t + 2)
                        link(v.tensor_tensor(t1, x, x, ALU.mult))
                        v.tensor_reduce(qk_ss[:, t, :], t1.rearrange("p (h d) -> p h d", d=HD), AX.X, ALU.add)\
                            .then_inc(ss_ready, 1)
                        dve.wait_ge(std_ready, t + 1)
                        link(v.reciprocal(qk_rstd[:, t, :], qk_std[:, t, :]))
                        xh = x.rearrange("p (h d) -> p h d", d=HD)
                        link(v.tensor_tensor(xh, xh, bc(qk_rstd[:, t, :], (1, 10), (0, HD)), ALU.mult))
                        link(v.tensor_tensor(xh[:, 0:NH, :], xh[:, 0:NH, :], bc(gain[:, 0, :], (0, NH), (1, HD)), ALU.mult))
                        link(v.tensor_tensor(xh[:, NH:10, :], xh[:, NH:10, :], bc(gain[:, 1, :], (0, KVH), (1, HD)), ALU.mult))
                        if t < NLT:
                            link(v.tensor_tensor(t1.rearrange("p (h d) -> p h d", d=HD), xh,
                                                 bc(rope[:, t, 0, :], (0, 10), (1, HD)), ALU.mult))
                            link(v.tensor_tensor(t2.rearrange("p (h d) -> p h d", d=HD), xh,
                                                 bc(rope[:, t, 1, :], (0, 10), (1, HD)), ALU.mult))
                            x4, c4, s4 = (z.rearrange("p (h q n) -> p h q n", h=20, q=2) for z in (x, t1, t2))
                            link(v.tensor_tensor(x4[:, :, 0, :], c4[:, :, 0, :], s4[:, :, 1, :], ALU.subtract))
                            link(v.tensor_tensor(x4[:, :, 1, :], s4[:, :, 0, :], c4[:, :, 1, :], ALU.add))
                        if t >= 2:
                            dve.wait_ge(gt_full, t - 1)
                        duplicate(kdup[:, t % 2, :], x[:, BW:BW + P]).then_inc(gtok_ready, 1)
                        for n in STEP_PRODUCTS[t]:
                            low_weights(n + 1)
                    low_weights(26)
                    dve.wait_ge(kcache_in, 32)
                    dve.wait_ge(gt_full, NT - 1)
                    duplicate(kdup[:, NT % 2, :], g_cached).then_inc(gc_dup, 1)

                    dve.wait_ge(gc_full, 1)
                    for i in range(3):
                        link(v.memset(pu[i], 0.0))

                    def pooling(f, win):
                        dve.wait_ge(pool_copied, f + 1)
                        if f:
                            dve.wait_ge(pool_ready, f)
                        u, wa, wb = pu[0], pu[1], pu[2]
                        link(v.tensor_copy(u[:, 8:8 + LAT], br[:, 3, f, 0:LAT]))
                        link(v.tensor_copy(u[:, 24 + LAT:24 + TOK], br[:, 3, f, LAT:TOK]))
                        link(v.tensor_tensor(wa[:, 1:PW], u[:, 0:PW - 1], u[:, 1:PW], ALU.add))
                        cur, other, step, lo = wa, wb, 1, 1
                        while 2 * step < win:
                            lo += step
                            link(v.tensor_tensor(other[:, lo:PW - lo + 1], cur[:, lo - step:PW - lo + 1 - step],
                                                 cur[:, lo + step:PW - lo + 1 + step], ALU.add))
                            cur, other, step = other, cur, 2 * step
                        for at0, n in ((8, LAT), (24 + LAT, CTX)):
                            e = bc(cur[:, at0:at0 + 1], (n - 8, 2), (1, 8))
                            link(v.tensor_tensor(e, e, corr[:, f, :].rearrange("p (a b) -> p a b", a=2), ALU.mult))
                        for at0, n, o in ((8, LAT, 0), (24 + LAT, CTX, LAT)):
                            ins = v.scalar_tensor_tensor(out=br[:, 3, f, o:o + n], in0=cur[:, at0:at0 + n],
                                                         scalar=1.0 / win, in1=u[:, at0:at0 + n],
                                                         op0=ALU.mult, op1=ALU.subtract)
                            if o == 0:
                                link(ins)
                        ins.then_inc(pool_ready, 1)

                    for f, win in enumerate(POOL_WINDOWS):
                        low_weights(PRODUCT_NO["ch", f] + 1)
                        pooling(f, win)
                        dve.wait_ge(c_copied, f + 1)
                        dve.wait_ge(*done(PRODUCT_NO["ch", f]))
                        u = by_half(br[:, 2, f, :])
                        v.tensor_tensor(u, halves(("ch", f)), u, ALU.mult).then_inc(u_ready, 1)
                    def conv_product(f):
                        dve.wait_ge(*done(PRODUCT_NO["cb", f]))
                        v.tensor_tensor(by_half(br[:, 2, f, :]), halves(("cb", f)), by_half(conv_y), ALU.mult)\
                            .then_inc(conv_ready, 1)

                    dve.wait_ge(pool_ready, 4)
                    for f in range(BK):
                        if f < BK - 1:
                            low_weights(PRODUCT_NO["cb", f] + 1)
                        dve.wait_ge(u_ready, f + 1)
                        if f:
                            dve.wait_ge(conv_ready, f)
                        u = br[:, 2, f, :]
                        tap = [smallp[:, 48 + 3 * f + j:49 + 3 * f + j] for j in range(3)]
                        link(v.tensor_scalar(conv_y, u, tap[1], smallp[:, 60 + f:61 + f], ALU.mult, ALU.add))
                        for lo, hi in ((0, LAT), (LAT, TOK)):
                            link(v.scalar_tensor_tensor(out=conv_y[:, lo + 1:hi], in0=u[:, lo:hi - 1], scalar=tap[0],
                                                        in1=conv_y[:, lo + 1:hi], op0=ALU.mult, op1=ALU.add))
                            link(v.scalar_tensor_tensor(out=conv_y[:, lo:hi - 1], in0=u[:, lo + 1:hi], scalar=tap[2],
                                                        in1=conv_y[:, lo:hi - 1], op0=ALU.mult, op1=ALU.add))
                        if f < BK - 1:
                            conv_product(f)

                    def maxima(a):
                        kind, b, h = ATT[a]
                        n = key_tiles(a) * P
                        out = scores_at(a)
                        dve.wait_ge(scores_full, a + 1)
                        if kind == "na" and b < NB:
                            if a == 0:
                                dve.wait_ge(bias_in, 16 * GR * GR)
                            win = out[:, 0:NWIN].rearrange("p (r c) -> p r c", c=KC)
                            link(v.tensor_tensor(win, win, bias_of(h, b), ALU.add))
                        v.reduce_max(negmax[:, a:a + 1], out[:, 0:n], AX.X, negate=True).then_inc(rowmax_ready, 1)

                    def block_norm(j):
                        dve.wait_ge(pv_done, NH * (j + 1))
                        link(v.reciprocal(rsum[:, NH * j:NH * (j + 1)], sums[:, NH * j:NH * (j + 1)]))
                        if j >= 2:
                            dve.wait_ge(ot_full, j - 1)
                        v.tensor_tensor(otok[:, j % 2, :].rearrange("p (h d) -> p h d", d=HD),
                                        out_at(j).rearrange("p (h d) -> p h d", d=HD),
                                        bc(rsum[:, NH * j:NH * (j + 1)], (1, NH), (0, HD)), ALU.mult)\
                            .then_inc(o_copied, 1)

                    def low_branch(n):
                        for k in range(BK):
                            dve.wait_ge(br_high_ready, BK * n + k + 1)
                            v.tensor_tensor(br_r[:, n, k, :], br[:, n, k, :], br_high[:, k, :], ALU.subtract)\
                                .then_inc(br_ready, 1)

                    for a in range(-1, NATT):
                        for u in units_to_score(a):
                            maxima(u)
                        if a == -1:
                            conv_product(BK - 1)
                        if a == NATT - 2:
                            low_weights(PRODUCT_NO["L", 0])
                            low_branch(0)
                        if NA_UNITS <= a + 1 < NATT:
                            n = key_tiles(a + 1) * P
                            dve.wait_ge(pt_full, a + 2)
                            dve.wait_ge(pv_done, a)
                            v.tensor_copy(pT[:, (a + 1) % 2, 0:n], turned_at(a + 1)[:, 0:n])\
                                .then_inc(pt_copied_dve, 1)
                        if a >= 0 and a % NH == NH - 1:
                            block_norm(a // NH)

                    dve.wait_ge(ot_full, NBLK)
                    low_weights(PRODUCT_NO["B", 0])
                    added = 0
                    for g in range(4 * DK):
                        if g + 1 < 4 * DK:
                            low_weights(PRODUCT_NO["L", g + 1])
                            low_weights(PRODUCT_NO["B", g + 1])
                        n, _, d = merge_unit(g)
                        if g and g % DK == 0:
                            low_branch(n)
                        a = accf[pair(("B", g))][:, 0:TOK] if n == 0 else halves(("B", g))
                        gates = sg[:, g % 2, :] if n == 0 else by_half(sg[:, g % 2, :])
                        dve.wait_ge(sig_ready, g + 1)
                        dve.wait_ge(*done(PRODUCT_NO["B", g]))
                        if n == 0:
                            v.tensor_tensor(merged[:, d, :], a, gates, ALU.mult).then_inc(prod_done, 1)
                            continue
                        if added:
                            dve.wait_ge(merged_add, added)
                        added += 1
                        v.tensor_tensor(by_half(prod[:, g % 2, :]), a, gates, ALU.mult).then_inc(prod_done, 1)
                        dve.wait_ge(prod_done, g + 1)
                        v.tensor_tensor(merged[:, d, :], merged[:, d, :], prod[:, g % 2, :], ALU.add)\
                            .then_inc(merged_add, 1)

                    def layer_norm(n, t, z, out, var_ready, std_ready, got):
                        for j in range(2):
                            link(v.bn_stats(stats[:, n, t, 6 * j:6 * j + 6], z[:, j * BANK:(j + 1) * BANK]))
                        v.bn_aggr(mv[:, n, t, :], stats[:, n, t, :]).then_inc(var_ready, 1)
                        dve.wait_ge(std_ready, t + 1)
                        link(v.reciprocal(rstd[:, n, t:t + 1], std[:, n, t:t + 1]))
                        link(v.tensor_scalar(z, z, mv[:, n, t, 0:1], rstd[:, n, t:t + 1], ALU.subtract, ALU.mult))
                        link(v.tensor_tensor(z, z, lng, ALU.mult))
                        v.tensor_tensor(out, z, lnb, ALU.add).then_inc(got, 1)

                    dve.wait_ge(ln1_in, 32)
                    dve.wait_ge(gate1_in, 32)
                    for t in range(NT + 3):
                        if t < NT:
                            g = 0 if t < NLT else 1
                            z = zt[:, t % 2, :]
                            dve.wait_ge(y_full, t + 1)
                            link(v.tensor_tensor(z, accf[pair(("y", t))], gate1[:, g, :], ALU.mult))
                            dve.wait_ge(xin_in[t % 2], 16 * (t // 2 + 1))
                            v.scalar_tensor_tensor(out=z, in0=xin[:, t % 2, :], scalar=ALPHA, in1=z,
                                                   op0=ALU.mult, op1=ALU.add).then_inc(z_free, 1)
                            dve.wait_ge(z_free, t + 1)
                            if t >= 2:
                                dve.wait_ge(x1T_full, t - 1)
                                dve.wait_ge(x1_out[t % 2], 32 * (t // 2))
                            layer_norm(0, t, z, x1[:, t % 2, :], var_ready, std1_ready, x1_ready)
                            dve.wait_ge(x1_ready, t + 1)
                            v.tensor_scalar(xa[:, t % 2, :], x1[:, t % 2, :], ALPHA, None, ALU.mult)\
                                .then_inc(xa_ready, 1)
                        if 2 <= t < NT + 2:
                            q = t - 2
                            a = accf[pair(("r", q))][:, 0:NE]
                            dve.wait_ge(r_full, q + 1)
                            v.reduce_max(lg[:, q, 1:2], a, AX.X, negate=True).then_inc(negl_ready, 1)
                            dve.wait_ge(el_ready, q + 1)
                            link(v.reciprocal(lg[:, q, 3:4], lg[:, q, 2:3]))
                            v.tensor_scalar(aff[:, q, :], lg[:, q, 4:4 + NE], lg[:, q, 3:4], None, ALU.mult)\
                                .then_inc(aff_ready, 1)
                        if t >= 3:
                            q = t - 3
                            dve.wait_ge(affT_full, q + 1)
                            v.tensor_copy(affT[:, q * P:(q + 1) * P], accf[pair(("affT", q))][0:NE, 0:P])\
                                .then_inc(affT_copied, 1)

                    dve.wait_ge(affT_copied, NT)
                    for g, cap, first in ((0, CAP_L, 0), (1, CAP_C, CAP_L)):
                        row = affT[:, group_cols(g)]
                        for r in range(cap // 8):
                            v8 = vals[:, first + 8 * r:first + 8 * r + 8]
                            link(v.max(v8, row))
                            link(v.max_index(idx_u[:, first + 8 * r:first + 8 * r + 8], v8, row))
                            link(v.match_replace(row, v8, row, -1.0))
                    link(v.tensor_copy(idx_f[:, 0:CAP_L], idx_u[:, 0:CAP_L]))
                    v.tensor_scalar(idx_f[:, CAP_L:CAP], idx_u[:, CAP_L:CAP], float(LAT), None, ALU.add)\
                        .then_inc(topk_ready, 1)
                    dve.wait_ge(sel_full, 1)
                    a = accf[pair(("sel",))]
                    link(v.tensor_copy(idx_t[:, NE:NE + 1], a[0:CAP, 0:1]))
                    link(v.tensor_copy(g_t[:, NE:NE + 1], a[0:CAP, NE:NE + 1]))
                    v.tensor_copy(idx_t[:, 0:NE], a[0:CAP, 0:NE]).then_inc(sel_ready, 1)
                    v.tensor_copy(g_t[:, 0:NE], a[0:CAP, NE:2 * NE]).then_inc(sel_ready, 1)
                    dve.wait_ge(sel_ready, 2)

                    dve.sem_inc(hidden_ready, 2)
                    dve.sem_inc(ye_ready, 1)

                    def choose(e, j, first):
                        v.tensor_copy(idx_cur[:, j:j + 1], idx_t[:, bass.ds(e, 1)]).then_inc(first, 1)
                        v.tensor_copy(g_cur[:, j:j + 1], g_t[:, bass.ds(e, 1)]).then_inc(sel_cur, 1)

                    def modulate(x, half, sem_, count):
                        def parts(a, base, step):
                            return bc(a[:, base:base + 1], (CAP, 4), (1, step))
                        for vec, op in ((32 + 4 * half, ALU.mult), (24 + 4 * half, ALU.add)):
                            for g, c0, n in ((0, 0, CAP_L), (1, CAP_L, CAP_C)):
                                dst = parts(x, 4 * CAP * half + c0, n)
                                src = parts(acc[3][:, 1, :], c0, n) if op == ALU.mult else dst
                                ins = v.tensor_tensor(dst, src, bc(mod[:, g, vec:vec + 1], (1, 4), (0, n)), op)
                                if op == ALU.add and g == 1:
                                    ins.then_inc(xsT_ready, 1)
                                else:
                                    ins.then_inc(sem_, 1)
                            if op == ALU.mult:
                                dve.wait_ge(sem_, count + 2)

                    choose(0, 0, dve_step)
                    chained[0] += 1
                    for half in range(2):
                        dve.wait_ge(xT_full, half + 1)
                        modulate(xsT[:, 0, :], half, dve_step, chained[0])
                        chained[0] += 3
                    dve.wait_ge(gate2_in, 32)
                    LOOP_INCS = 7
                    with dve.Fori(0, NE // EXPERTS_IN_BODY) as i:
                        for j in range(EXPERTS_IN_BODY):
                            e1 = i * EXPERTS_IN_BODY + (j + 1)
                            e2 = i * (2 * EXPERTS_IN_BODY) + 2 * (j + 1)
                            base = i * (LOOP_INCS * EXPERTS_IN_BODY) + LOOP_INCS * j

                            def hidden(half):
                                cols = slice(half * BANK, (half + 1) * BANK)
                                dve.wait_ge((up0_done, up1_done)[half], e1)
                                dve.wait_ge(silu_done, e2 + 1 + half)
                                v.tensor_tensor(hdn[:, cols], acc[1][0:CAP, half, :], act_s[:, cols], ALU.mult)\
                                    .then_inc(hidden_ready, 1)

                            hidden(0)
                            dve.wait_ge(ye_free, e1 + 1)
                            choose(e1, 1 - j, dve_loop)
                            hidden(1)
                            for half in range(2):
                                dve.wait_ge(xT_full, e2 + 1 + half)
                                modulate(xsT[:, 1 - j, :], half, dve_loop, base + 1 + 3 * half)
                            dve.wait_ge(down1_done, e1)
                            dve.wait_ge(ye_free, e1)
                            v.scalar_tensor_tensor(out=ye[:, j, :], in0=accf[2][0:CAP, :], scalar=g_cur[:, j:j + 1],
                                                   in1=gate2, op0=ALU.mult, op1=ALU.mult).then_inc(ye_ready, 1)

                    dve.wait_ge(ln2_in, 32)
                    for t in range(NT):
                        dve.wait_ge(zin_in[t % 2], 16 * (t // 2 + 1))
                        if t >= 2:
                            dve.wait_ge(x2_out[t % 2], 16 * (t // 2))
                        layer_norm(1, t, xin[:, t % 2, :], x1[:, t % 2, :], var2_ready, std2_ready, x2_ready)

                @block.gpsimd
                def _(pool):
                    pool.sem_inc(ye_free, 2)
                    for p in range(2):
                        pool.wait_ge(x1_out[p], 32 * ((NT + 1 - p) // 2))

                    def gather(j):
                        pool.indirect_dma_start(xs[:, j, :], None, x1_scr,
                                                bass.IndirectOffsetOnAxis(ap=idx_cur[:, j:j + 1], axis=0))\
                            .then_inc(gather_done, 16)

                    pool.wait_ge(sel_cur, 1)
                    gather(0)
                    with pool.Fori(0, NE // EXPERTS_IN_BODY) as i:
                        for j in range(EXPERTS_IN_BODY):
                            e1 = i * EXPERTS_IN_BODY + (j + 1)
                            pool.wait_ge(sel_cur, e1 + 1)
                            pool.sem_inc(pool_turn, 1)
                            gather(1 - j)
                            pool.wait_ge(ye_ready, e1 + 1)
                            pool.sem_inc(pool_turn, 1)
                            pool.indirect_dma_start(y_acc, bass.IndirectOffsetOnAxis(ap=idx_cur[:, j:j + 1], axis=0),
                                                    ye[:, j, :], None, compute_op=ALU.add).then_inc(scatter_done, 16)
                            pool.wait_ge(scatter_done, layer * (16 * NE) + i * (16 * EXPERTS_IN_BODY) + 16 * (j + 1))
                            pool.sem_inc(ye_free, 1)
                    pool.wait_ge(gather_done, layer * (16 * (NE + 1)) + 16 * (NE + 1))

            nc.multi_engine_barrier(nc.engines, sems_to_clear=range(cleared_from.num, cleared_to.num + 1))


def layout(inputs):
    a = {k: np.asarray(v) for k, v in inputs.items()}

    def blocks(w, n_k, width):
        lead = w.shape[:-2]
        w = w.reshape(*lead, n_k, P, w.shape[-1] // width, width)
        w = np.moveaxis(w, -2, -4)
        w = np.swapaxes(w, -3, -2)
        return np.ascontiguousarray(w).reshape(*lead, w.shape[-4], P, n_k * width)

    def columns(v):
        return np.swapaxes(v.reshape(*v.shape[:-1], -1, P), -1, -2)

    gate, up = (blocks(a[n], DK, BANK) for n in ("w_gate", "w_up"))
    down = a["w_down"].reshape(DEPTH, NE, 2, 4, P, D).swapaxes(3, 4).reshape(DEPTH, NE, 2, P, SLOT)
    experts = np.stack([gate[:, :, 0], up[:, :, 0], gate[:, :, 1], up[:, :, 1], down[:, :, 0], down[:, :, 1]],
                       axis=2)
    L = DEPTH
    w_in = a["w_in"]
    offs = np.cumsum([0, 512, 512, 512, 512, 128, 128, 512, 512, 512, 512])
    col = {n: w_in[:, :, offs[i]:offs[i + 1]] for i, n in
           enumerate(["q", "k", "v", "gq", "gk", "gv", "cb", "cc", "ch", "pool"])}
    gates = w_in[:, :, offs[-1]:].reshape(L, D, 4, 2, BANK).transpose(0, 3, 2, 1, 4)
    out = {
        "x_sample": a["x_sample"], "x_prompt": a["x_prompt"],
        "cna_k": a["cache_na_k"].reshape(L, PAST, BW), "cna_v": a["cache_na_v"].reshape(L, PAST, BW),
        "cg_k": a["cache_gqa_k"].reshape(L, PAST, P), "cg_v": a["cache_gqa_v"].reshape(L, PAST, P),
        "cond": np.stack([columns(a["c"][0]), columns(a["c_ctx"])], axis=-1),
        "small": np.concatenate([columns(a["b_ada"]),
                                 columns(a["conv_w"]).transpose(0, 2, 3, 1).reshape(L, P, 12),
                                 columns(a["conv_b"]), columns(a["pool_scale"])], axis=-1),
        "w_ada": blocks(a["w_ada"], DK, BANK),
        "w_main": np.stack([blocks(col[n], DK, BANK)[:, 0] for n in MAIN if n != "gkv"], axis=1),
        "w_gkv": blocks(np.concatenate([col["gk"], col["gv"]], axis=-1), DK, 2 * P)[:, 0],
        "w_gate_in": blocks(gates, DK, BANK).reshape(L, 8, P, SLOT),
        "w_branch": blocks(a["w_branch"], BK, BANK).transpose(0, 2, 1, 3, 4).reshape(L, 8, P, BK * BANK),
        "w_out": blocks(a["w_out"], DK, BANK),
        "bias_rows": np.pad(a["na_rpb"], ((0, 0), (0, 0), (0, 0), (QC, QC)))[:, :, ::-1, ::-1],
        "pool_w": a["pool_w"].transpose(0, 2, 1, 3),
        "w_router": a["w_router"].reshape(L, DK, P, NE).transpose(0, 2, 1, 3),
        "qk_gain": np.concatenate([a["qn_g"], a["kn_g"]], axis=-1),
        "ln_p": np.stack([a["ln1_g"], a["ln1_b"], a["ln2_g"], a["ln2_b"]], axis=1),
        "w_exp": experts,
    }
    out["bias_rows"] = np.pad(out["bias_rows"], ((0, 0), (0, 0), (0, 0), (0, 1)))
    return {k: np.ascontiguousarray(v) for k, v in out.items()}


def shape_constants():
    q = np.arange(P)
    i, keys = q // GR, np.arange(NWIN)
    mask = np.zeros((P, 3, NWIN), np.float32)
    for n, b in ((0, 0), (1, 1), (2, NB - 1)):
        start = np.clip(QC * b + i - WIN_C // 2, 0, GW - WIN_C)[:, None]
        ck = KEY_COL[b] + keys[None, :] % KC
        mask[:, n] = np.where((ck >= start) & (ck < start + WIN_C), 0.0, MASKED)
    n_freq = HD // 4
    inv = THETA ** (-np.arange(n_freq, dtype=np.float32) / n_freq)
    t = np.arange(LAT)
    rope = np.zeros((LAT, 2, 2, 2, n_freq), np.float32)
    for n, pos in enumerate((t // GW, t % GW)):
        ang = pos.astype(np.float32)[:, None] * inv.astype(np.float32)
        rope[:, 0, n] = np.cos(ang)[:, None, :]
        rope[:, 1, n] = np.sin(ang)[:, None, :]
    rope = rope.reshape(NLT, P, 2, HD).transpose(1, 0, 2, 3)
    corr = np.ones((4, 2, 8), np.float32)
    for g, win in enumerate(POOL_WINDOWS):
        n = 64
        pos = np.arange(n)
        count = np.clip(pos + win // 2, 0, n) - np.clip(pos - win // 2, 0, n)
        corr[g, 0], corr[g, 1] = win / count[:8], win / count[-8:]
    return {"ident_in": np.eye(P, dtype=np.float32), "mask_in": mask.reshape(P, 3 * NWIN),
            "rope_in": np.ascontiguousarray(rope),
            "corr_in": np.ascontiguousarray(np.broadcast_to(corr.reshape(1, 4, 16), (P, 4, 16)))}


OUTS = {"y_prompt": (1, CTX, D), "y_sample": (1, LAT, D), "st_na_k": (DEPTH, CTX, BW),
        "st_na_v": (DEPTH, CTX, BW), "st_g_k": (DEPTH, CTX, P), "st_g_v": (DEPTH, CTX, P)}


def kernel(**inputs):
    import concourse.bacc as bacc
    from concourse.bass_utils import run_bass_kernel_spmd

    arrays = {**layout(inputs), **shape_constants()}
    nc = bacc.Bacc("TRN2", target_bir_lowering=False, num_devices=1)
    args = {n: nc.dram_tensor(n, a.shape, F32, kind="ExternalInput").ap() for n, a in arrays.items()}
    for n, shape in OUTS.items():
        args[n] = nc.dram_tensor(n, shape, F32, kind="ExternalOutput").ap()
    build_program(nc, **args)
    r = run_bass_kernel_spmd(nc, [arrays], core_ids=[0]).results[0]
    return (r["y_prompt"], r["y_sample"],
            r["st_na_k"].reshape(1, DEPTH, CTX, NH, HD), r["st_na_v"].reshape(1, DEPTH, CTX, NH, HD),
            r["st_g_k"].reshape(1, DEPTH, CTX, KVH, HD), r["st_g_v"].reshape(1, DEPTH, CTX, KVH, HD))
```

```python
from contextlib import ExitStack

import numpy as np

import concourse.bass as bass
from concourse import mybir

F32 = mybir.dt.float32
F32R = mybir.dt.float32r
BF16 = mybir.dt.bfloat16
U32 = mybir.dt.uint32
ALU = mybir.AluOpType
ACT = mybir.ActivationFunctionType
AX = mybir.AxisListType

P = 128
BANK = 512
D = 1024
DK = D // P
DEPTH = 2
LAT, CTX, PAST = 512, 128, 128
TOK = LAT + CTX
NT = TOK // P
NLT = LAT // P
HT = TOK // 2
GW = 64
GR = LAT // GW
HD = 64
NH = 8
KVH = 2
BW = 512
BK = BW // P
WIN_R, WIN_C = 8, 16
NE = 16
FF = 1024
FK = FF // P
CAP_L = 2 * LAT // NE
CAP_C = 2 * CTX // NE
CAP = CAP_L + CAP_C
POOL_WINDOWS = (2, 4, 8, 16)
THETA = 10000.0
EPS = 1e-6
ALPHA = float((2 * DEPTH) ** 0.25)
QSCALE = HD ** -0.5

QC = P // GR
NB = GW // QC
KC = 32
KEY_COL = [min(max(QC * b - WIN_C // 2, 0), GW - KC) for b in range(NB)]
BIAS_W = KC + QC
BIAS_AT = [KEY_COL[b] - QC * b + QC for b in range(NB)]
NWIN = GR * KC
NA_KEYS = NWIN + PAST
MASKED = -(2.0 ** 99)
FILLERS = 5

RING = 3
SLOT = DK * BANK
ADA_SLOTS = 12
ADA_EARLY = 4
ADA_AHEAD = ADA_EARLY + 2
MAIN = ["q", "k", "v", "gq", "gkv", "pool", "cc", "ch", "cb"]
SLOTS = [("ada", i) for i in range(ADA_SLOTS)] + [(m, 0) for m in MAIN]
for _n in range(4):
    for _dc in range(2):
        SLOTS += [("gate", 4 * _dc + _n), ("wb", 4 * _dc + _n)]
SLOTS += [("wo", 0), ("wo", 1)]
PER_EXPERT = 6
EXPERTS_IN_BODY = 2
BODY_SLOTS = PER_EXPERT * EXPERTS_IN_BODY
EXP_RING = 4
HIGHS = 3
assert BODY_SLOTS % EXP_RING == 0 and BODY_SLOTS % HIGHS == 0
SPLIT_PARTS = PER_EXPERT - 1


def slot_of(key):
    s = SLOTS.index(key)
    return s % RING, len([n for n in range(ADA_AHEAD, s + 1) if n % RING == s % RING])


def ahead(k, layer):
    per_layer = len([n for n in range(ADA_AHEAD) if n % RING == k % RING])
    return layer * (16 * per_layer) + 16 * (k // RING + 1)


PROJ = [(m, f) for m in MAIN for f in range(2 if m == "gkv" else BK)]
NPROJ = len(PROJ)
PRODUCTS = list(PROJ)
for _g in range(4 * DK):
    PRODUCTS += [("L", _g), ("B", _g)]
PRODUCT_NO = {key: n for n, key in enumerate(PRODUCTS)}
STEP_PRODUCTS = [[18], [19, 20], [21], [22, 23], [24], [25]]
assert PROJ[18] == ("pool", 0) and PROJ[25] == ("cc", BK - 1)


def merge_unit(g):
    return g // 8, g // 4 % 2, g % 8


def slot_key(key):
    kind, g = key
    if kind in ("L", "B"):
        n, dc, _ = merge_unit(g)
        return ("gate" if kind == "L" else "wb"), 4 * dc + n
    return kind, 0


ATT = [(kind, b, h) for kind in ("na", "gqa") for b in range(NB + 1) for h in range(NH)]
NATT = len(ATT)
NBLK = NATT // NH
NA_UNITS = NATT // 2


def units_to_score(step):
    return [u for u in range(NATT) if max(u - (3 if u < NA_UNITS else 2), -1) == step]


def build_program(nc, x_sample, x_prompt, cna_k, cna_v, cg_k, cg_v, cond, small, w_ada, w_main, w_gkv,
                  w_ada_ahead, w_gate_in, w_branch, w_out, bias_rows, pool_w, w_router, qk_gain, ln_p, w_exp,
                  ident_in, mask_in, rope_in, corr_in,
                  y_prompt, y_sample, st_na_k, st_na_v, st_g_k, st_g_v):
    with ExitStack() as ctx:
        def sb(name, shape, dt=F32):
            return ctx.enter_context(nc.sbuf_tensor(name, shape, dt))

        def sem(name):
            return ctx.enter_context(nc.semaphore(name))

        def sb_twice(name, shape):
            with nc.sbuf_tensor(name, shape, F32) as plain:
                pass
            return plain, sb(name + "_r", shape, F32R)

        ring, ring_r = sb_twice("ring", [P, RING, SLOT])
        hT, hT_r = sb_twice("hT", [P, DK, TOK])
        h_high = sb("h_high", [P, DK, TOK], F32R)
        br, br_r = sb_twice("br", [P, 4, BK, TOK])
        shared, shared_r = sb_twice("shared", [P, 13568])
        work, work_r = sb_twice("work", [P, 4224])
        ident = sb("ident", [P, P])
        ident_b = sb("ident_b", [P, P], BF16)
        mask_f = work[:, 0:3 * NWIN]
        mask_b = sb("mask_b", [P, 3, NWIN], BF16)
        rope = sb("rope", [P, NLT, 2, HD])
        corr = sb("corr", [P, 4, 16])
        eps = sb("eps", [P, 1])
        cvec = sb("cvec", [P, DK, 2])
        smallp = sb("smallp", [P, 68])
        mod = sb("mod", [P, 2, 48])
        router = sb("router", [P, DK, NE])
        negmax = sb("negmax", [P, NATT])
        sums = sb("sums", [P, NATT])
        qk_ss = sb("qk_ss", [P, NT, 10])
        qk_std = sb("qk_std", [P, NT, 10])
        qk_rstd = sb("qk_rstd", [P, NT, 10])
        grow = sb("grow", [32, P])
        stats = sb("stats", [P, 2, NT, 12])
        mv = sb("mv", [P, 2, NT, 2])
        std = sb("std", [P, 2, NT])
        rstd = sb("rstd", [P, 2, NT])
        lg = sb("lg", [P, NT, 4 + NE])
        gate_cols = lg[:, :, :].rearrange("p a b -> p (a b)")[:, 0:32]
        aff = sb("aff", [P, NT, NE])
        rsum = aff[:, :, :].rearrange("p a b -> p (a b)")[:, 0:NATT]
        vals = sb("vals", [NE, CAP])
        idx_u = sb("idx_u", [NE, CAP], U32)
        idx_f = sb("idx_f", [NE, CAP])
        idx_t = sb("idx_t", [CAP, NE + 1], U32)
        g_t = sb("g_t", [CAP, NE + 1])
        idx_cur = sb("idx_cur", [CAP, 2], U32)
        g_cur = sb("g_cur", [CAP, 2])

        class Carve:
            def __init__(self, arena, size):
                self.arena, self.size, self.at = arena, size, 0

            def take(self, *dims):
                n = int(np.prod(dims))
                a = self.arena[:, self.at:self.at + n]
                self.at += n
                assert self.at <= self.size, (self.at, self.size)
                if len(dims) == 2:
                    a = a.rearrange("p (a b) -> p a b", a=dims[0])
                if len(dims) == 3:
                    a = a.rearrange("p (a b c) -> p a b c", a=dims[0], b=dims[1])
                return a

        c = Carve(shared, 13568)
        na_kT = c.take(BK, TOK + PAST)
        bias_at = c.at
        bias = c.take(NH, GR, BIAS_W)
        vwin_at = c.at
        vwin = c.take(2 * NB, BW)
        vcache = c.take(BW)
        vctx = c.take(BW)
        gkT = c.take(KVH, TOK + PAST)
        gv = c.take(NT + 1, P)
        na_cached, g_cached = vwin[:, 0, :], vwin[:, 1, 0:P]
        gain = vwin[:, 1, P:2 * P].rearrange("p (a b) -> p a b", a=2)
        poolw = vwin[:, 2, :].rearrange("p (a b) -> p a b", a=4)
        high_at = vwin_at + 4 * BW
        gq_raw = shared[:, bias_at:bias_at + BK * TOK].rearrange("p (a b) -> p a b", a=BK)
        PW = 8 + LAT + 8 + 8 + CTX + 8
        pu = [work[:, 1536 + i * PW:1536 + (i + 1) * PW] for i in range(3)]
        c = Carve(shared, 13568)
        merged = c.take(DK, TOK)
        sg = c.take(2, TOK)
        prod = c.take(2, TOK)
        br_high_at = c.at
        c.take(BK, TOK)
        br_high = shared_r[:, br_high_at:c.at].rearrange("p (a b) -> p a b", a=BK)
        lnb = shared[:, c.at:c.at + D]
        L_high_at = c.at
        assert L_high_at == vwin_at + 2 * NB * BW
        c.take(DK * P)
        gate1 = c.take(2, D)
        affT = sg.rearrange("p a b -> p (a b)")[0:NE, 0:TOK]
        lng = prod.rearrange("p a b -> p (a b)")[:, 0:D]
        xsT, xsT_r = (a[:, br_high_at:br_high_at + 2 * DK * CAP].rearrange("p (a b) -> p a b", a=2)
                      for a in (shared, shared_r))
        xs_high = shared_r[:, br_high_at + 2 * DK * CAP:br_high_at + 4 * DK * CAP].rearrange("p (a b) -> p a b", a=2)
        m = Carve(shared, DK * TOK)
        act_s = m.take(FF)[0:CAP, :]
        hdn = m.take(FF)[0:CAP, :]
        hdnT = m.take(FK // 2 * CAP)
        hid_at = m.at
        m.take(FK * CAP)
        hid_high, hid_low = (shared_r[:, hid_at + i * FK // 2 * CAP:hid_at + (i + 1) * FK // 2 * CAP] for i in range(2))
        gate2 = m.take(D)[0:CAP, :]

        c = Carve(work, 4224)
        gtok = c.take(2, 768)
        t1 = c.take(640)
        t2 = c.take(640)
        kdup = c.take(2, 2 * P)
        c = Carve(work, 4224)
        probs = c.take(3, 640)
        pT = c.take(2, 640)
        otok = c.take(2, BW)
        conv_y = work[:, 3200:3200 + TOK]
        L_high = [shared_r[:, L_high_at:L_high_at + DK * P], work_r[:, 640:640 + DK * P]]
        B_high = [work_r[:, 1664 + i * BK * P:1664 + (i + 1) * BK * P] for i in range(2)]
        adarow = work[0:2, 0:2 * BANK].rearrange("p (a b) -> p a b", a=2)
        k_state = work[:, 0:BW]

        qT = br[:, 0]
        gqT = br[:, 1]
        vT = br[:, 1]
        kv_slot = SLOTS.index(("gkv", 0)) % RING
        kv_raw = ring[:, kv_slot, SLOT // 2:SLOT // 2 + 2 * TOK].rearrange("p (a b) -> p a b", a=2)
        vstage = br[:, 3].rearrange("p a b -> p (a b)")[:, 0:NLT * BW].rearrange("p (t n) -> p t n", t=NLT)
        brf = br[:, :, :, :].rearrange("p a b c -> p (a b c)")
        xstage = brf[:, 0:NT * D].rearrange("p (a b) -> p a b", a=NT)
        zt = brf[:, 0:2048].rearrange("p (a b) -> p a b", a=2)
        x1 = brf[:, 2048:4096].rearrange("p (a b) -> p a b", a=2)
        xa = brf[:, 4096:6144].rearrange("p (a b) -> p a b", a=2)
        xin = brf[:, 6144:8192].rearrange("p (a b) -> p a b", a=2)
        z2 = brf[:, 0:NT * D].rearrange("p (a b) -> p a b", a=NT)
        xmT = brf[:, 8192:10240].rearrange("p (a b c) -> p a b c", a=2, b=DK)
        hf = hT[:, :, :].rearrange("p a b -> p (a b)")
        xs = hf[0:CAP, 0:2048].rearrange("p (a b) -> p a b", a=2)
        ye = hf[0:CAP, 2048:4096].rearrange("p (a b) -> p a b", a=2)
        brf_r = br_r[:, :, :, :].rearrange("p a b c -> p (a b c)")
        exp_slot = [ring[:, r, :] for r in range(RING)] + [work[:, 0:SLOT]]
        exp_slot_r = [ring_r[:, r, :] for r in range(RING)] + [work_r[:, 0:SLOT]]
        exp_high = [h_high[:, :, :].rearrange("p a b -> p (a b)")[:, 0:SLOT], brf_r[:, 0:SLOT], brf_r[:, SLOT:2 * SLOT]]

        acc = [ctx.enter_context(nc.psum_tensor(f"acc{i}", [P, 2, BANK], F32)) for i in range(4)]
        accf = [a[:, :, :].rearrange("p a b -> p (a b)") for a in acc]
        o_bank, ot_bank = acc[3][:, 0, :], acc[3][:, 1, :]

        v_scr = nc.dram_tensor("v_scr", [LAT, BW], F32, kind="Internal").ap()
        gate_scr = nc.dram_tensor("gate_scr", [32, P], F32, kind="Internal").ap()
        x1_scr = nc.dram_tensor("x1_scr", [TOK, D], F32, kind="Internal").ap()
        y_acc = nc.dram_tensor("y_acc", [TOK, D], F32, kind="Internal").ap()

        def out_rows(t):
            return y_sample[0, t * P:(t + 1) * P, :] if t < NLT else y_prompt[0, :, :]

        def bc(ap, *dims):
            return bass.AP(ap.tensor, ap.offset, [list(ap.ap[0])] + [list(d) for d in dims])

        consts_in = sem("consts_in")
        x_copied = sem("x_copied")
        const_ready = sem("const_ready")
        gather_done = sem("gather_done")
        scatter_done = sem("scatter_done")
        ada_ahead = [sem(f"ada_ahead{r}") for r in range(RING)]
        first_done, first_copied, first_turned = sem("first_done"), sem("first_copied"), sem("first_turned")
        cond_in = sem("cond_in")
        cond_ready = sem("cond_ready")
        cleared_from = sem("cleared_from")
        slot_full = [sem(f"slot_full{r}") for r in range(RING)]
        x_in = sem("x_in")
        exp_full = [sem(f"exp_full{r}") for r in range(EXP_RING)]
        exp_high_ready = sem("exp_high_ready")
        exp_ready = sem("exp_ready")
        hid_low_ready = sem("hid_low_ready")
        xin_in = [sem(f"xin_in{i}") for i in range(2)]
        x1_out = [sem(f"x1_out{i}") for i in range(2)]
        zin_in = [sem(f"zin_in{t}") for t in range(NT)]
        x2_out = sem("x2_out")
        small_in = sem("small_in")
        param_in = sem("param_in")
        early_done, early_copied, early_turned = sem("early_done"), sem("early_copied"), sem("early_turned")
        ada_done = sem("ada_done")
        ada_copied = sem("ada_copied")
        mod_full = sem("mod_full")
        xt_full = sem("xt_full")
        xt_copied = sem("xt_copied")
        mod_ready = sem("mod_ready")
        h_whole = sem("h_whole")
        h_high_ready = sem("h_high_ready")
        h_ready = sem("h_ready")
        w_high_ready = sem("w_high_ready")
        w_ready = sem("w_ready")
        product_done = sem("product_done")
        vraw_copied = sem("vraw_copied")
        graw_copied = sem("graw_copied")
        pool_copied = sem("pool_copied")
        br_high_ready = sem("br_high_ready")
        br_ready = sem("br_ready")
        gateT_full = sem("gateT_full")
        gateT_copied = sem("gateT_copied")
        gate_out = sem("gate_out")
        gate1_in = sem("gate1_in")
        ln1_in = sem("ln1_in")
        q_copied = sem("q_copied")
        k_copied = sem("k_copied")
        kcache_in = sem("kcache_in")
        kc_full = sem("kc_full")
        kc_copied = sem("kc_copied")
        ks_full = sem("ks_full")
        ks_copied = sem("ks_copied")
        v_full = sem("v_full")
        v_copied = sem("v_copied")
        vscr_out = sem("vscr_out")
        vwin_in = [sem(f"vwin_in{i}") for i in range(2)]
        cachev_in = sem("cachev_in")
        state_out = sem("state_out")
        g_full = sem("g_full")
        g_copied = sem("g_copied")
        ss_ready = sem("ss_ready")
        std_ready = sem("std_ready")
        gtok_ready = sem("gtok_ready")
        gt_full = sem("gt_full")
        gt_copied = sem("gt_copied")
        gc_dup = sem("gc_dup")
        gc_full = sem("gc_full")
        gc_copied = sem("gc_copied")
        pool_ready = sem("pool_ready")
        mix_full = sem("mix_full")
        mix_copied = sem("mix_copied")
        c_copied = sem("c_copied")
        u_ready = sem("u_ready")
        conv_ready = sem("conv_ready")
        bias_in = sem("bias_in")
        scores_full = sem("scores_full")
        rowmax_ready = sem("rowmax_ready")
        probs_ready = sem("probs_ready")
        pt_full = sem("pt_full")
        pt_copied_act = sem("pt_copied_act")
        pt_copied_dve = sem("pt_copied_dve")
        pv_done = sem("pv_done")
        o_copied = sem("o_copied")
        ot_full = sem("ot_full")
        ot_copied = sem("ot_copied")
        sig_ready = sem("sig_ready")
        merged_add = sem("merged_add")
        prod_done = sem("prod_done")
        y_full = sem("y_full")
        z_free = sem("z_free")
        var_ready = sem("var_ready")
        std1_ready = sem("std1_ready")
        x1_ready = sem("x1_ready")
        xa_ready = sem("xa_ready")
        x1T_full = sem("x1T_full")
        xmT_ready = sem("xmT_ready")
        r_full = sem("r_full")
        negl_ready = sem("negl_ready")
        el_ready = sem("el_ready")
        aff_ready = sem("aff_ready")
        affT_full = sem("affT_full")
        affT_copied = sem("affT_copied")
        topk_ready = sem("topk_ready")
        sel_full = sem("sel_full")
        sel_ready = sem("sel_ready")
        sel_cur = sem("sel_cur")
        xT_full = sem("xT_full")
        xsT_ready = sem("xsT_ready")
        gate0_done = sem("gate0_done")
        up0_done = sem("up0_done")
        gate1_done = sem("gate1_done")
        up1_done = sem("up1_done")
        down0_done = sem("down0_done")
        down1_done = sem("down1_done")
        silu_done = sem("silu_done")
        hidden_ready = sem("hidden_ready")
        hT_full = sem("hT_full")
        hT_copied = sem("hT_copied")
        gate2_in = sem("gate2_in")
        ye_ready = sem("ye_ready")
        ye_free = sem("ye_free")
        ln2_in = sem("ln2_in")
        var2_ready = sem("var2_ready")
        std2_ready = sem("std2_ready")
        x2_ready = sem("x2_ready")
        dve_step = sem("dve_step")
        dve_loop = sem("dve_loop")
        pool_turn = sem("pool_turn")
        blocks_in = sem("blocks_in")
        cleared_to = sem("cleared_to")


        plan, freed_by = [], {}

        def unit(key, semaphore, count):
            freed_by[key] = (semaphore, count)
            plan.append(key)

        for i in range(ADA_EARLY, ADA_SLOTS):
            unit(("ada", i), ada_copied, i - ADA_EARLY + 1)
            if i == ADA_EARLY + 1:
                for t in range(NT):
                    unit(("xt", t), xt_copied, t + 1)
        for f in range(BK):
            unit(("q", f), q_copied, 3 * f + 3)
        unit(("gateT",), gateT_copied, 1)
        for f in range(BK):
            unit(("k", f), k_copied, f + 1)
        for f in range(BK):
            unit(("v", f), vraw_copied, f + 1)
            if f == 0:
                unit(("kc",), kc_copied, 1)
                unit(("ks",), ks_copied, 1)
        for f in range(BK):
            unit(("gq", f), graw_copied, f + 1)
            if f == 0:
                for t in range(NT):
                    unit(("vt", t), v_copied, t + 1)
        for f in range(2):
            unit(("gkv", f), graw_copied, BK + f + 1)
        for t in range(NT + 1):
            if t < NT:
                unit(("g", t), g_copied, 2 * t + 2)
            for n in STEP_PRODUCTS[t]:
                kind, f = PROJ[n]
                unit(PROJ[n], pool_copied if kind == "pool" else c_copied, f + 1)
            if t >= 1:
                unit(("gt", t - 1), gt_copied, 2 * (t - 1) + 2)
        unit(("gc",), gc_copied, 1)
        for f in range(BK):
            unit(("ch", f), u_ready, f + 1)
            unit(("mix", f), mix_copied, f + 1)
        for f in range(BK):
            unit(("cb", f), conv_ready, f + 1)
        AFTER_ATT = len(plan)
        for g in range(4 * DK):
            unit(("L", g), sig_ready, g + 1)
            unit(("B", g), prod_done, g + 1)
        for t in range(NT + 2):
            if t < NT:
                unit(("y", t), z_free, t + 1)
            if t >= 2:
                unit(("affT", t - 2), affT_copied, t - 1)
            if 1 <= t < NT + 1:
                unit(("x1T", t - 1), xmT_ready, DK * t)
                unit(("r", t - 1), el_ready, t)
        unit(("sel",), sel_ready, 2)
        at = {key: n for n, key in enumerate(plan)}

        place = [n % 3 if n < AFTER_ATT else (n - AFTER_ATT) % 3 for n in range(len(plan))]
        place[at["cb", 2]], place[at["cb", 3]] = 2, 3
        for key, n in at.items():
            if key[0] in ("y", "x1T", "r", "affT"):
                place[n] = {"y": key[1] % 2, "x1T": 2, "r": 3, "affT": 3}[key[0]]

        def last_user(n):
            first = 0 if n < AFTER_ATT else AFTER_ATT
            users = [i for i in range(first, n) if place[i] == place[n]]
            return users[-1] if users else None

        def pair(key):
            return place[at[key]]

        def scores_at(a):
            return accf[(a % 4) // 2][:, (a % 2) * BANK:] if a < NA_UNITS else accf[a % 2]

        def turned_at(a):
            return acc[2][:, a % 2, :] if a < NA_UNITS else accf[2]

        def out_at(block):
            return acc[3][:, block % 2, :]

        def turned_free(a):
            return (pt_copied_act, a + 1) if a < NA_UNITS else (pt_copied_dve, a - NA_UNITS + 1)

        def halves(key):
            return acc[pair(key)][:, :, 0:HT]

        def by_half(a):
            return a.rearrange("p (a b) -> p a b", a=2)

        def released(key):
            kind, n = key
            if kind == "ada":
                return ada_done, n - ADA_EARLY + 1
            if kind == "wo":
                return y_full, NT
            if kind == "gkv":
                return g_full, NT
            return product_done, max(PRODUCT_NO[p] for p in PRODUCTS if slot_key(p) == key) + 1

        def done(n):
            return product_done, n + 1

        def weight_tile(n):
            kind, f = PRODUCTS[n]
            r, _ = slot_of(slot_key(PRODUCTS[n]))
            n_k = BK if kind == "B" else DK
            width = 2 * P if kind == "gkv" else BANK
            col = (f % 4) * P
            if n < NPROJ:
                high = shared_r[:, high_at + (n % 2) * DK * P:high_at + (n % 2 + 1) * DK * P]
            else:
                high = (B_high if kind == "B" else L_high)[f % 2]
            whole, low = (a[:, r, 0:n_k * width].rearrange("p (k n) -> p k n", k=n_k)[:, :, col:col + P]
                          for a in (ring, ring_r))
            return whole, low, high.rearrange("p (k n) -> p k n", k=n_k)

        def splits(i, n):
            return i * (SPLIT_PARTS * EXPERTS_IN_BODY) + (n // PER_EXPERT * SPLIT_PARTS + n % PER_EXPERT + 1)

        def arrivals(i, n):
            return i * (16 * BODY_SLOTS // EXP_RING) + 16 * (n // EXP_RING + 1)

        def multiplied(i, n):
            part = n % PER_EXPERT
            return part_done[part], i * EXPERTS_IN_BODY + (n // PER_EXPERT + 1 + (part == PER_EXPERT - 1))

        part_done = [gate0_done, up0_done, gate1_done, up1_done, down0_done, down1_done]

        def key_tiles(a):
            kind, b, _ = ATT[a]
            return 1 if b == NB else (NA_KEYS if kind == "na" else LAT + PAST) // P

        def value_tile(a, j):
            kind, b, h = ATT[a]
            if kind == "na":
                cols = slice(h * HD, (h + 1) * HD)
                return vctx[:, cols] if b == NB else vwin[:, 2 * b + j, cols] if j < 2 else vcache[:, cols]
            g = h // (NH // KVH)
            tile = NT - 1 if b == NB else j if j < NLT else NT
            return gv[:, tile, g * HD:(g + 1) * HD]

        def bias_of(h, b):
            last = bias[:, h, GR - 1, BIAS_W - 1 - BIAS_AT[b]:BIAS_W - BIAS_AT[b]]
            return bc(last, (-BIAS_W, GR), (-1, KC))

        def group_cols(g):
            return slice(0, LAT) if g == 0 else slice(LAT, TOK)

        def ada_product(out, i):
            for k in range(DK):
                mm = nc.tensor.matmul(out[0:2, 0:BANK], cvec[:, k, :], ring[:, i % RING, k * BANK:(k + 1) * BANK],
                                      start=(k == 0), stop=(k == DK - 1))
            return mm

        def ada_turn(i):
            for j in range(4):
                c0 = 2 * (4 * i + j)
                mm = nc.tensor.transpose((o_bank if i < 4 else ot_bank)[:, c0:c0 + 2], adarow[:, i % 2, j * P:(j + 1) * P],
                                         ident[0:2, 0:2])
            return mm

        def early_loads(sp, layer, done_sem, first=0):
            for k in range(first, ADA_AHEAD):
                if k >= RING:
                    sp.wait_ge(done_sem, k - RING + 1)
                sp.dma_start(ring[:, k % RING, :], w_ada_ahead[layer, k]).then_inc(ada_ahead[k % RING], 16)

        def early_products(pe, layer, done_sem, copied, turned):
            for i in range(ADA_EARLY):
                pe.wait_ge(ada_ahead[i % RING], ahead(i, layer))
                if i >= 2:
                    pe.wait_ge(copied, i - 1)
                ada_product(accf[i % 2], i).then_inc(done_sem, 1)
                if i:
                    pe.wait_ge(copied, i)
                    ada_turn(i - 1).then_inc(turned, 1)
            pe.wait_ge(copied, ADA_EARLY)
            ada_turn(ADA_EARLY - 1).then_inc(turned, 1)

        def early_rows(act, done_sem, copied, turned):
            for i in range(ADA_EARLY):
                act.wait_ge(done_sem, i + 1)
                if i >= 2:
                    act.wait_ge(turned, i - 1)
                nc.scalar.activation(adarow[:, i % 2, :], accf[i % 2][0:2, 0:BANK], ACT.Copy).then_inc(copied, 1)

        with nc.Block() as block:
            @block.sync
            def _(sp):
                sp.dma_start(cvec[:], cond).then_inc(cond_in, 16)
                sp.dma_start(ring[:, 0, :], w_ada_ahead[0, 0]).then_inc(ada_ahead[0], 16)
                sp.dma_start(y_sample[0], x_sample[0]).then_inc(x_copied, 16)
                sp.dma_start(y_prompt[0], x_prompt[0]).then_inc(x_copied, 16)
                sp.dma_start(ident[:], ident_in).then_inc(consts_in, 16)
                sp.dma_start(mask_f, mask_in).then_inc(consts_in, 16)
                sp.dma_start(rope[:], rope_in).then_inc(consts_in, 16)
                sp.dma_start(corr[:], corr_in).then_inc(consts_in, 16)
                early_loads(sp, 0, first_done, first=1)
                sp.wait_ge(x_copied, 32)

            @block.tensor
            def _(pe):
                pe.wait_ge(cond_ready, 1)
                pe.wait_ge(consts_in, 64)
                early_products(pe, 0, first_done, first_copied, first_turned)

            @block.scalar
            def _(act):
                act.wait_ge(cond_in, 16)
                nc.scalar.activation(cvec[:], cvec[:], ACT.Silu).then_inc(cond_ready, 1)
                act.wait_ge(cond_ready, 1)
                act.wait_ge(const_ready, 3)
                early_rows(act, first_done, first_copied, first_turned)

            @block.vector
            def _(dve):
                nc.vector.memset(eps[:], EPS).then_inc(const_ready, 1)
                dve.wait_ge(consts_in, 64)
                nc.vector.tensor_copy(ident_b[:], ident[:]).then_inc(const_ready, 1)
                nc.vector.tensor_copy(mask_b[:].rearrange("p a b -> p (a b)"), mask_f).then_inc(const_ready, 1)
                dve.wait_ge(const_ready, 3)

        with nc.Fori(0, DEPTH) as layer:
            with nc.Block() as block:

                @block.sync
                def _(sp):
                    src = {"ada": lambda i: w_ada[layer, i], "gkv": lambda i: w_gkv[layer],
                           "gate": lambda i: w_gate_in[layer, i], "wb": lambda i: w_branch[layer, i],
                           "wo": lambda i: w_out[layer, i]}
                    for i, mname in enumerate(n for n in MAIN if n != "gkv"):
                        src[mname] = lambda _, i=i: w_main[layer, i]
                    sp.dma_start(xstage[:, 0:NLT, :], y_sample[0].rearrange("(t p) n -> p t n", p=P))\
                        .then_inc(x_in, 16)
                    sp.dma_start(xstage[:, NLT, :], y_prompt[0]).then_inc(x_in, 16)
                    sp.dma_start(smallp[:], small[layer]).then_inc(small_in, 16)
                    for n, key in enumerate(SLOTS):
                        r, _ = slot_of(key)
                        a = src[key[0]](key[1])
                        if n >= ADA_AHEAD:
                            if n - RING >= ADA_EARLY:
                                sp.wait_ge(*released(SLOTS[n - RING]))
                            sp.dma_start(ring[:, r, 0:a.shape[1]], a).then_inc(slot_full[r], 16)
                        if key == ("cb", 0):
                            sp.wait_ge(g_full, NT)
                            for row in range(GR):
                                for rr in range(GR):
                                    a = bias_rows[layer]
                                    sp.dma_start(bias[row:P:GR, :, rr, :],
                                                 bass.AP(a.tensor, a.offset + (row + rr) * 64,
                                                         [[1, QC], [15 * 64, NH], [1, BIAS_W]])).then_inc(bias_in, 16)
                        if n == ADA_AHEAD:
                            sp.dma_start(na_cached, cna_k[layer]).then_inc(kcache_in, 16)
                            sp.dma_start(vcache, cna_v[layer]).then_inc(cachev_in, 16)
                            sp.dma_start(g_cached, cg_k[layer]).then_inc(kcache_in, 16)
                            sp.dma_start(gv[:, NT, :], cg_v[layer]).then_inc(cachev_in, 16)
                            sp.dma_start(gain.rearrange("p a b -> p (a b)"),
                                         bass.AP(qk_gain.tensor, qk_gain[layer].offset,
                                                 [[0, P], [1, 2 * HD]])).then_inc(param_in, 16)
                            sp.dma_start(poolw, pool_w[layer]).then_inc(param_in, 16)
                            sp.dma_start(router[:], w_router[layer]).then_inc(param_in, 16)
                    for n in range(EXP_RING):
                        if n < RING:
                            sp.wait_ge(*released([key for key in SLOTS if slot_of(key)[0] == n][-1]))
                        else:
                            sp.wait_ge(*done(len(PRODUCTS) - 1))
                        sp.dma_start(exp_slot[n], w_exp[layer, 0, n]).then_inc(exp_full[n], 16)

                    def refill(i, n):
                        ahead = n + EXP_RING
                        sp.wait_ge(*multiplied(i, n))
                        sp.dma_start(exp_slot[n % EXP_RING],
                                     w_exp[layer, i * EXPERTS_IN_BODY + ahead // PER_EXPERT, ahead % PER_EXPERT])\
                            .then_inc(exp_full[n % EXP_RING], 16)

                    last = NE // EXPERTS_IN_BODY - 1
                    with sp.Fori(0, last) as i:
                        for n in range(BODY_SLOTS):
                            refill(i, n)
                    for n in range(BODY_SLOTS - EXP_RING):
                        refill(last, n)
                    for k in range(RING):
                        sp.wait_ge(*multiplied(last, BODY_SLOTS - EXP_RING + k))
                        sp.dma_start(ring[:, k, :], w_ada_ahead[layer + 1, k]).then_inc(ada_ahead[k], 16)
                    early_loads(sp, layer + 1, early_done, first=RING)
                    for k in range(ADA_AHEAD - RING, ADA_AHEAD):
                        sp.wait_ge(ada_ahead[k % RING], ahead(k, layer + 1))
                    sp.sem_inc(blocks_in, 1)

                @block.tensor
                def _(pe):
                    def acquire(key):
                        n = last_user(at[key])
                        if n is not None:
                            pe.wait_ge(*freed_by[plan[n]])
                        return accf[pair(key)]

                    def arrived(key):
                        r, use = slot_of(key)
                        pe.wait_ge(slot_full[r], 16 * use)
                        return ring[:, r, :]

                    def h_cols(k, half):
                        cols = slice(half * HT, (half + 1) * HT)
                        return h_high[:, k, cols], hT_r[:, k, cols]

                    def product(key, rhs, groups=((0, HT), (BANK, HT))):
                        n = PRODUCT_NO[key]
                        pe.wait_ge(w_ready, n + 1)
                        out = acquire(key)
                        _, low, high = weight_tile(n)
                        n_k = low.shape[1]
                        for i, (at0, count) in enumerate(groups):
                            o = out[:, at0:at0 + count]
                            for k in range(n_k):
                                x_high, x_low = rhs(k, i)
                                nc.tensor.matmul(o, high[:, k, :], x_high, start=(k == 0), stop=False)
                                nc.tensor.matmul(o, high[:, k, :], x_low, start=False, stop=False)
                                mm = nc.tensor.matmul(o, low[:, k, :], x_high, start=False, stop=(k == n_k - 1))
                        mm.then_inc(product_done, 1)

                    def turn_input():
                        pe.wait_ge(x_in, 32)
                        for t in range(NT):
                            out = acquire(("xt", t))
                            for k in range(DK):
                                mm = nc.tensor.transpose(out[:, k * P:(k + 1) * P], xstage[:, t, k * P:(k + 1) * P],
                                                         ident[:])
                            mm.then_inc(xt_full, 1)

                    def turn_ada(i):
                        pe.wait_ge(ada_copied, i - ADA_EARLY + 1)
                        ada_turn(i).then_inc(mod_full, 1)

                    for i in range(ADA_EARLY, ADA_SLOTS):
                        if i < ADA_AHEAD:
                            pe.wait_ge(ada_ahead[i % RING], ahead(i, layer))
                        else:
                            arrived(("ada", i))
                        ada_product(acquire(("ada", i)), i).then_inc(ada_done, 1)
                        if i > ADA_EARLY:
                            turn_ada(i - 1)
                        if i == ADA_EARLY + 1:
                            turn_input()
                    turn_ada(ADA_SLOTS - 1)
                    pe.wait_ge(h_ready, DK)
                    for f in range(BK):
                        product(("q", f), h_cols)
                    pe.wait_ge(mod_ready, 2)
                    out = acquire(("gateT",))
                    nc.tensor.transpose(out[0:32, 0:P], gate_cols, ident[:]).then_inc(gateT_full, 1)
                    for f in range(BK):
                        product(("k", f), h_cols)
                    for f in range(BK):
                        product(("v", f), h_cols)
                        if f == 0:
                            pe.wait_ge(kcache_in, 32)
                            out = acquire(("kc",))
                            for i in range(BK):
                                mm = nc.tensor.transpose(out[:, i * P:(i + 1) * P], na_cached[:, i * P:(i + 1) * P],
                                                         ident[:])
                            mm.then_inc(kc_full, 1)
                            pe.wait_ge(k_copied, BK)
                            out = acquire(("ks",))
                            for i in range(BK):
                                mm = nc.tensor.transpose(out[:, i * P:(i + 1) * P], na_kT[:, i, LAT:TOK], ident[:])
                            mm.then_inc(ks_full, 1)
                    for f in range(BK):
                        product(("gq", f), h_cols)
                        if f == 0:
                            pe.wait_ge(vraw_copied, BK)
                            for t in range(NT):
                                out = acquire(("vt", t))
                                for i in range(BK):
                                    mm = nc.tensor.transpose(out[:, i * P:(i + 1) * P], vT[:, i, t * P:(t + 1) * P],
                                                             ident[:])
                                mm.then_inc(v_full, 1)
                    for f in range(2):
                        product(("gkv", f), h_cols)

                    pe.wait_ge(graw_copied, BK + 2)
                    for t in range(NT + 1):
                        if t < NT:
                            out = acquire(("g", t))
                            for f in range(BK + 2):
                                src = gq_raw[:, f, :] if f < BK else kv_raw[:, f - BK, :]
                                mm = nc.tensor.transpose(out[:, f * P:(f + 1) * P], src[:, t * P:(t + 1) * P], ident[:])
                            mm.then_inc(g_full, 1)
                        for n in STEP_PRODUCTS[t]:
                            product(PROJ[n], h_cols)
                        if t >= 1:
                            pe.wait_ge(gtok_ready, t)
                            out = acquire(("gt", t - 1))
                            for f in range(BK):
                                nc.tensor.transpose(out[:, f * P:(f + 1) * P],
                                                    gtok[:, (t - 1) % 2, f * P:(f + 1) * P], ident[:])
                            for g in range(KVH):
                                mm = nc.tensor.transpose(out[:, BW + g * P:BW + (g + 1) * P],
                                                         kdup[:, (t - 1) % 2, g * P:(g + 1) * P], ident[:])
                            mm.then_inc(gt_full, 1)
                    pe.wait_ge(gc_dup, 1)
                    out = acquire(("gc",))
                    for g in range(KVH):
                        mm = nc.tensor.transpose(out[:, g * P:(g + 1) * P], kdup[:, NT % 2, g * P:(g + 1) * P], ident[:])
                    mm.then_inc(gc_full, 1)

                    pe.wait_ge(param_in, 48)
                    for f in range(4):
                        product(("ch", f), h_cols)
                        pe.wait_ge(pool_ready, f + 1)
                        out = acquire(("mix", f))
                        for g, (lo, hi) in enumerate(((0, LAT), (LAT, TOK))):
                            mm = nc.tensor.matmul(out[:, lo:hi], poolw[:, f, :], br[:, 3, f, lo:hi],
                                                  start=True, stop=True)
                        mm.then_inc(mix_full, 1)
                    for f in range(BK - 1):
                        product(("cb", f), h_cols)

                    def scores(a):
                        kind, b, h = ATT[a]
                        if a < NA_UNITS:
                            if a >= 4:
                                pe.wait_ge(probs_ready, a - 3)
                        else:
                            pe.wait_ge(probs_ready, a - 1)
                        out = scores_at(a)
                        half = slice(HD * (h % 2), HD * (h % 2) + HD)
                        q = (qT if kind == "na" else gqT)[half, h // 2, b * P:(b + 1) * P]
                        if kind == "na":
                            kt = na_kT[half, h // 2, :]
                            if b < NB:
                                win = kt[:, 0:LAT].rearrange("p (r c) -> p r c", c=GW)[:, :, KEY_COL[b]:KEY_COL[b] + KC]
                                nc.tensor.matmul(out[:, 0:NWIN], q, win, start=True, stop=False)
                                nc.tensor.matmul(out[:, 0:NWIN], ident_b[:], mask_b[:, (0, 1, 1, 2)[b], :],
                                                 start=False, stop=True)
                                mm = nc.tensor.matmul(out[:, NWIN:NA_KEYS], q, kt[:, TOK:TOK + PAST],
                                                      start=True, stop=True)
                            else:
                                mm = nc.tensor.matmul(out[:, 0:CTX], q, kt[:, LAT:TOK], start=True, stop=True)
                        else:
                            kt = gkT[half, h // (NH // KVH), :]
                            if b < NB:
                                nc.tensor.matmul(out[:, 0:LAT], q, kt[:, 0:LAT], start=True, stop=True)
                                mm = nc.tensor.matmul(out[:, LAT:LAT + PAST], q, kt[:, TOK:TOK + PAST],
                                                      start=True, stop=True)
                            else:
                                mm = nc.tensor.matmul(out[:, 0:CTX], q, kt[:, LAT:TOK], start=True, stop=True)
                        mm.then_inc(scores_full, 1)

                    def turn_probs(a):
                        if a >= 2:
                            pe.wait_ge(*turned_free(a - 2 if a < NA_UNITS else a - 1))
                        out = turned_at(a)
                        if key_tiles(a) == 1:
                            for _ in range(FILLERS):
                                nc.tensor.matmul(out[:, P:P + NWIN], ident_b[:], mask_b[:, 0, :], start=True, stop=True)
                        pe.wait_ge(probs_ready, a + 1)
                        for j in range(key_tiles(a)):
                            mm = nc.tensor.transpose(out[:, j * P:(j + 1) * P], probs[:, a % 3, j * P:(j + 1) * P],
                                                     ident[:])
                        mm.then_inc(pt_full, 1)

                    def values(a):
                        n, h = key_tiles(a), ATT[a][2]
                        pe.wait_ge(*turned_free(a))
                        if h == 0 and a >= 2 * NH:
                            pe.wait_ge(ot_copied, a // NH - 1)
                        if a == 2 * NH:
                            pe.wait_ge(vwin_in[1], 16 * NB)
                        for j in range(n):
                            mm = nc.tensor.matmul(out_at(a // NH)[:, h * HD:(h + 1) * HD],
                                                  pT[:, a % 2, j * P:(j + 1) * P],
                                                  value_tile(a, j), start=(j == 0), stop=(j == n - 1))
                        mm.then_inc(pv_done, 1)

                    def turn_block(j):
                        pe.wait_ge(o_copied, j + 1)
                        for f in range(BK):
                            mm = nc.tensor.transpose(out_at(j)[:, f * P:(f + 1) * P], otok[:, j % 2, f * P:(f + 1) * P],
                                                     ident[:])
                        mm.then_inc(ot_full, 1)

                    pe.wait_ge(gt_copied, 2 * NT)
                    pe.wait_ge(gc_copied, 1)
                    pe.wait_ge(kc_copied, 1)
                    pe.wait_ge(mix_copied, 4)
                    pe.wait_ge(conv_ready, 2)
                    for a in range(-1, NATT):
                        for u in units_to_score(a):
                            scores(u)
                        if a == -1:
                            product(("cb", BK - 1), h_cols)
                            pe.wait_ge(vwin_in[0], 16 * NB)
                            pe.wait_ge(cachev_in, 32)
                            pe.wait_ge(conv_ready, BK)
                        if a + 1 < NATT:
                            turn_probs(a + 1)
                        if a == NATT - 1:
                            product(("L", 0), h_cols)
                        if a >= 0:
                            values(a)
                        if a % NH == 1 and a > NH:
                            turn_block(a // NH - 1)
                    turn_block(NBLK - 1)

                    def branch_cols(n):
                        def rhs(k, i):
                            high, low = br_high[:, k, :], br_r[:, n, k, :]
                            if n == 0:
                                if i == 0:
                                    return tuple(a[:, 0:LAT].rearrange("p (b i r) -> p r b i", b=NB, i=QC)
                                                 for a in (high, low))
                                return high[:, LAT:TOK], low[:, LAT:TOK]
                            return high[:, i * HT:(i + 1) * HT], low[:, i * HT:(i + 1) * HT]
                        return rhs

                    pe.wait_ge(ot_copied, NBLK)
                    pe.wait_ge(*turned_free(NATT - 1))
                    for g in range(4 * DK):
                        n = merge_unit(g)[0]
                        if g:
                            product(("L", g), h_cols)
                        pe.wait_ge(br_ready, BK * (n + 1))
                        if n == 0:
                            product(("B", g), branch_cols(n), ((0, LAT), (LAT, CTX)))
                        else:
                            product(("B", g), branch_cols(n))

                    pe.wait_ge(merged_add, 2 * 4 * 4 - 2 * 4)
                    pe.wait_ge(prod_done, 4 * DK)
                    wo = [arrived(("wo", j)) for j in range(2)]

                    def half_output(out, t, j):
                        for k in range(DK):
                            mm = nc.tensor.matmul(out[:, j * BANK:(j + 1) * BANK], merged[:, k, t * P:(t + 1) * P],
                                                  wo[j][:, k * BANK:(k + 1) * BANK],
                                                  start=(k == 0), stop=(k == DK - 1))
                        return mm

                    for t in range(NT + 2):
                        if t < NT:
                            out = acquire(("y", t))
                            half_output(out, t, 0)
                        if t >= 2:
                            pe.wait_ge(aff_ready, t - 1)
                            out = acquire(("affT", t - 2))
                            nc.tensor.transpose(out[0:NE, 0:P], aff[:, t - 2, :], ident[:]).then_inc(affT_full, 1)
                        if 1 <= t < NT + 1:
                            pe.wait_ge(x1_ready, t)
                            out = acquire(("x1T", t - 1))
                            for k in range(DK):
                                mm = nc.tensor.transpose(out[:, k * P:(k + 1) * P],
                                                         x1[:, (t - 1) % 2, k * P:(k + 1) * P], ident[:])
                            mm.then_inc(x1T_full, 1)
                        if t < NT:
                            half_output(accf[pair(("y", t))], t, 1).then_inc(y_full, 1)
                        if 1 <= t < NT + 1:
                            pe.wait_ge(xmT_ready, DK * t)
                            out = acquire(("r", t - 1))
                            for k in range(DK):
                                mm = nc.tensor.matmul(out[:, 0:NE], xmT[:, (t - 1) % 2, k, :], router[:, k, :],
                                                      start=(k == 0), stop=(k == DK - 1))
                            mm.then_inc(r_full, 1)
                    pe.wait_ge(topk_ready, 1)
                    out = acquire(("sel",))
                    nc.tensor.transpose(out[0:CAP, 0:NE], idx_f[:, :], ident[0:NE, 0:NE])
                    nc.tensor.transpose(out[0:CAP, NE:2 * NE], vals[:, :], ident[0:NE, 0:NE]).then_inc(sel_full, 1)

                    def split_block(i, n):
                        pe.wait_ge(exp_ready, splits(i, n))
                        return exp_high[n % HIGHS], exp_slot_r[n % EXP_RING]

                    def three(out, x_high, x_low, w_high, w_low, start, stop):
                        nc.tensor.matmul(out, x_high, w_high, start=start, stop=False)
                        nc.tensor.matmul(out, x_high, w_low, start=False, stop=False)
                        return nc.tensor.matmul(out, x_low, w_high, start=False, stop=stop)

                    def half_product(i, j, part, pair_no, half):
                        w_high, w_low = split_block(i, PER_EXPERT * j + part)
                        for k in range(DK):
                            rows, cols = slice(k * CAP, (k + 1) * CAP), slice(k * BANK, (k + 1) * BANK)
                            mm = three(acc[pair_no][0:CAP, half, :], xs_high[:, j, rows], xsT_r[:, j, rows],
                                       w_high[:, cols], w_low[:, cols], k == 0, k == DK - 1)
                        mm.then_inc(part_done[part], 1)

                    def down_product(i, j, half):
                        n = PER_EXPERT * j + 4 + half
                        if half == 0:
                            w_high, w_low = split_block(i, n)
                        else:
                            pe.wait_ge(exp_full[n % EXP_RING], arrivals(i, n))
                            w = exp_slot[n % EXP_RING]
                        for c in range(2):
                            for k in range(4):
                                rows = slice(k * CAP, (k + 1) * CAP)
                                cols = slice(k * D + c * BANK, k * D + (c + 1) * BANK)
                                out = acc[2][0:CAP, c, :]
                                if half == 0:
                                    mm = three(out, hid_high[:, rows], hid_low[:, rows], w_high[:, cols], w_low[:, cols],
                                               k == 0, False)
                                else:
                                    mm = nc.tensor.matmul(out, hdnT[:, rows], w[:, cols], start=False, stop=(k == 3))
                        mm.then_inc(part_done[4 + half], 1)

                    def turn_hidden(half):
                        for k in range(4):
                            mm = nc.tensor.transpose(acc[3][:, 0, k * CAP:(k + 1) * CAP],
                                                     hdn[:, half * BANK + k * P:half * BANK + (k + 1) * P],
                                                     ident[0:CAP, 0:CAP])
                        mm.then_inc(hT_full, 1)

                    def turn_rows(j, half):
                        for k in range(4):
                            mm = nc.tensor.transpose(acc[3][:, 1, k * CAP:(k + 1) * CAP],
                                                     xs[:, j, (4 * half + k) * P:(4 * half + k + 1) * P],
                                                     ident[0:CAP, 0:CAP])
                        mm.then_inc(xT_full, 1)

                    pe.sem_inc(down1_done, 1)
                    pe.wait_ge(gather_done, layer * (16 * (NE + 1)) + 16)
                    turn_rows(0, 0)
                    pe.wait_ge(xsT_ready, 1)
                    turn_rows(0, 1)
                    with pe.Fori(0, NE // EXPERTS_IN_BODY) as i:
                        for j in range(EXPERTS_IN_BODY):
                            e1 = i * EXPERTS_IN_BODY + (j + 1)
                            e2 = i * (2 * EXPERTS_IN_BODY) + 2 * (j + 1)
                            pe.wait_ge(xsT_ready, e2)
                            pe.wait_ge(silu_done, e2 - 1)
                            half_product(i, j, 0, 0, 0)
                            pe.wait_ge(hidden_ready, e2 - 1)
                            half_product(i, j, 1, 1, 0)
                            pe.wait_ge(silu_done, e2)
                            half_product(i, j, 2, 0, 1)
                            pe.wait_ge(hidden_ready, e2 + 1)
                            pe.wait_ge(hT_copied, e2)
                            turn_hidden(0)
                            half_product(i, j, 3, 1, 1)
                            pe.wait_ge(gather_done, layer * (16 * (NE + 1)) + i * (16 * EXPERTS_IN_BODY) + 16 * (j + 2))
                            turn_rows(1 - j, 0)
                            pe.wait_ge(hT_copied, e2 + 1)
                            pe.wait_ge(hid_low_ready, e1)
                            pe.wait_ge(ye_ready, e1)
                            down_product(i, j, 0)
                            pe.wait_ge(hidden_ready, e2 + 2)
                            turn_hidden(1)
                            pe.wait_ge(xsT_ready, e2 + 1)
                            turn_rows(1 - j, 1)
                            pe.wait_ge(hT_copied, e2 + 2)
                            down_product(i, j, 1)
                    pe.wait_ge(xsT_ready, 2 * (NE + 1))
                    early_products(pe, layer + 1, early_done, early_copied, early_turned)

                @block.scalar
                def _(act):
                    copy = ACT.Copy
                    def high_weights(n):
                        r, use = slot_of(slot_key(PRODUCTS[n]))
                        kind, f = PRODUCTS[n]
                        act.wait_ge(slot_full[r], 16 * use)
                        if n < NPROJ:
                            if n >= 2:
                                act.wait_ge(*done(n - 2))
                        elif f >= 2:
                            act.wait_ge(*done(PRODUCT_NO[kind, f - 2]))
                        whole, _, high = weight_tile(n)
                        nc.scalar.activation(high, whole, copy).then_inc(w_high_ready, 1)

                    def high_ahead_of(n):
                        if 1 <= n < NPROJ - 1:
                            high_weights(n + 1)
                        act.wait_ge(*done(n))

                    for i in range(ADA_EARLY, ADA_SLOTS):
                        act.wait_ge(ada_done, i - ADA_EARLY + 1)
                        if i >= ADA_EARLY + 2:
                            act.wait_ge(mod_full, i - ADA_EARLY - 1)
                        nc.scalar.activation(adarow[:, i % 2, :], accf[pair(("ada", i))][0:2, 0:BANK], copy)\
                            .then_inc(ada_copied, 1)
                        if i == ADA_EARLY + 1:
                            for t in range(NT):
                                act.wait_ge(xt_full, t + 1)
                                nc.scalar.activation(hT[:, :, t * P:(t + 1) * P],
                                                     accf[pair(("xt", t))].rearrange("p (k n) -> p k n", k=DK), copy)\
                                    .then_inc(xt_copied, 1)
                        if i in (7, 8):
                            for k in range((i - 7) * 4, (i - 6) * 4):
                                act.wait_ge(h_whole, 2 * (k + 1))
                                nc.scalar.activation(h_high[:, k, :], hT[:, k, :], copy).then_inc(h_high_ready, 1)
                        if i == ADA_SLOTS - 2:
                            high_weights(0)
                            high_weights(1)
                    for f in range(BK):
                        high_ahead_of(PRODUCT_NO["q", f])
                        a = acc[pair(("q", f))]
                        blocks = qT[:, f, 0:LAT].rearrange("p (b i r) -> p r b i", b=NB, i=QC)
                        rows = HT // GW
                        nc.scalar.activation(blocks[:, 0:rows], a[:, 0, 0:HT].rearrange("p (r b i) -> p r b i", r=rows, b=NB),
                                             copy, scale=QSCALE).then_inc(q_copied, 1)
                        nc.scalar.activation(blocks[:, rows:GR], a[:, 1, 0:LAT - HT]
                                             .rearrange("p (r b i) -> p r b i", r=GR - rows, b=NB),
                                             copy, scale=QSCALE).then_inc(q_copied, 1)
                        nc.scalar.activation(qT[:, f, LAT:TOK], a[:, 1, LAT - HT:HT], copy, scale=QSCALE)\
                            .then_inc(q_copied, 1)
                    act.wait_ge(gateT_full, 1)
                    nc.scalar.activation(grow[:], accf[pair(("gateT",))][0:32, 0:P], copy).then_inc(gateT_copied, 1)
                    act.wait_ge(gateT_copied, 1)
                    act.dma_start(gate_scr, grow[:]).then_inc(gate_out, 16)
                    for f in range(BK):
                        high_ahead_of(PRODUCT_NO["k", f])
                        nc.scalar.activation(by_half(na_kT[:, f, 0:TOK]), halves(("k", f)), copy).then_inc(k_copied, 1)
                    for f in range(BK):
                        high_ahead_of(PRODUCT_NO["v", f])
                        nc.scalar.activation(by_half(vT[:, f, :]), halves(("v", f)), copy).then_inc(vraw_copied, 1)
                        if f == 0:
                            act.wait_ge(kc_full, 1)
                            nc.scalar.activation(na_kT[:, :, TOK:TOK + PAST],
                                                 accf[pair(("kc",))][:, 0:BW].rearrange("p (f n) -> p f n", f=BK), copy)\
                                .then_inc(kc_copied, 1)
                            act.wait_ge(ks_full, 1)
                            nc.scalar.activation(k_state, accf[pair(("ks",))][:, 0:BW], copy).then_inc(ks_copied, 1)
                            act.wait_ge(ks_copied, 1)
                            act.dma_start(st_na_k[layer], k_state).then_inc(state_out, 16)

                    def copy_gq(f):
                        high_ahead_of(PRODUCT_NO["gq", f])
                        nc.scalar.activation(by_half(gq_raw[:, f, :]), halves(("gq", f)), copy).then_inc(graw_copied, 1)

                    copy_gq(0)
                    for t in range(NT):
                        act.wait_ge(v_full, t + 1)
                        nc.scalar.activation(vstage[:, t, :] if t < NLT else vctx, accf[pair(("vt", t))][:, 0:BW], copy)\
                            .then_inc(v_copied, 1)
                    act.wait_ge(v_copied, NT)
                    act.dma_start(st_na_v[layer], vctx).then_inc(state_out, 16)
                    act.dma_start(v_scr.rearrange("(t p) n -> p t n", p=P), vstage).then_inc(vscr_out, 16)

                    for f in range(1, BK):
                        copy_gq(f)
                    for f in range(2):
                        high_ahead_of(PRODUCT_NO["gkv", f])
                        nc.scalar.activation(by_half(kv_raw[:, f, :]), halves(("gkv", f)), copy)\
                            .then_inc(graw_copied, 1)

                    act.wait_ge(state_out, 32)
                    for t in range(NT + 1):
                        if t < NT:
                            act.wait_ge(g_full, t + 1)
                            a = accf[pair(("g", t))]
                            if t >= 2:
                                act.wait_ge(gt_full, t - 1)
                            nc.scalar.activation(gtok[:, t % 2, 0:640], a[:, 0:640], copy).then_inc(g_copied, 1)
                            nc.scalar.activation(gv[:, t, :], a[:, 640:768], copy).then_inc(g_copied, 1)
                            act.wait_ge(ss_ready, t + 1)
                            nc.scalar.activation(qk_std[:, t, :], qk_ss[:, t, :], ACT.Sqrt, bias=eps[:, 0:1],
                                                 scale=1.0 / HD).then_inc(std_ready, 1)
                        for n in STEP_PRODUCTS[t]:
                            high_ahead_of(n)
                            kind, f = PROJ[n]
                            if n == 18:
                                act.wait_ge(vscr_out, 16)
                            nc.scalar.activation(by_half(br[:, 3 if kind == "pool" else 2, f, :]), halves((kind, f)), copy)\
                                .then_inc(pool_copied if kind == "pool" else c_copied, 1)
                        if t >= 1:
                            act.wait_ge(gt_full, t)
                            a = accf[pair(("gt", t - 1))]
                            c0 = (t - 1) * P
                            nc.scalar.activation(gqT[:, :, c0:c0 + P],
                                                 a[:, 0:BW].rearrange("p (f n) -> p f n", f=BK), copy, scale=QSCALE)\
                                .then_inc(gt_copied, 1)
                            nc.scalar.activation(gkT[:, :, c0:c0 + P],
                                                 a[:, BW:BW + 2 * P].rearrange("p (f n) -> p f n", f=KVH), copy)\
                                .then_inc(gt_copied, 1)
                    act.wait_ge(gtok_ready, NT)
                    act.dma_start(st_g_k[layer], gtok[:, (NT - 1) % 2, BW:BW + P]).then_inc(state_out, 16)
                    act.wait_ge(g_copied, 2 * NT)
                    act.dma_start(st_g_v[layer], gv[:, NT - 1, :]).then_inc(state_out, 16)
                    act.wait_ge(gc_full, 1)
                    nc.scalar.activation(gkT[:, :, TOK:TOK + PAST],
                                         accf[pair(("gc",))][:, 0:2 * P].rearrange("p (f n) -> p f n", f=KVH), copy)\
                        .then_inc(gc_copied, 1)
                    act.wait_ge(small_in, 16)
                    for f in range(4):
                        high_weights(PRODUCT_NO["ch", f] + 1)
                        act.wait_ge(mix_full, f + 1)
                        nc.scalar.activation(br[:, 3, f, :], accf[pair(("mix", f))][:, 0:TOK], copy,
                                             scale=smallp[:, 64 + f:65 + f]).then_inc(mix_copied, 1)

                    def load_windows(first):
                        for b in range(first, first + 2):
                            for half in range(2):
                                rows = v_scr.rearrange("(r c) n -> r c n", c=GW)[4 * half:4 * half + 4,
                                                                               KEY_COL[b]:KEY_COL[b] + KC, :]
                                act.dma_start(vwin[:, 2 * b + half, :], rows).then_inc(vwin_in[first // 2], 16)

                    for f in range(1, BK):
                        high_weights(PRODUCT_NO["cb", f])
                        if f == 1:
                            act.wait_ge(kc_full, 1)
                            act.wait_ge(gc_dup, 1)
                            act.wait_ge(gtok_ready, NT)
                            load_windows(0)
                    def exps(a):
                        n = key_tiles(a) * P
                        act.wait_ge(rowmax_ready, a + 1)
                        if a >= 3:
                            act.wait_ge(pt_full, a - 2)
                        nc.scalar.activation(probs[:, a % 3, 0:n], scores_at(a)[:, 0:n], ACT.Exp,
                                             bias=negmax[:, a:a + 1], accum_out=sums[:, a:a + 1])\
                            .then_inc(probs_ready, 1)

                    def block_out(j):
                        kind, b, _ = ATT[j * NH]
                        act.wait_ge(ot_full, j + 1)
                        dst = (qT if kind == "na" else gqT)[:, :, b * P:(b + 1) * P]
                        nc.scalar.activation(dst, out_at(j).rearrange("p (f n) -> p f n", f=BK), copy)\
                            .then_inc(ot_copied, 1)

                    def high_branch(n):
                        for k in range(BK):
                            nc.scalar.activation(br_high[:, k, :], br[:, n, k, :], copy).then_inc(br_high_ready, 1)

                    act.wait_ge(state_out, 64)
                    for a in range(-1, NATT):
                        if a == NATT - 2:
                            high_weights(PRODUCT_NO["L", 0])
                            act.wait_ge(ot_copied, NBLK // 2)
                            high_branch(0)
                        for u in units_to_score(a):
                            exps(u)
                        if a + 1 < NA_UNITS:
                            n = key_tiles(a + 1) * P
                            act.wait_ge(pt_full, a + 2)
                            if a >= 1:
                                act.wait_ge(pv_done, a)
                            nc.scalar.activation(pT[:, (a + 1) % 2, 0:n], turned_at(a + 1)[:, 0:n], copy)\
                                .then_inc(pt_copied_act, 1)
                        if a == 0:
                            act.wait_ge(*done(NPROJ - 1))
                            load_windows(2)
                        if a % NH == 1 and a > NH:
                            block_out(a // NH - 1)
                    block_out(NBLK - 1)

                    act.wait_ge(ot_copied, NBLK)
                    act.wait_ge(conv_ready, BK)
                    high_weights(PRODUCT_NO["B", 0])
                    act.wait_ge(gate_out, 16)

                    def load_ln(n, dst, signal):
                        a = ln_p[layer, n]
                        act.dma_start(dst, bass.AP(a.tensor, a.offset, [[0, P], [1, D]])).then_inc(signal, 16)

                    for g in range(2):
                        act.dma_start(gate1[:, g, :].rearrange("p (k n) -> p k n", k=DK),
                                      bass.AP(gate_scr.tensor, gate_scr.offset + g * P, [[0, P], [2 * P, DK], [1, P]]))\
                            .then_inc(gate1_in, 16)
                    for g in range(4 * DK):
                        if g + 1 < 4 * DK:
                            high_weights(PRODUCT_NO["L", g + 1])
                        if g and g % DK == 0:
                            act.wait_ge(*done(PRODUCT_NO["B", g - 1]))
                            high_branch(g // DK)
                        act.wait_ge(*done(PRODUCT_NO["L", g]))
                        if g >= 2:
                            act.wait_ge(prod_done, g - 1)
                        nc.scalar.activation(by_half(sg[:, g % 2, :]), halves(("L", g)), ACT.Sigmoid)\
                            .then_inc(sig_ready, 1)
                        if g + 1 < 4 * DK:
                            high_weights(PRODUCT_NO["B", g + 1])

                    def load_x(t):
                        if t >= 2:
                            act.wait_ge(z_free, t - 1)
                        act.dma_start(xin[:, t % 2, :], out_rows(t)).then_inc(xin_in[t % 2], 16)

                    act.wait_ge(prod_done, 4 * DK)
                    act.wait_ge(merged_add, 3 * DK)
                    load_ln(0, lng, ln1_in)
                    load_ln(1, lnb, ln1_in)
                    load_x(0)
                    load_x(1)
                    for t in range(NT + 1):
                        if t >= 1:
                            act.wait_ge(x1T_full, t)
                            if t >= 3:
                                act.wait_ge(r_full, t - 2)
                            g = 0 if t - 1 < NLT else 1
                            for k in range(DK):
                                nc.scalar.activation(xmT[:, (t - 1) % 2, k, :],
                                                     accf[pair(("x1T", t - 1))][:, k * P:(k + 1) * P], ACT.Identity,
                                                     scale=mod[:, g, 32 + k:33 + k], bias=mod[:, g, 24 + k:25 + k])\
                                    .then_inc(xmT_ready, 1)
                            act.wait_ge(negl_ready, t)
                            nc.scalar.activation(lg[:, t - 1, 4:4 + NE], accf[pair(("r", t - 1))][:, 0:NE], ACT.Exp,
                                                 bias=lg[:, t - 1, 1:2], accum_out=lg[:, t - 1, 2:3])\
                                .then_inc(el_ready, 1)
                        if t < NT:
                            act.wait_ge(var_ready, t + 1)
                            nc.scalar.activation(std[:, 0, t:t + 1], mv[:, 0, t, 1:2], ACT.Sqrt, bias=eps[:, 0:1])\
                                .then_inc(std1_ready, 1)
                            if t + 2 < NT:
                                load_x(t + 2)
                            act.wait_ge(x1_ready, t + 1)
                            act.dma_start(x1_scr[t * P:(t + 1) * P, :], x1[:, t % 2, :]).then_inc(x1_out[t % 2], 16)
                            act.wait_ge(xa_ready, t + 1)
                            act.dma_start(y_acc[t * P:(t + 1) * P, :], xa[:, t % 2, :]).then_inc(x1_out[t % 2], 16)

                    act.sem_inc(silu_done, 2)
                    act.sem_inc(hT_copied, 2)
                    act.wait_ge(xa_ready, NT)
                    load_ln(2, lng, ln2_in)
                    load_ln(3, lnb, ln2_in)
                    act.wait_ge(y_full, NT)
                    for g, lo, hi in ((0, 0, CAP_L), (1, CAP_L, CAP)):
                        act.dma_start(gate2[lo:hi, :].rearrange("p (k n) -> p k n", k=DK),
                                      bass.AP(gate_scr.tensor, gate_scr.offset + (16 + g) * P,
                                              [[0, hi - lo], [2 * P, DK], [1, P]])).then_inc(gate2_in, 16)
                    def high_block(i, n, first=False):
                        act.wait_ge(exp_full[n % EXP_RING], arrivals(i, n))
                        if not first:
                            act.wait_ge(*multiplied(i, n - HIGHS))
                        nc.scalar.activation(exp_high[n % HIGHS], exp_slot[n % EXP_RING], copy).then_inc(exp_high_ready, 1)

                    act.wait_ge(*done(len(PRODUCTS) - 1))
                    for p in range(2):
                        act.wait_ge(x1_out[p], 32 * ((NT + 1 - p) // 2))
                    high_block(0, 0, first=True)
                    high_block(0, 1, first=True)

                    def experts_act(i, last):
                        for j in range(EXPERTS_IN_BODY):
                            e1 = i * EXPERTS_IN_BODY + (j + 1)
                            e2 = i * (2 * EXPERTS_IN_BODY) + 2 * (j + 1)
                            n = PER_EXPERT * j

                            def silu(half):
                                cols = slice(half * BANK, (half + 1) * BANK)
                                act.wait_ge((gate0_done, gate1_done)[half], e1)
                                act.wait_ge(hidden_ready, e2 - 1 + half)
                                nc.scalar.activation(act_s[:, cols], acc[0][0:CAP, half, :], ACT.Silu)\
                                    .then_inc(silu_done, 1)

                            def copy_hidden(half):
                                act.wait_ge(hT_full, e2 - 1 + half)
                                nc.scalar.activation(hid_high if half == 0 else hdnT, acc[3][:, 0, 0:4 * CAP], copy)\
                                    .then_inc(hT_copied, 1)

                            high_block(i, n + 2)
                            silu(0)
                            high_block(i, n + 3)
                            high_block(i, n + 4)
                            silu(1)
                            copy_hidden(0)
                            more = not (last and j == EXPERTS_IN_BODY - 1)
                            if more:
                                high_block(i, n + PER_EXPERT)
                            copy_hidden(1)
                            if more:
                                high_block(i, n + PER_EXPERT + 1)

                    with act.Fori(0, NE // EXPERTS_IN_BODY - 1) as i:
                        experts_act(i, False)
                    experts_act(NE // EXPERTS_IN_BODY - 1, True)

                    act.wait_ge(scatter_done, layer * (16 * NE) + 16 * NE)
                    for t in range(NT):
                        act.dma_start(z2[:, t, :], y_acc[t * P:(t + 1) * P, :]).then_inc(zin_in[t], 16)

                    def std2(t):
                        act.wait_ge(var2_ready, t + 1)
                        nc.scalar.activation(std[:, 1, t:t + 1], mv[:, 1, t, 1:2], ACT.Sqrt, bias=eps[:, 0:1])\
                            .then_inc(std2_ready, 1)

                    def store(t):
                        act.wait_ge(x2_ready, t + 1)
                        act.dma_start(out_rows(t), z2[:, t, :]).then_inc(x2_out, 16)

                    def early_row(i):
                        act.wait_ge(early_done, i + 1)
                        if i >= 2:
                            act.wait_ge(early_turned, i - 1)
                        nc.scalar.activation(adarow[:, i % 2, :], accf[i % 2][0:2, 0:BANK], copy)\
                            .then_inc(early_copied, 1)

                    for step, n in ((std2, 0), (early_row, 0), (store, 0), (std2, 1), (store, 1), (early_row, 1),
                                    (std2, 2), (store, 2), (early_row, 2), (std2, 3), (store, 3), (std2, 4),
                                    (early_row, 3), (store, 4)):
                        step(n)
                    act.wait_ge(x2_out, 16 * NT)

                @block.vector
                def _(dve):
                    v = nc.vector
                    chained = [0]

                    def link(ins):
                        chained[0] += 1
                        ins.then_inc(dve_step, 1)
                        dve.wait_ge(dve_step, chained[0])

                    def low_weights(n):
                        dve.wait_ge(w_high_ready, n + 1)
                        whole, low, high = weight_tile(n)
                        v.tensor_tensor(low, whole, high, ALU.subtract).then_inc(w_ready, 1)

                    def modulation(lo, hi, bank):
                        return v.tensor_tensor(mod[:].rearrange("p g c -> p c g")[:, lo:hi],
                                               bank[:, 2 * lo:2 * hi].rearrange("p (c g) -> p c g", g=2),
                                               bc(smallp[:, lo:hi], (1, hi - lo), (0, 2)), ALU.add)

                    dve.wait_ge(small_in, 16)
                    link(modulation(0, 16, o_bank))
                    link(v.tensor_scalar(mod[:, :, 8:16], mod[:, :, 8:16], 1.0, None, ALU.add))
                    dve.wait_ge(xt_copied, NT)
                    for k in range(DK):
                        for g in range(2):
                            x = hT[:, k, group_cols(g)]
                            v.tensor_scalar(x, x, mod[:, g, 8 + k:9 + k], mod[:, g, k:k + 1], ALU.mult, ALU.add)\
                                .then_inc(h_whole, 1)
                    for k in range(DK):
                        dve.wait_ge(h_high_ready, k + 1)
                        v.tensor_tensor(hT_r[:, k, :], hT[:, k, :], h_high[:, k, :], ALU.subtract).then_inc(h_ready, 1)
                    low_weights(0)
                    low_weights(1)
                    dve.wait_ge(mod_full, ADA_SLOTS - ADA_EARLY)
                    modulation(16, 48, ot_bank).then_inc(mod_ready, 1)
                    dve.wait_ge(mod_ready, 1)
                    v.tensor_scalar(mod[:, :, 32:40], mod[:, :, 32:40], 1.0, None, ALU.add).then_inc(dve_step, 1)
                    chained[0] += 1
                    v.tensor_copy(gate_cols.rearrange("p (j k g) -> p j k g", j=2, g=2),
                                  bc(mod[:, 0, 16:24], (24, 2), (1, DK), (48, 2))).then_inc(mod_ready, 1)
                    dve.wait_ge(dve_step, chained[0])
                    for n in range(2, 19):
                        low_weights(n)

                    def duplicate(dst, src):
                        return v.tensor_copy(dst.rearrange("p (g c n) -> p g c n", g=KVH, c=2),
                                             bc(src, (HD, KVH), (0, 2), (1, HD)))

                    dve.wait_ge(param_in, 48)
                    for t in range(NT):
                        x = gtok[:, t % 2, 0:640]
                        dve.wait_ge(g_copied, 2 * t + 2)
                        link(v.tensor_tensor(t1, x, x, ALU.mult))
                        v.tensor_reduce(qk_ss[:, t, :], t1.rearrange("p (h d) -> p h d", d=HD), AX.X, ALU.add)\
                            .then_inc(ss_ready, 1)
                        dve.wait_ge(std_ready, t + 1)
                        link(v.reciprocal(qk_rstd[:, t, :], qk_std[:, t, :]))
                        xh = x.rearrange("p (h d) -> p h d", d=HD)
                        link(v.tensor_tensor(xh, xh, bc(qk_rstd[:, t, :], (1, 10), (0, HD)), ALU.mult))
                        link(v.tensor_tensor(xh[:, 0:NH, :], xh[:, 0:NH, :], bc(gain[:, 0, :], (0, NH), (1, HD)), ALU.mult))
                        link(v.tensor_tensor(xh[:, NH:10, :], xh[:, NH:10, :], bc(gain[:, 1, :], (0, KVH), (1, HD)), ALU.mult))
                        if t < NLT:
                            link(v.tensor_tensor(t1.rearrange("p (h d) -> p h d", d=HD), xh,
                                                 bc(rope[:, t, 0, :], (0, 10), (1, HD)), ALU.mult))
                            link(v.tensor_tensor(t2.rearrange("p (h d) -> p h d", d=HD), xh,
                                                 bc(rope[:, t, 1, :], (0, 10), (1, HD)), ALU.mult))
                            x4, c4, s4 = (z.rearrange("p (h q n) -> p h q n", h=20, q=2) for z in (x, t1, t2))
                            link(v.tensor_tensor(x4[:, :, 0, :], c4[:, :, 0, :], s4[:, :, 1, :], ALU.subtract))
                            link(v.tensor_tensor(x4[:, :, 1, :], s4[:, :, 0, :], c4[:, :, 1, :], ALU.add))
                        if t >= 2:
                            dve.wait_ge(gt_full, t - 1)
                        duplicate(kdup[:, t % 2, :], x[:, BW:BW + P]).then_inc(gtok_ready, 1)
                        for n in STEP_PRODUCTS[t]:
                            low_weights(n + 1)
                    low_weights(26)
                    dve.wait_ge(kcache_in, 32)
                    dve.wait_ge(gt_full, NT - 1)
                    duplicate(kdup[:, NT % 2, :], g_cached).then_inc(gc_dup, 1)

                    dve.wait_ge(gc_full, 1)
                    for i in range(3):
                        link(v.memset(pu[i], 0.0))

                    def pooling(f, win):
                        dve.wait_ge(pool_copied, f + 1)
                        if f:
                            dve.wait_ge(pool_ready, f)
                        u, wa, wb = pu[0], pu[1], pu[2]
                        link(v.tensor_copy(u[:, 8:8 + LAT], br[:, 3, f, 0:LAT]))
                        link(v.tensor_copy(u[:, 24 + LAT:24 + TOK], br[:, 3, f, LAT:TOK]))
                        link(v.tensor_tensor(wa[:, 1:PW], u[:, 0:PW - 1], u[:, 1:PW], ALU.add))
                        cur, other, step, lo = wa, wb, 1, 1
                        while 2 * step < win:
                            lo += step
                            link(v.tensor_tensor(other[:, lo:PW - lo + 1], cur[:, lo - step:PW - lo + 1 - step],
                                                 cur[:, lo + step:PW - lo + 1 + step], ALU.add))
                            cur, other, step = other, cur, 2 * step
                        for at0, n in ((8, LAT), (24 + LAT, CTX)):
                            e = bc(cur[:, at0:at0 + 1], (n - 8, 2), (1, 8))
                            link(v.tensor_tensor(e, e, corr[:, f, :].rearrange("p (a b) -> p a b", a=2), ALU.mult))
                        for at0, n, o in ((8, LAT, 0), (24 + LAT, CTX, LAT)):
                            ins = v.scalar_tensor_tensor(out=br[:, 3, f, o:o + n], in0=cur[:, at0:at0 + n],
                                                         scalar=1.0 / win, in1=u[:, at0:at0 + n],
                                                         op0=ALU.mult, op1=ALU.subtract)
                            if o == 0:
                                link(ins)
                        ins.then_inc(pool_ready, 1)

                    for f, win in enumerate(POOL_WINDOWS):
                        low_weights(PRODUCT_NO["ch", f] + 1)
                        pooling(f, win)
                        dve.wait_ge(c_copied, f + 1)
                        dve.wait_ge(*done(PRODUCT_NO["ch", f]))
                        u = by_half(br[:, 2, f, :])
                        v.tensor_tensor(u, halves(("ch", f)), u, ALU.mult).then_inc(u_ready, 1)
                    def conv_product(f):
                        dve.wait_ge(*done(PRODUCT_NO["cb", f]))
                        v.tensor_tensor(by_half(br[:, 2, f, :]), halves(("cb", f)), by_half(conv_y), ALU.mult)\
                            .then_inc(conv_ready, 1)

                    dve.wait_ge(pool_ready, 4)
                    for f in range(BK):
                        if f < BK - 1:
                            low_weights(PRODUCT_NO["cb", f] + 1)
                        dve.wait_ge(u_ready, f + 1)
                        if f:
                            dve.wait_ge(conv_ready, f)
                        u = br[:, 2, f, :]
                        tap = [smallp[:, 48 + 3 * f + j:49 + 3 * f + j] for j in range(3)]
                        link(v.tensor_scalar(conv_y, u, tap[1], smallp[:, 60 + f:61 + f], ALU.mult, ALU.add))
                        for lo, hi in ((0, LAT), (LAT, TOK)):
                            link(v.scalar_tensor_tensor(out=conv_y[:, lo + 1:hi], in0=u[:, lo:hi - 1], scalar=tap[0],
                                                        in1=conv_y[:, lo + 1:hi], op0=ALU.mult, op1=ALU.add))
                            link(v.scalar_tensor_tensor(out=conv_y[:, lo:hi - 1], in0=u[:, lo + 1:hi], scalar=tap[2],
                                                        in1=conv_y[:, lo:hi - 1], op0=ALU.mult, op1=ALU.add))
                        if f < BK - 1:
                            conv_product(f)

                    def maxima(a):
                        kind, b, h = ATT[a]
                        n = key_tiles(a) * P
                        out = scores_at(a)
                        dve.wait_ge(scores_full, a + 1)
                        if kind == "na" and b < NB:
                            if a == 0:
                                dve.wait_ge(bias_in, 16 * GR * GR)
                            win = out[:, 0:NWIN].rearrange("p (r c) -> p r c", c=KC)
                            link(v.tensor_tensor(win, win, bias_of(h, b), ALU.add))
                        v.reduce_max(negmax[:, a:a + 1], out[:, 0:n], AX.X, negate=True).then_inc(rowmax_ready, 1)

                    def block_norm(j):
                        dve.wait_ge(pv_done, NH * (j + 1))
                        link(v.reciprocal(rsum[:, NH * j:NH * (j + 1)], sums[:, NH * j:NH * (j + 1)]))
                        if j >= 2:
                            dve.wait_ge(ot_full, j - 1)
                        v.tensor_tensor(otok[:, j % 2, :].rearrange("p (h d) -> p h d", d=HD),
                                        out_at(j).rearrange("p (h d) -> p h d", d=HD),
                                        bc(rsum[:, NH * j:NH * (j + 1)], (1, NH), (0, HD)), ALU.mult)\
                            .then_inc(o_copied, 1)

                    def low_branch(n):
                        for k in range(BK):
                            dve.wait_ge(br_high_ready, BK * n + k + 1)
                            v.tensor_tensor(br_r[:, n, k, :], br[:, n, k, :], br_high[:, k, :], ALU.subtract)\
                                .then_inc(br_ready, 1)

                    for a in range(-1, NATT):
                        for u in units_to_score(a):
                            maxima(u)
                        if a == -1:
                            conv_product(BK - 1)
                        if a == NATT - 2:
                            low_weights(PRODUCT_NO["L", 0])
                            low_branch(0)
                        if NA_UNITS <= a + 1 < NATT:
                            n = key_tiles(a + 1) * P
                            dve.wait_ge(pt_full, a + 2)
                            dve.wait_ge(pv_done, a)
                            v.tensor_copy(pT[:, (a + 1) % 2, 0:n], turned_at(a + 1)[:, 0:n])\
                                .then_inc(pt_copied_dve, 1)
                        if a >= 0 and a % NH == NH - 1:
                            block_norm(a // NH)

                    dve.wait_ge(ot_full, NBLK)
                    low_weights(PRODUCT_NO["B", 0])
                    added = 0
                    for g in range(4 * DK):
                        if g + 1 < 4 * DK:
                            low_weights(PRODUCT_NO["L", g + 1])
                        n, _, d = merge_unit(g)
                        if g and g % DK == 0:
                            low_branch(n)
                        a = accf[pair(("B", g))][:, 0:TOK] if n == 0 else halves(("B", g))
                        gates = sg[:, g % 2, :] if n == 0 else by_half(sg[:, g % 2, :])
                        dve.wait_ge(sig_ready, g + 1)
                        dve.wait_ge(*done(PRODUCT_NO["B", g]))
                        if n == 0:
                            v.tensor_tensor(merged[:, d, :], a, gates, ALU.mult).then_inc(prod_done, 1)
                            low_weights(PRODUCT_NO["B", g + 1])
                            continue
                        if added:
                            dve.wait_ge(merged_add, added)
                        added += 1
                        v.tensor_tensor(by_half(prod[:, g % 2, :]), a, gates, ALU.mult).then_inc(prod_done, 1)
                        if g + 1 < 4 * DK:
                            low_weights(PRODUCT_NO["B", g + 1])
                        dve.wait_ge(prod_done, g + 1)
                        v.tensor_tensor(merged[:, d, :], merged[:, d, :], prod[:, g % 2, :], ALU.add)\
                            .then_inc(merged_add, 1)

                    def layer_norm(n, t, z, out, var_ready, std_ready, got):
                        for j in range(2):
                            link(v.bn_stats(stats[:, n, t, 6 * j:6 * j + 6], z[:, j * BANK:(j + 1) * BANK]))
                        v.bn_aggr(mv[:, n, t, :], stats[:, n, t, :]).then_inc(var_ready, 1)
                        dve.wait_ge(std_ready, t + 1)
                        link(v.reciprocal(rstd[:, n, t:t + 1], std[:, n, t:t + 1]))
                        link(v.tensor_scalar(z, z, mv[:, n, t, 0:1], rstd[:, n, t:t + 1], ALU.subtract, ALU.mult))
                        link(v.tensor_tensor(z, z, lng, ALU.mult))
                        v.tensor_tensor(out, z, lnb, ALU.add).then_inc(got, 1)

                    dve.wait_ge(ln1_in, 32)
                    dve.wait_ge(gate1_in, 32)
                    def choice(g, cap, first):
                        row = affT[:, group_cols(g)]
                        for r in range(cap // 8):
                            v8 = vals[:, first + 8 * r:first + 8 * r + 8]
                            link(v.max(v8, row))
                            link(v.max_index(idx_u[:, first + 8 * r:first + 8 * r + 8], v8, row))
                            link(v.match_replace(row, v8, row, -1.0))

                    for t in range(NT + 2):
                        if t >= 2:
                            q = t - 2
                            dve.wait_ge(affT_full, q + 1)
                            v.tensor_copy(affT[:, q * P:(q + 1) * P], accf[pair(("affT", q))][0:NE, 0:P])\
                                .then_inc(affT_copied, 1)
                            if q == NLT - 1:
                                dve.wait_ge(affT_copied, NLT)
                                choice(0, CAP_L, 0)
                        if 1 <= t < NT + 1:
                            q = t - 1
                            a = accf[pair(("r", q))][:, 0:NE]
                            dve.wait_ge(r_full, q + 1)
                            v.reduce_max(lg[:, q, 1:2], a, AX.X, negate=True).then_inc(negl_ready, 1)
                            dve.wait_ge(el_ready, q + 1)
                            link(v.reciprocal(lg[:, q, 3:4], lg[:, q, 2:3]))
                            v.tensor_scalar(aff[:, q, :], lg[:, q, 4:4 + NE], lg[:, q, 3:4], None, ALU.mult)\
                                .then_inc(aff_ready, 1)
                        if t < NT:
                            g = 0 if t < NLT else 1
                            z = zt[:, t % 2, :]
                            dve.wait_ge(y_full, t + 1)
                            link(v.tensor_tensor(z, accf[pair(("y", t))], gate1[:, g, :], ALU.mult))
                            dve.wait_ge(xin_in[t % 2], 16 * (t // 2 + 1))
                            v.scalar_tensor_tensor(out=z, in0=xin[:, t % 2, :], scalar=ALPHA, in1=z,
                                                   op0=ALU.mult, op1=ALU.add).then_inc(z_free, 1)
                            dve.wait_ge(z_free, t + 1)
                            if t >= 2:
                                dve.wait_ge(x1T_full, t - 1)
                                dve.wait_ge(x1_out[t % 2], 32 * (t // 2))
                            layer_norm(0, t, z, x1[:, t % 2, :], var_ready, std1_ready, x1_ready)
                            dve.wait_ge(x1_ready, t + 1)
                            v.tensor_scalar(xa[:, t % 2, :], x1[:, t % 2, :], ALPHA, None, ALU.mult)\
                                .then_inc(xa_ready, 1)

                    dve.wait_ge(affT_copied, NT)
                    choice(1, CAP_C, CAP_L)
                    link(v.tensor_copy(idx_f[:, 0:CAP_L], idx_u[:, 0:CAP_L]))
                    v.tensor_scalar(idx_f[:, CAP_L:CAP], idx_u[:, CAP_L:CAP], float(LAT), None, ALU.add)\
                        .then_inc(topk_ready, 1)
                    dve.wait_ge(sel_full, 1)
                    a = accf[pair(("sel",))]
                    link(v.tensor_copy(idx_t[:, NE:NE + 1], a[0:CAP, 0:1]))
                    link(v.tensor_copy(g_t[:, NE:NE + 1], a[0:CAP, NE:NE + 1]))
                    v.tensor_copy(idx_t[:, 0:NE], a[0:CAP, 0:NE]).then_inc(sel_ready, 1)
                    v.tensor_copy(g_t[:, 0:NE], a[0:CAP, NE:2 * NE]).then_inc(sel_ready, 1)
                    dve.wait_ge(sel_ready, 2)

                    dve.sem_inc(hidden_ready, 2)
                    dve.sem_inc(ye_ready, 1)

                    def choose(e, j, first):
                        v.tensor_copy(idx_cur[:, j:j + 1], idx_t[:, bass.ds(e, 1)]).then_inc(first, 1)
                        v.tensor_copy(g_cur[:, j:j + 1], g_t[:, bass.ds(e, 1)]).then_inc(sel_cur, 1)

                    def modulate(b, half, sem_, count):
                        x = xsT[:, b, :]
                        def parts(a, base, step):
                            return bc(a[:, base:base + 1], (CAP, 4), (1, step))
                        for vec, op in ((32 + 4 * half, ALU.mult), (24 + 4 * half, ALU.add)):
                            for g, c0, n in ((0, 0, CAP_L), (1, CAP_L, CAP_C)):
                                dst = parts(x, 4 * CAP * half + c0, n)
                                src = parts(acc[3][:, 1, :], c0, n) if op == ALU.mult else dst
                                v.tensor_tensor(dst, src, bc(mod[:, g, vec:vec + 1], (1, 4), (0, n)), op)\
                                    .then_inc(sem_, 1)
                            dve.wait_ge(sem_, count + (2 if op == ALU.mult else 4))
                        cols = slice(4 * CAP * half, 4 * CAP * (half + 1))
                        v.tensor_copy(xs_high[:, b, cols], x[:, cols]).then_inc(sem_, 1)
                        dve.wait_ge(sem_, count + 5)
                        v.tensor_tensor(xsT_r[:, b, cols], x[:, cols], xs_high[:, b, cols], ALU.subtract)\
                            .then_inc(xsT_ready, 1)

                    def low_block(i, n):
                        dve.wait_ge(exp_high_ready, splits(i, n))
                        v.tensor_tensor(exp_slot_r[n % EXP_RING], exp_slot[n % EXP_RING], exp_high[n % HIGHS],
                                        ALU.subtract).then_inc(exp_ready, 1)

                    choose(0, 0, dve_step)
                    chained[0] += 1
                    low_block(0, 0)
                    for half in range(2):
                        dve.wait_ge(xT_full, half + 1)
                        modulate(0, half, dve_step, chained[0])
                        chained[0] += 5
                    low_block(0, 1)
                    dve.wait_ge(gate2_in, 32)
                    LOOP_INCS = 11

                    def experts_dve(i, last):
                        for j in range(EXPERTS_IN_BODY):
                            e1 = i * EXPERTS_IN_BODY + (j + 1)
                            e2 = i * (2 * EXPERTS_IN_BODY) + 2 * (j + 1)
                            base = i * (LOOP_INCS * EXPERTS_IN_BODY) + LOOP_INCS * j
                            n = PER_EXPERT * j
                            more = not (last and j == EXPERTS_IN_BODY - 1)

                            def hidden(half):
                                cols = slice(half * BANK, (half + 1) * BANK)
                                dve.wait_ge((up0_done, up1_done)[half], e1)
                                dve.wait_ge(silu_done, e2 + 1 + half)
                                v.tensor_tensor(hdn[:, cols], acc[1][0:CAP, half, :], act_s[:, cols], ALU.mult)\
                                    .then_inc(hidden_ready, 1)

                            low_block(i, n + 2)
                            hidden(0)
                            dve.wait_ge(ye_free, e1 + 1)
                            choose(e1, 1 - j, dve_loop)
                            low_block(i, n + 3)
                            low_block(i, n + 4)
                            dve.wait_ge(hT_copied, e2 + 1)
                            v.tensor_tensor(hid_low, acc[3][:, 0, 0:4 * CAP], hid_high, ALU.subtract)\
                                .then_inc(hid_low_ready, 1)
                            hidden(1)
                            dve.wait_ge(xT_full, e2 + 1)
                            modulate(1 - j, 0, dve_loop, base + 1)
                            if more:
                                low_block(i, n + PER_EXPERT)
                            dve.wait_ge(xT_full, e2 + 2)
                            modulate(1 - j, 1, dve_loop, base + 6)
                            if more:
                                low_block(i, n + PER_EXPERT + 1)
                            dve.wait_ge(*multiplied(i, n + PER_EXPERT - 1))
                            dve.wait_ge(ye_free, e1)
                            v.scalar_tensor_tensor(out=ye[:, j, :], in0=accf[2][0:CAP, :], scalar=g_cur[:, j:j + 1],
                                                   in1=gate2, op0=ALU.mult, op1=ALU.mult).then_inc(ye_ready, 1)

                    with dve.Fori(0, NE // EXPERTS_IN_BODY - 1) as i:
                        experts_dve(i, False)
                    experts_dve(NE // EXPERTS_IN_BODY - 1, True)

                    dve.wait_ge(ln2_in, 32)
                    for t in range(NT):
                        dve.wait_ge(zin_in[t], 16)
                        layer_norm(1, t, z2[:, t, :], z2[:, t, :], var2_ready, std2_ready, x2_ready)

                @block.gpsimd
                def _(pool):
                    pool.sem_inc(ye_free, 2)
                    for p in range(2):
                        pool.wait_ge(x1_out[p], 32 * ((NT + 1 - p) // 2))

                    def gather(j):
                        pool.indirect_dma_start(xs[:, j, :], None, x1_scr,
                                                bass.IndirectOffsetOnAxis(ap=idx_cur[:, j:j + 1], axis=0))\
                            .then_inc(gather_done, 16)

                    pool.wait_ge(sel_cur, 1)
                    gather(0)
                    with pool.Fori(0, NE // EXPERTS_IN_BODY) as i:
                        for j in range(EXPERTS_IN_BODY):
                            e1 = i * EXPERTS_IN_BODY + (j + 1)
                            pool.wait_ge(sel_cur, e1 + 1)
                            pool.sem_inc(pool_turn, 1)
                            gather(1 - j)
                            pool.wait_ge(ye_ready, e1 + 1)
                            pool.sem_inc(pool_turn, 1)
                            pool.indirect_dma_start(y_acc, bass.IndirectOffsetOnAxis(ap=idx_cur[:, j:j + 1], axis=0),
                                                    ye[:, j, :], None, compute_op=ALU.add).then_inc(scatter_done, 16)
                            pool.wait_ge(scatter_done, layer * (16 * NE) + i * (16 * EXPERTS_IN_BODY) + 16 * (j + 1))
                            pool.sem_inc(ye_free, 1)
                    pool.wait_ge(gather_done, layer * (16 * (NE + 1)) + 16 * (NE + 1))

            nc.multi_engine_barrier(nc.engines, sems_to_clear=range(cleared_from.num, cleared_to.num + 1))


def layout(inputs):
    a = {k: np.asarray(v) for k, v in inputs.items()}

    def blocks(w, n_k, width):
        lead = w.shape[:-2]
        w = w.reshape(*lead, n_k, P, w.shape[-1] // width, width)
        w = np.moveaxis(w, -2, -4)
        w = np.swapaxes(w, -3, -2)
        return np.ascontiguousarray(w).reshape(*lead, w.shape[-4], P, n_k * width)

    def columns(v):
        return np.swapaxes(v.reshape(*v.shape[:-1], -1, P), -1, -2)

    gate, up = (blocks(a[n], DK, BANK) for n in ("w_gate", "w_up"))
    down = a["w_down"].reshape(DEPTH, NE, 2, 4, P, D).swapaxes(3, 4).reshape(DEPTH, NE, 2, P, SLOT)
    experts = np.stack([gate[:, :, 0], up[:, :, 0], gate[:, :, 1], up[:, :, 1], down[:, :, 0], down[:, :, 1]],
                       axis=2)
    L = DEPTH
    w_in = a["w_in"]
    offs = np.cumsum([0, 512, 512, 512, 512, 128, 128, 512, 512, 512, 512])
    col = {n: w_in[:, :, offs[i]:offs[i + 1]] for i, n in
           enumerate(["q", "k", "v", "gq", "gk", "gv", "cb", "cc", "ch", "pool"])}
    gates = w_in[:, :, offs[-1]:].reshape(L, D, 4, 2, BANK).transpose(0, 3, 2, 1, 4)
    ada = blocks(a["w_ada"], DK, BANK)
    out = {
        "x_sample": a["x_sample"], "x_prompt": a["x_prompt"],
        "cna_k": a["cache_na_k"].reshape(L, PAST, BW), "cna_v": a["cache_na_v"].reshape(L, PAST, BW),
        "cg_k": a["cache_gqa_k"].reshape(L, PAST, P), "cg_v": a["cache_gqa_v"].reshape(L, PAST, P),
        "cond": np.stack([columns(a["c"][0]), columns(a["c_ctx"])], axis=-1),
        "small": np.concatenate([columns(a["b_ada"]),
                                 columns(a["conv_w"]).transpose(0, 2, 3, 1).reshape(L, P, 12),
                                 columns(a["conv_b"]), columns(a["pool_scale"])], axis=-1),
        "w_ada": ada,
        "w_ada_ahead": np.concatenate([ada[:, :ADA_AHEAD], ada[:1, :ADA_AHEAD]]),
        "w_main": np.stack([blocks(col[n], DK, BANK)[:, 0] for n in MAIN if n != "gkv"], axis=1),
        "w_gkv": blocks(np.concatenate([col["gk"], col["gv"]], axis=-1), DK, 2 * P)[:, 0],
        "w_gate_in": blocks(gates, DK, BANK).reshape(L, 8, P, SLOT),
        "w_branch": blocks(a["w_branch"], BK, BANK).transpose(0, 2, 1, 3, 4).reshape(L, 8, P, BK * BANK),
        "w_out": blocks(a["w_out"], DK, BANK),
        "bias_rows": np.pad(a["na_rpb"], ((0, 0), (0, 0), (0, 0), (QC, QC)))[:, :, ::-1, ::-1],
        "pool_w": a["pool_w"].transpose(0, 2, 1, 3),
        "w_router": a["w_router"].reshape(L, DK, P, NE).transpose(0, 2, 1, 3),
        "qk_gain": np.concatenate([a["qn_g"], a["kn_g"]], axis=-1),
        "ln_p": np.stack([a["ln1_g"], a["ln1_b"], a["ln2_g"], a["ln2_b"]], axis=1),
        "w_exp": experts,
    }
    out["bias_rows"] = np.pad(out["bias_rows"], ((0, 0), (0, 0), (0, 0), (0, 1)))
    return {k: np.ascontiguousarray(v) for k, v in out.items()}


def shape_constants():
    q = np.arange(P)
    i, keys = q // GR, np.arange(NWIN)
    mask = np.zeros((P, 3, NWIN), np.float32)
    for n, b in ((0, 0), (1, 1), (2, NB - 1)):
        start = np.clip(QC * b + i - WIN_C // 2, 0, GW - WIN_C)[:, None]
        ck = KEY_COL[b] + keys[None, :] % KC
        mask[:, n] = np.where((ck >= start) & (ck < start + WIN_C), 0.0, MASKED)
    n_freq = HD // 4
    inv = THETA ** (-np.arange(n_freq, dtype=np.float32) / n_freq)
    t = np.arange(LAT)
    rope = np.zeros((LAT, 2, 2, 2, n_freq), np.float32)
    for n, pos in enumerate((t // GW, t % GW)):
        ang = pos.astype(np.float32)[:, None] * inv.astype(np.float32)
        rope[:, 0, n] = np.cos(ang)[:, None, :]
        rope[:, 1, n] = np.sin(ang)[:, None, :]
    rope = rope.reshape(NLT, P, 2, HD).transpose(1, 0, 2, 3)
    corr = np.ones((4, 2, 8), np.float32)
    for g, win in enumerate(POOL_WINDOWS):
        n = 64
        pos = np.arange(n)
        count = np.clip(pos + win // 2, 0, n) - np.clip(pos - win // 2, 0, n)
        corr[g, 0], corr[g, 1] = win / count[:8], win / count[-8:]
    return {"ident_in": np.eye(P, dtype=np.float32), "mask_in": mask.reshape(P, 3 * NWIN),
            "rope_in": np.ascontiguousarray(rope),
            "corr_in": np.ascontiguousarray(np.broadcast_to(corr.reshape(1, 4, 16), (P, 4, 16)))}


OUTS = {"y_prompt": (1, CTX, D), "y_sample": (1, LAT, D), "st_na_k": (DEPTH, CTX, BW),
        "st_na_v": (DEPTH, CTX, BW), "st_g_k": (DEPTH, CTX, P), "st_g_v": (DEPTH, CTX, P)}


def kernel(**inputs):
    import concourse.bacc as bacc
    from concourse.bass_utils import run_bass_kernel_spmd

    arrays = {**layout(inputs), **shape_constants()}
    nc = bacc.Bacc("TRN2", target_bir_lowering=False, num_devices=1)
    args = {n: nc.dram_tensor(n, a.shape, F32, kind="ExternalInput").ap() for n, a in arrays.items()}
    for n, shape in OUTS.items():
        args[n] = nc.dram_tensor(n, shape, F32, kind="ExternalOutput").ap()
    build_program(nc, **args)
    r = run_bass_kernel_spmd(nc, [arrays], core_ids=[0]).results[0]
    return (r["y_prompt"], r["y_sample"],
            r["st_na_k"].reshape(1, DEPTH, CTX, NH, HD), r["st_na_v"].reshape(1, DEPTH, CTX, NH, HD),
            r["st_g_k"].reshape(1, DEPTH, CTX, KVH, HD), r["st_g_v"].reshape(1, DEPTH, CTX, KVH, HD))
```
